# Optimizing a Trainium2 kernel written in Bass

```python
import math, functools
import jax, jax.numpy as jnp
from jax import lax
import numpy as np

D_MODEL = 1024
BATCH = 1
SEQ = 128
DEPTH = 1
DEC_BATCH = 1
DEC_SEQ = 256
PAST_LEN = 128

GRID_W = 64
GLA_HEADS = 4
GLA_DK = 128
GLA_DV = 256
GLA_QK = GLA_HEADS * GLA_DK
GLA_VW = GLA_HEADS * GLA_DV
GLA_RANK = 16
GLA_TAU = 16.0
CHUNK = 64
DIFF_HEADS = 8
DIFF_DH = 64
DIFF_QK = DIFF_HEADS * 2 * DIFF_DH
DIFF_VW = DIFF_HEADS * 2 * DIFF_DH
Q_BLOCK = 128
ROPE_BASE = 10000.0
ROPE_AXIS_DIM = DIFF_DH // 2
N_EXPERTS = 16
EXPERT_FF = 2816
CAPACITY_FACTOR = 2
EPS = 1e-6
IN_SIZES = (GLA_QK, GLA_QK, GLA_VW, GLA_VW, GLA_RANK, GLA_RANK, DIFF_QK, DIFF_QK, DIFF_VW, D_MODEL, D_MODEL)
IN_WIDTH = 2 * GLA_QK + 2 * GLA_VW + 2 * GLA_RANK + 2 * DIFF_QK + DIFF_VW + 2 * D_MODEL

kernel_name = 'hybrid_gla_diffattn_ec_dit_step'

def ln_plain(x):
    x32 = x.astype(jnp.float32)
    mu = jnp.mean(x32, axis=-1, keepdims=True)
    var = jnp.mean(jnp.square(x32 - mu), axis=-1, keepdims=True)
    return ((x32 - mu) * lax.rsqrt(var + EPS)).astype(x.dtype)

def ln_affine(x, g, b):
    x32 = x.astype(jnp.float32)
    mu = jnp.mean(x32, axis=-1, keepdims=True)
    var = jnp.mean(jnp.square(x32 - mu), axis=-1, keepdims=True)
    y = (x32 - mu) * lax.rsqrt(var + EPS) * g.astype(jnp.float32) + b.astype(jnp.float32)
    return y.astype(x.dtype)

def rms_norm(x, g):
    x32 = x.astype(jnp.float32)
    y = x32 * lax.rsqrt(jnp.mean(jnp.square(x32), axis=-1, keepdims=True) + EPS)
    return (y * g.astype(jnp.float32)).astype(x.dtype)

def grid_angles(n_tokens):
    rows = n_tokens // GRID_W
    pos_r = jnp.repeat(jnp.arange(rows, dtype=jnp.float32), GRID_W)
    pos_c = jnp.tile(jnp.arange(GRID_W, dtype=jnp.float32), rows)
    half = ROPE_AXIS_DIM // 2
    inv = ROPE_BASE ** (-jnp.arange(half, dtype=jnp.float32) / half)
    return pos_r[:, None] * inv, pos_c[:, None] * inv

def rope_half(x, ang):
    p = x.shape[-1] // 2
    cos = jnp.cos(ang)[None, :, None, None, :]
    sin = jnp.sin(ang)[None, :, None, None, :]
    x32 = x.astype(jnp.float32)
    x1, x2 = x32[..., :p], x32[..., p:]
    return jnp.concatenate([x1 * cos - x2 * sin, x1 * sin + x2 * cos], axis=-1).astype(x.dtype)

def axial_rope(x, ang_r, ang_c):
    return jnp.concatenate([rope_half(x[..., :ROPE_AXIS_DIM], ang_r),
                            rope_half(x[..., ROPE_AXIS_DIM:], ang_c)], axis=-1)

def gla_scan(q, k, v, log_a, s0):
    B, L, H, _ = q.shape
    dv = v.shape[-1]
    n = L // CHUNK

    def to_chunks(t):
        return jnp.moveaxis(t.astype(jnp.float32).reshape(B, n, CHUNK, H, t.shape[-1]), 1, 0)

    mask = jnp.tril(jnp.ones((CHUNK, CHUNK), dtype=bool))

    def step(S, inp):
        qc, kc, vc, gc = inp
        b = jnp.cumsum(gc, axis=1)
        b_last = b[:, -1]
        qe = qc * jnp.exp(b)
        ke = kc * jnp.exp(-b)
        o = jnp.einsum('bihk,bhkv->bihv', qe, S)
        A = jnp.where(mask, jnp.einsum('bihk,bjhk->bhij', qe, ke), 0.0)
        o = o + jnp.einsum('bhij,bjhv->bihv', A, vc)
        kd = kc * jnp.exp(b_last[:, None] - b)
        S = jnp.exp(b_last)[..., None] * S + jnp.einsum('bjhk,bjhv->bhkv', kd, vc)
        return S, o

    S, o = lax.scan(step, s0.astype(jnp.float32), (to_chunks(q), to_chunks(k), to_chunks(v), to_chunks(log_a)))
    o = jnp.moveaxis(o, 0, 1).reshape(B, L, H, dv)
    return o.astype(v.dtype), S

def diff_attention(q, k, v, lam):
    B, Lq, H, _, dh = q.shape
    nb = Lq // Q_BLOCK
    qb = jnp.moveaxis(q.reshape(B, nb, Q_BLOCK, H, 2, dh), 1, 0)
    scale = dh ** -0.5

    def block(qi):
        s = jnp.einsum('bqhcd,bkhcd->bhcqk', qi, k).astype(jnp.float32) * scale
        p = jax.nn.softmax(s, axis=-1)
        pd = (p[:, :, 0] - lam * p[:, :, 1]).astype(v.dtype)
        return jnp.einsum('bhqk,bkhe->bqhe', pd, v)

    o = lax.map(block, qb)
    return jnp.moveaxis(o, 0, 1).reshape(B, Lq, H, v.shape[-1])

def token_mixers(h, w_in, w_alpha_f, b_alpha_f, w_alpha_b, b_alpha_b, gla_norm_g, w_proj_a,
                 lam, lam_init, subln_g, w_proj_b, w_out, rope_ang, s0_f, s0_b, k_ctx, v_ctx):
    B, L, _ = h.shape
    offs, acc = [], 0
    for s in IN_SIZES[:-1]:
        acc += s
        offs.append(acc)
    qa, ka, va, ra, af, ab, qd, kd, vd, ga, gb = jnp.split(h @ w_in, offs, axis=-1)
    qa = qa.reshape(B, L, GLA_HEADS, GLA_DK) * (GLA_DK ** -0.5)
    ka = ka.reshape(B, L, GLA_HEADS, GLA_DK)
    va = va.reshape(B, L, GLA_HEADS, GLA_DV)
    log_f = (jax.nn.log_sigmoid((af @ w_alpha_f + b_alpha_f).astype(jnp.float32)) / GLA_TAU).reshape(B, L, GLA_HEADS, GLA_DK)
    log_b = (jax.nn.log_sigmoid((ab @ w_alpha_b + b_alpha_b).astype(jnp.float32)) / GLA_TAU).reshape(B, L, GLA_HEADS, GLA_DK)
    o_f, s_f = gla_scan(qa, ka, va, log_f, s0_f)
    o_b, s_b = gla_scan(jnp.flip(qa, 1), jnp.flip(ka, 1), jnp.flip(va, 1), jnp.flip(log_b, 1), s0_b)
    o_a = rms_norm(o_f + jnp.flip(o_b, 1), gla_norm_g) * jax.nn.silu(ra.reshape(B, L, GLA_HEADS, GLA_DV))
    o_a = o_a.reshape(B, L, GLA_VW)
    qd = qd.reshape(B, L, DIFF_HEADS, 2, DIFF_DH)
    kd = kd.reshape(B, L, DIFF_HEADS, 2, DIFF_DH)
    vd = vd.reshape(B, L, DIFF_HEADS, 2 * DIFF_DH)
    q_att, k_att, v_att = qd, kd, vd
    if rope_ang is not None:
        q_att = axial_rope(qd, rope_ang[0], rope_ang[1])
        k_att = axial_rope(kd, rope_ang[0], rope_ang[1])
    if k_ctx is not None:
        k_att = jnp.concatenate([k_att, k_ctx.astype(k_att.dtype)], axis=1)
        v_att = jnp.concatenate([v_att, v_ctx.astype(v_att.dtype)], axis=1)
    o_d = diff_attention(q_att, k_att, v_att, lam)
    o_d = (rms_norm(o_d, subln_g) * (1.0 - lam_init)).reshape(B, L, DIFF_VW)
    merged = jax.nn.sigmoid(ga) * (o_a @ w_proj_a) + jax.nn.sigmoid(gb) * (o_d @ w_proj_b)
    return merged @ w_out, kd, vd, s_f, s_b

def ec_moe(h, w_router, w_gate, w_up, w_down):
    B, L, D = h.shape
    n = B * L
    xt = h.reshape(n, D)
    aff = jax.nn.softmax((xt @ w_router).astype(jnp.float32), axis=-1)
    cap = CAPACITY_FACTOR * n // N_EXPERTS
    gate, idx = lax.top_k(aff.T, cap)
    xe = jnp.take(xt, idx, axis=0)
    hid = jax.nn.silu(jnp.einsum('ecd,edf->ecf', xe, w_gate)) * jnp.einsum('ecd,edf->ecf', xe, w_up)
    ye = jnp.einsum('ecf,efd->ecd', hid, w_down) * gate[..., None].astype(h.dtype)
    out = jnp.zeros_like(xt).at[idx.reshape(-1)].add(ye.reshape(-1, D))
    return out.reshape(B, L, D)

def trunk_layer(x, mod, mixer, moe, ln1_g, ln1_b, ln2_g, ln2_b, alpha, rope_ang, s0_f, s0_b, k_ctx, v_ctx):
    sh1, sc1, g1, sh2, sc2, g2 = jnp.split(mod[:, None, :].astype(x.dtype), 6, axis=-1)
    h = ln_plain(x) * (1 + sc1) + sh1
    mix, kd, vd, s_f, s_b = mixer(h, rope_ang=rope_ang, s0_f=s0_f, s0_b=s0_b, k_ctx=k_ctx, v_ctx=v_ctx)
    x = ln_affine(alpha * x + g1 * mix, ln1_g, ln1_b)
    h = ln_plain(x) * (1 + sc2) + sh2
    x = ln_affine(alpha * x + g2 * moe(h), ln2_g, ln2_b)
    return x, kd, vd, s_f, s_b

def setup_inputs(seed: int = 0) -> dict:
    key = jax.random.key(seed)
    ks = jax.random.split(key, 40)
    D = D_MODEL
    beta = (8.0 * DEPTH) ** -0.25

    def nrm(k, shape, s):
        return jax.random.normal(k, shape, jnp.float32) * s

    return {
        'x_prompt': nrm(ks[0], (BATCH, SEQ, D), 1.0),
        'x_sample': nrm(ks[1], (DEC_BATCH, DEC_SEQ, D), 1.0),
        'cache_diff_k': nrm(ks[2], (DEC_BATCH, DEPTH, PAST_LEN, DIFF_HEADS, 2, DIFF_DH), 1.0),
        'cache_diff_v': nrm(ks[3], (DEC_BATCH, DEPTH, PAST_LEN, DIFF_HEADS, 2 * DIFF_DH), 1.0),
        'state_gla_fwd': nrm(ks[4], (DEC_BATCH, DEPTH, GLA_HEADS, GLA_DK, GLA_DV), 0.1),
        'state_gla_bwd': nrm(ks[5], (DEC_BATCH, DEPTH, GLA_HEADS, GLA_DK, GLA_DV), 0.1),
        'c': nrm(ks[6], (DEC_BATCH, D), 1.0),
        'c_ctx': nrm(ks[7], (D,), 1.0),
        'w_mod': nrm(ks[8], (DEPTH, D, 6 * D), 0.5 * D ** -0.5),
        'b_mod': nrm(ks[9], (DEPTH, 6 * D), 0.02),
        'w_in': nrm(ks[10], (DEPTH, D, IN_WIDTH), D ** -0.5),
        'w_alpha_f': nrm(ks[11], (DEPTH, GLA_RANK, GLA_QK), GLA_RANK ** -0.5),
        'b_alpha_f': nrm(ks[12], (DEPTH, GLA_QK), 0.02),
        'w_alpha_b': nrm(ks[13], (DEPTH, GLA_RANK, GLA_QK), GLA_RANK ** -0.5),
        'b_alpha_b': nrm(ks[14], (DEPTH, GLA_QK), 0.02),
        'gla_norm_g': 1.0 + nrm(ks[15], (DEPTH, GLA_DV), 0.02),
        'w_proj_a': nrm(ks[16], (DEPTH, GLA_VW, D), GLA_VW ** -0.5),
        'lambda_q1': nrm(ks[17], (DEPTH, DIFF_DH), 0.1),
        'lambda_k1': nrm(ks[18], (DEPTH, DIFF_DH), 0.1),
        'lambda_q2': nrm(ks[19], (DEPTH, DIFF_DH), 0.1),
        'lambda_k2': nrm(ks[20], (DEPTH, DIFF_DH), 0.1),
        'subln_g': 1.0 + nrm(ks[21], (DEPTH, 2 * DIFF_DH), 0.02),
        'w_proj_b': nrm(ks[22], (DEPTH, DIFF_VW, D), DIFF_VW ** -0.5),
        'w_out': nrm(ks[23], (DEPTH, D, D), beta * D ** -0.5),
        'ln1_g': 1.0 + nrm(ks[24], (DEPTH, D), 0.02),
        'ln1_b': nrm(ks[25], (DEPTH, D), 0.02),
        'w_router': nrm(ks[26], (DEPTH, D, N_EXPERTS), D ** -0.5),
        'w_exp_gate': nrm(ks[27], (DEPTH, N_EXPERTS, D, EXPERT_FF), D ** -0.5),
        'w_exp_up': nrm(ks[28], (DEPTH, N_EXPERTS, D, EXPERT_FF), D ** -0.5),
        'w_exp_down': nrm(ks[29], (DEPTH, N_EXPERTS, EXPERT_FF, D), beta * EXPERT_FF ** -0.5),
        'ln2_g': 1.0 + nrm(ks[30], (DEPTH, D), 0.02),
        'ln2_b': nrm(ks[31], (DEPTH, D), 0.02),
    }

def reference(x_prompt, x_sample, cache_diff_k, cache_diff_v, state_gla_fwd, state_gla_bwd, c, c_ctx,
              w_mod, b_mod, w_in, w_alpha_f, b_alpha_f, w_alpha_b, b_alpha_b, gla_norm_g, w_proj_a,
              lambda_q1, lambda_k1, lambda_q2, lambda_k2, subln_g, w_proj_b, w_out, ln1_g, ln1_b,
              w_router, w_exp_gate, w_exp_up, w_exp_down, ln2_g, ln2_b):
    alpha = (2.0 * DEPTH) ** 0.25
    ang_r, ang_c = grid_angles(x_sample.shape[1])
    xp, xs = x_prompt, x_sample
    new_k, new_v, new_f, new_b = [], [], [], []
    for l in range(DEPTH):
        lam_init = 0.8 - 0.6 * math.exp(-0.3 * l)
        lam = (jnp.exp(jnp.sum(lambda_q1[l].astype(jnp.float32) * lambda_k1[l].astype(jnp.float32)))
               - jnp.exp(jnp.sum(lambda_q2[l].astype(jnp.float32) * lambda_k2[l].astype(jnp.float32)))
               + lam_init)
        mixer = functools.partial(token_mixers, w_in=w_in[l], w_alpha_f=w_alpha_f[l], b_alpha_f=b_alpha_f[l],
                                  w_alpha_b=w_alpha_b[l], b_alpha_b=b_alpha_b[l], gla_norm_g=gla_norm_g[l],
                                  w_proj_a=w_proj_a[l], lam=lam, lam_init=lam_init, subln_g=subln_g[l],
                                  w_proj_b=w_proj_b[l], w_out=w_out[l])
        moe = functools.partial(ec_moe, w_router=w_router[l], w_gate=w_exp_gate[l],
                                w_up=w_exp_up[l], w_down=w_exp_down[l])
        mod_ctx = jax.nn.silu(c_ctx)[None, :] @ w_mod[l] + b_mod[l]
        mod_lat = jax.nn.silu(c) @ w_mod[l] + b_mod[l]
        zeros = jnp.zeros((xp.shape[0], GLA_HEADS, GLA_DK, GLA_DV), jnp.float32)
        xp, kd, vd, s_f, s_b = trunk_layer(xp, mod_ctx, mixer, moe, ln1_g[l], ln1_b[l], ln2_g[l], ln2_b[l], alpha,
                                           rope_ang=None, s0_f=zeros, s0_b=zeros, k_ctx=None, v_ctx=None)
        new_k.append(kd)
        new_v.append(vd)
        new_f.append(s_f)
        new_b.append(s_b)
        xs = trunk_layer(xs, mod_lat, mixer, moe, ln1_g[l], ln1_b[l], ln2_g[l], ln2_b[l], alpha,
                         rope_ang=(ang_r, ang_c), s0_f=state_gla_fwd[:, l], s0_b=state_gla_bwd[:, l],
                         k_ctx=cache_diff_k[:, l], v_ctx=cache_diff_v[:, l])[0]
    new_diff_k = jnp.stack(new_k, axis=1)
    new_diff_v = jnp.stack(new_v, axis=1)
    new_gla_fwd = jnp.stack(new_f, axis=1)
    new_gla_bwd = jnp.stack(new_b, axis=1)
    return (xp, xs, new_diff_k, new_diff_v, new_gla_fwd, new_gla_bwd)


_drawn_inputs = setup_inputs


def setup_inputs(seed=0):
    import zlib

    import numpy as np

    out = dict(_drawn_inputs(seed))
    spreads = {}
    factors = {'cache_diff_k': 3.68,
     'cache_diff_v': 3.176,
     'state_gla_fwd': 45.812,
     'state_gla_bwd': 42.192,
     'b_alpha_f': 6.266,
     'b_alpha_b': 6.631,
     'gla_norm_g': 64.0,
     'lambda_q1': 8.0,
     'lambda_k1': 26.486,
     'lambda_q2': 8.0,
     'lambda_k2': 8.0,
     'subln_g': 52.572,
     'ln1_g': 8.114,
     'ln1_b': 7.949,
     'ln2_g': 7.702,
     'ln2_b': 8.03,
     'w_router': 5.077,
     'w_exp_gate': 5.215,
     'w_exp_up': 4.859,
     'w_exp_down': 4.863}
    for name, (base, spread) in spreads.items():
        noise = np.random.default_rng([zlib.crc32(name.encode()), seed]).standard_normal(out[name].shape)
        drawn = base * np.exp(spread * noise) if base else spread * noise
        out[name] = __import__('jax').numpy.asarray(drawn.astype(out[name].dtype))
    for name, factor in factors.items():
        out[name] = (out[name] * factor).astype(out[name].dtype)
    return out
```

```python
from contextlib import ExitStack

import numpy as np
import concourse.bass as bass
from concourse import mybir

ALU = mybir.AluOpType
ACT = mybir.ActivationFunctionType
AX = mybir.AxisListType
F32 = mybir.dt.float32
I32 = mybir.dt.int32
U32 = mybir.dt.uint32

P = 128
D = 1024
KT = D // P
SEQ, DEC, PAST = 128, 256, 128
T = (SEQ + DEC) // P
NT = T * P
BANK = 512
GRID_W = 64

GH, DK, DV, RANK, CHUNK = 4, 128, 256, 16, 64
NCH = NT // CHUNK
GLA_TAU = 16.0
AH, DH = 8, 64
NKEY = NT + PAST
LAM_INIT = 0.8 - 0.6
ROPE_HALF = DH // 4
NE, FF = 16, 2816
CAP_C, CAP_L = 2 * SEQ // NE, 2 * DEC // NE
SLOT = 64
LAT0, CTX0, END0 = 0, CAP_L, CAP_L + CAP_C
ALPHA = 2.0 ** 0.25
EPS = 1e-6

C_QA, C_KA, C_VA, C_RA = 0, 512, 1024, 2048
C_AB = 3072
C_QD = C_AB + 2 * RANK
C_KD, C_VD, C_GA, C_GB = C_QD + D, C_QD + 2 * D, C_QD + 3 * D, C_QD + 4 * D

WCHUNKS = ([("mod", c) for c in range(4)] + [("in", C_QA), ("in", C_KA), ("in", C_VA), ("in", C_VA + BANK)]
           + [("mod", c) for c in range(4, 12)]
           + [("in", c0 + h * BANK) for c0 in (C_QD, C_KD, C_VD, C_RA, C_GA, C_GB) for h in range(2)]
           + [(w, h * BANK) for w in ("pa", "pb", "out") for h in range(2)])
WSLOTS = 4
CHUNK_OF = {c: n for n, c in enumerate(WCHUNKS)}

JOBS = []


def _jobs(kind, chunk, subs, engines):
    n0 = len(JOBS)
    for i in range(subs):
        JOBS.append((kind, chunk, i, engines[i % len(engines)]))
    return list(range(n0, len(JOBS)))


J_MOD = [None] * 3
J_MOD[0] = _jobs("mod", 0, 1, "v")[0]
J_QA = _jobs("qa", CHUNK_OF["in", C_QA], GH, "a")
J_KA = _jobs("ka", CHUNK_OF["in", C_KA], GH, "v")
J_AB = _jobs("ab", None, 1, "v")
J_AL = _jobs("al", None, 2 * GH, "v")
J_VA = _jobs("va", CHUNK_OF["in", C_VA], T, "a") + _jobs("va", CHUNK_OF["in", C_VA + BANK], T, "a")
J_MOD[1] = _jobs("mod", 1, 1, "v")[0]
J_MOD[2] = _jobs("mod", 2, 1, "v")[0]


def _two(kind, c0, engines):
    return _jobs(kind, CHUNK_OF["in", c0], T, engines) + _jobs(kind, CHUNK_OF["in", c0 + BANK], T, engines)


J_QD = _two("qd", C_QD, "a")
J_KD = _two("kd", C_KD, "a")
J_VD = _two("vd", C_VD, "av")
J_RA = _two("ra", C_RA, "av")
J_GA = _two("ga", C_GA, "av")
J_GB = _two("gb", C_GB, "a")
J_PA = _jobs("pa", CHUNK_OF["pa", 0], T, "v") + _jobs("pa", CHUNK_OF["pa", BANK], T, "v")
J_PB = _jobs("pb", CHUNK_OF["pb", 0], T, "v") + _jobs("pb", CHUNK_OF["pb", BANK], T, "v")
J_WO = _jobs("wo", CHUNK_OF["out", 0], T, "v") + _jobs("wo", CHUNK_OF["out", BANK], T, "v")


def copied_before(j, engine):
    return sum(1 for job in JOBS[:j] if job[3] == engine)


def last_job_of(chunk):
    kind, c = WCHUNKS[chunk]
    if kind == "mod":
        return J_MOD[c // 4]
    return max(j for j, job in enumerate(JOBS) if job[1] == chunk and job[0] != "mod")


GLA_ITEMS = [(h, s) for h in range(GH) for s in range(2)]
GLA_TILES = {0: [0], 1: [1, 2]}
GLA_UPD = {0: [(0, 0), (0, 1), (1, 1), (1, 0)], 1: [(0, 2), (0, 3), (0, 4), (1, 5), (1, 4), (1, 3)]}

ATT_ITEMS = [(t, h) for t in range(T) for h in range(AH)]

F_HT, F_QT, F_KT, F_OA, F_OD, F_M, F_H2 = range(7)

SM = {}
_at = 0
for _name, _n in (("sc1", 16), ("sh1", 16), ("bn", 36), ("mv", 6), ("std", 3), ("rstd", 3), ("eps", 1), ("one", 1),
                  ("eb", 48), ("balpha", 8), ("gla_g", 2), ("sub_g", 1), ("dots", 2), ("edots", 2),
                  ("nlam", 1), ("mx", 4), ("nb", 4), ("sum", 4), ("rs", 4), ("msa", 12), ("rsa", 12)):
    SM[_name] = (_at, _at + _n)
    _at += _n
SM_N = _at


def host_constants():
    pos = np.arange(DEC)
    inv = (10000.0 ** (-np.arange(ROPE_HALF, dtype=np.float32) / ROPE_HALF)).astype(np.float32)
    ang = np.stack([(pos // GRID_W).astype(np.float32)[:, None] * inv,
                    (pos % GRID_W).astype(np.float32)[:, None] * inv], 1)
    ang = ang.reshape(2, P, 2 * ROPE_HALF).transpose(1, 0, 2).reshape(P, -1)
    f = np.concatenate([np.eye(P), np.cos(ang), np.sin(ang),
                        np.arange(P)[:, None] + P * np.arange(T)[None]], 1).astype(np.float32)
    j, i = np.arange(P)[:, None], np.arange(P)[None]
    same = (j // CHUNK) == (i // CHUNK)
    m = np.concatenate([same & (j <= i), same & (j >= i)], 1).astype(np.int32)
    r = np.stack([(np.arange(NT) % CHUNK != 0), np.arange(NT)]).astype(np.float32)
    return f, m, r


CF_N = P + 4 * ROPE_HALF * 2 + T

QUARTER = 2 * FF
RING = 6 * QUARTER
FT = FF // (2 * P)
DOWN_GROUPS = [(0, 3), (3, 6), (6, 9), (9, 11)]
DOWN0 = 2 * QUARTER
HALF = FF // 2
FCH = [(0, 4), (4, 8), (8, 11)]

UNIT = T * D
WS0 = RING - WSLOTS * KT * BANK


def trunk_layer(nc, x_prompt, x_sample, cache_k, cache_v, st_f, st_b, c, c_ctx, w_mod, b_mod, w_in,
                w_alpha_f, b_alpha_f, w_alpha_b, b_alpha_b, gla_g, w_pa, lq1, lk1, lq2, lk2, sub_g, w_pb,
                w_out, ln1_g, ln1_b, w_router, w_gate, w_up, w_down, ln2_g, ln2_b, k_f, k_m, k_r,
                y_prompt, y_sample, new_k, new_v, new_f, new_b):
    mods = nc.dram_tensor("mods", (2, 6, D), F32, kind="Internal").ap()
    slot_tokens = nc.dram_tensor("slot_tokens", (NE, SLOT), F32, kind="Internal").ap()
    with ExitStack() as ctx:
        ctx.enter_context(nc.allow_non_contiguous_dma(reason="a few short vectors, one value per partition"))

        def sb(name, shape, dt=F32):
            return ctx.enter_context(nc.sbuf_tensor(name, shape, dt))

        def sem(name):
            return ctx.enter_context(nc.semaphore(name))

        ring = sb("ring", [P, RING])
        X, H, O1, O2, O3, O4 = (sb(n, [P, UNIT]) for n in ("X", "H", "O1", "O2", "O3", "O4"))
        kf = sb("kf", [P, CF_N])
        km = sb("km", [P, 2 * P], I32)
        cT = sb("cT", [P, KT, 32])
        sm = sb("sm", [P, SM_N])
        banks = ctx.enter_context(nc.psum_tensor("banks", [P, 8, BANK], F32))

        ident = kf[:, 0:P]
        ropec = kf[:, P:P + 64].rearrange("p (t a i) -> p t a i", t=2, a=2)
        ropes = kf[:, P + 64:P + 128].rearrange("p (t a i) -> p t a i", t=2, a=2)
        iota_c = kf[:, P + 128:P + 128 + T]

        def s(name, a=0, b=None):
            lo, hi = SM[name]
            return sm[:, lo + a:(lo + b if b is not None else hi)]

        def rows(t):
            return t.rearrange("p (t d) -> p t d", t=T)

        def cols(t):
            return t.rearrange("p (k n) -> p k n", n=NT)

        def reg(a, n):
            return ring[:, a:a + n]

        wslot = [reg(WS0 + i * KT * BANK, KT * BANK).rearrange("p (k n) -> p k n", k=KT) for i in range(WSLOTS)]
        A, B, C = reg(0, UNIT), reg(UNIT, UNIT), reg(2 * UNIT, UNIT)
        Dm, E = reg(3 * UNIT, UNIT), reg(4 * UNIT, UNIT)
        spare = reg(5 * UNIT, 2048)
        hT = cols(H[:])
        x_r, xn = rows(X[:]), rows(O2[:])
        wab = O3[:, 0:256].rearrange("p (k n) -> p k n", k=KT)
        wal = O3[0:32, 256:1280]
        abT = O3[0:32, 1280:1280 + NT]
        lamv = O3[:, 1664:1920]
        crow = O3[0:16, 1920:2048]
        crow_s = O3[0:16, 2048:2176]
        lprod = O3[:, 2176:2304]
        modrow = O1[:, 0:3 * BANK].rearrange("p (b n) -> p b n", b=3)
        bmod = O1[:, 3 * BANK:6 * BANK].rearrange("p (b n) -> p b n", b=3)
        resetm = O4[:, 0:NT]
        qkT = A.rearrange("p (w h n) -> p w h n", w=2, h=GH)
        LG = B.rearrange("p (w m) -> p w m", w=2)
        LG4 = B.rearrange("p (w h n) -> p w h n", w=2, h=GH)
        LGc = B.rearrange("p (w c j) -> p w c j", w=2, j=CHUNK)
        QE, KE, KD = Dm, E, O2[:]

        def heads(t):
            return t.rearrange("p (w h n) -> p w h n", w=2, h=GH)

        va = rows(C)
        kdn = [A[:, i * 1024:(i + 1) * 1024].rearrange("p (a w r n) -> p a w r n", w=2, r=2, n=P) for i in range(2)]
        AF = A[:, 2048:2304].rearrange("p (a n) -> p a n", n=P)
        AB = A[:, 2304:2560].rearrange("p (a n) -> p a n", n=P)
        AS = [A[:, 2560 + 256 * i:2816 + 256 * i].rearrange("p (a n) -> p a n", n=P) for i in range(2)]
        S0 = spare.rearrange("p (w h v) -> p w h v", w=2, h=GH)
        SV = [B[:, i * 1536:(i + 1) * 1536].rearrange("p (u v) -> p u v", v=DV) for i in range(2)]
        eb = s("eb").rearrange("p (w c) -> p w c", w=2)
        o_a = rows(O1[:])
        qd, kd, vd = rows(O3[:]), rows(O4[:]), rows(O2[:])
        qT = cols(reg(0, UNIT))
        kT = reg(UNIT, AH * NKEY).rearrange("p (h n) -> p h n", n=NKEY)
        vc = reg(7168, D)
        kc = reg(8192, D)
        pp = [[Dm[:, (i * 4 + q) * 384:(i * 4 + q + 1) * 384] for q in range(4)] for i in range(2)]
        o_d = rows(O3[:])
        ra, ga, gb = rows(E), rows(O4[:]), rows(reg(0, UNIT))
        merged = rows(reg(UNIT, UNIT))
        oaT, odT = cols(reg(2 * UNIT, UNIT)), cols(Dm)
        pbtmp = spare[:, 0:BANK]
        junk = spare[:, 1024:1280]
        mT = cols(H[:])
        wotmp = O4[:, 0:BANK]
        g1b = O1[:, 0:2 * D].rearrange("p (g d) -> p g d", g=2)
        l1g, l1b = O1[:, 2 * D:3 * D], O2[:, 0:D]
        sh2b = O2[:, D:3 * D].rearrange("p (g d) -> p g d", g=2)
        sc2b = O3[:, 0:2 * D].rearrange("p (g d) -> p g d", g=2)
        wr = O3[:, 2 * D:2 * D + KT * NE].rearrange("p (k e) -> p k e", k=KT)
        iota_r = O3[:, 2560:2560 + NT]
        h2 = rows(O4[:])
        h2T = cols(H[:])
        r0 = 2 * D + KT * NE
        aff = O3[:, r0:r0 + T * NE].rearrange("p (t e) -> p t e", t=T)
        rst = O3[:, r0 + 48:r0 + 64]
        affT = H[0:NE, 0:NT]
        slots = H[0:NE, 384:512]
        gates = H[0:NE, 512:640]
        idxu = H[0:NE, 640:704].bitcast(U32)
        idxT, gateT = H[:, 704:720], H[:, 720:736]
        slot_bc = H[:, 1024:1024 + NE * SLOT].rearrange("p (e s) -> p e s", e=NE)
        acc = rows(O1[:])
        hid = O2[:, 0:HALF]
        hidT = O2[:, HALF:2 * HALF].rearrange("p (i n) -> p i n", n=P)
        sel = O2[:, 2 * HALF:2 * HALF + T * SLOT].rearrange("p (t s) -> p t s", t=T)
        xe = O3[:, 0:BANK]
        xeT = O3[:, BANK:2 * BANK].rearrange("p (i n) -> p i n", n=P)
        yrow = O3[:, 2 * BANK:4 * BANK]
        selT = O3[:, 4 * BANK:4 * BANK + NT]
        g2b = reg(0, 2 * D).rearrange("p (g d) -> p g d", g=2)
        l2g, l2b = reg(2 * D, D), reg(3 * D, D)

        def bank(i, n=BANK):
            return banks[:, i, 0:n]

        ld_x = sem("x_loaded")
        ld_c = sem("conditioning_loaded")
        ld_k = sem("constants_loaded")
        ld_bm = sem("mod_bias_loaded")
        ld_ab = sem("decay_weights_loaded")
        ld_small = sem("small_vectors_loaded")
        ld_s0 = sem("cached_states_loaded")
        ld_cache = sem("cached_kv_loaded")
        wsem = [sem(f"weight_slot{i}_loaded") for i in range(WSLOTS)]
        zeroed = sem("zeroed_by_gpsimd")
        v_chain = sem("vector_steps")
        a_chain = sem("scalar_steps")
        g_chain = sem("gpsimd_steps")
        c_silu = sem("c_silu")
        c_turned = sem("c_turned")
        c_ready = sem("c_ready")
        ln_var = sem("ln_variances")
        ln_std = sem("ln_deviations")
        xn_ready = sem("x_normalised")
        mod_turned = sem("mod_turned")
        mod_ready = sem("mod_columns_ready")
        mod_rows = sem("mod_rows_ready")
        mod_stored = sem("mod_rows_stored")
        job_done = sem("job_done")
        job_out = {"a": sem("job_copied_by_scalar"), "v": sem("job_copied_by_vector")}
        tb_done = sem("turned")
        tb_out = [sem("turned_copied_by_scalar"), sem("turned_copied_by_vector")]
        lg_soft = sem("gate_softplus")
        lg_sum = sem("decay_sums")
        lg_exp = sem("decay_exps")
        gla_in = sem("gla_operands")
        gla_kt = sem("gla_turned_and_scores")
        gla_kz = sem("gla_keys_zeroed")
        gla_kcp = sem("gla_keys_copied")
        gla_msk = sem("gla_scores_masked")
        gla_u = sem("gla_updates")
        gla_s = sem("gla_states")
        gla_st = sem("gla_states_stored")
        gla_o = sem("gla_outputs")
        gla_ocp = sem("gla_outputs_copied")
        oa_sq = sem("gla_deviations")
        oa_n = sem("gla_normalised")
        dot_done = sem("lambda_dots")
        dot_exp = sem("lambda_exps")
        rope_tmp = sem("rope_products")
        rope_done = sem("rope_done")
        kv_stored = sem("new_kv_stored")
        att_s = sem("att_scores")
        att_nb = sem("att_neg_max")
        att_e = sem("att_exps")
        att_pd = sem("att_diff_probs")
        att_t = sem("att_probs_turned")
        att_tcp = sem("att_probs_turned_copied")
        att_o = sem("att_outputs")
        att_ocp = sem("att_outputs_copied")
        od_sq = sem("att_deviations")
        gates_on = sem("gates_on")
        oa_g = sem("gla_gated")
        od_g = sem("att_normalised")
        bc_loaded = sem("broadcast_rows_loaded")
        x1_var = sem("x1_variances")
        x1_std = sem("x1_deviations")
        h2_ready = sem("h2_ready")
        rt_log = sem("router_logits")
        rt_max = sem("router_neg_max")
        rt_exp = sem("router_exps")
        rt_aff = sem("router_probs")
        rt_tr = sem("router_probs_turned")
        rt_slots = sem("slots_ready")
        rt_stored = sem("slots_stored")
        rt_bc = sem("slots_broadcast")
        rt_tt = sem("slots_turned")
        rt_cols = sem("slot_columns_ready")
        land_g = [sem(f"gate_quarter{i}_loaded") for i in range(4)]
        land_u = [sem(f"up_quarter{i}_loaded") for i in range(4)]
        land_d = [sem(f"down_group{i}_loaded") for i in range(4)]
        gate_used = sem("gate_quarters_used")
        up_used = sem("up_quarters_used")
        down_used = sem("down_groups_used")
        sel_ready = sem("selection_ready")
        selT_ready = sem("combination_ready")
        xe_done = sem("expert_rows_done")
        xe_cp = sem("expert_rows_copied")
        xet_done = sem("expert_columns_done")
        xet_cp = sem("expert_columns_copied")
        silu_done = sem("gate_silu")
        hid_done = sem("hidden_ready")
        hidt_done = sem("hidden_turned")
        hidt_cp = sem("hidden_turned_copied")
        y_cp = [sem("expert_out_copied_by_scalar"), sem("expert_out_copied_by_vector")]
        comb_done = sem("combined")
        acc_done = sem("accumulated")
        ld_end = sem("last_rows_loaded")
        f_var = sem("final_variances")
        f_std = sem("final_deviations")
        f_ready = sem("final_rows")
        stored = sem("outputs_stored")

        block = ctx.enter_context(nc.Block())

        def wait_job_copied(eng, j):
            who = JOBS[j][3]
            eng.wait_ge(job_out[who], copied_before(j, who) + 1)

        def wait_family(eng, f):
            eng.wait_ge(tb_out[0], 4 * (f + 1))
            eng.wait_ge(tb_out[1], 4 * (f + 1))

        def w_chunk(n):
            kind, cc = WCHUNKS[n]
            if kind == "mod":
                w, c0 = w_mod, cc * BANK
            else:
                w, c0 = {"in": w_in, "pa": w_pa, "pb": w_pb, "out": w_out}[kind], cc
            return w[0].rearrange("(k p) n -> p k n", p=P)[:, :, c0:c0 + BANK]

        gate_v = [w_gate[0], w_up[0]]

        @block.sync
        def _(sp):
            sp.dma_start(crow[0:8, :], c_ctx.rearrange("(k p) -> k p", p=P)).then_inc(ld_c, 16)
            sp.dma_start(crow[8:16, :], c.rearrange("b (k p) -> (b k) p", p=P)).then_inc(ld_c, 16)
            sp.dma_start(kf[:], k_f).then_inc(ld_k, 16)
            sp.dma_start(x_r[:, 0, :], x_prompt[0]).then_inc(ld_x, 16)
            sp.dma_start(x_r[:, 1:3, :], x_sample[0].rearrange("(t p) d -> p t d", p=P)).then_inc(ld_x, 16)
            for n in range(len(WCHUNKS)):
                if n >= WSLOTS:
                    sp.wait_ge(job_done, last_job_of(n - WSLOTS) + 1)
                sp.dma_start(wslot[n % WSLOTS], w_chunk(n)).then_inc(wsem[n % WSLOTS], 16)

            def gate_up(w, e, q):
                return gate_v[w][e].rearrange("(k p) f -> p k f", p=P)[:, 2 * q:2 * q + 2, :]

            def quarter(i):
                return reg(i * QUARTER, QUARTER).rearrange("p (k f) -> p k f", k=2)

            def down(e, g):
                a, b = DOWN_GROUPS[g]
                sp.dma_start(reg(DOWN0 + 2 * a * D, 2 * (b - a) * D).rearrange("p (i d) -> p i d", d=D),
                             w_down[0][e].rearrange("(i p) d -> p i d", p=P)[:, 2 * a:2 * b, :]).then_inc(land_d[g], 16)

            wait_family(sp, F_M)
            for q in range(4):
                if q == 2:
                    sp.wait_ge(job_done, J_WO[-1] + 1)
                sp.dma_start(quarter(q), gate_up(0, 0, q)).then_inc(land_g[q], 16)
            for q in range(4):
                if q >= 2:
                    sp.wait_ge(gate_used, q - 1)
                sp.dma_start(quarter((4 + q) % 6), gate_up(1, 0, q)).then_inc(land_u[q], 16)
            for g in range(4):
                if g == 0:
                    sp.wait_ge(gate_used, 4)
                else:
                    sp.wait_ge(up_used, min(g, 2))
                down(0, g)
            with sp.Fori(1, NE) as e:
                for q, (used, n) in enumerate(((up_used, 1), (up_used, 0), (down_used, 3), (down_used, 2))):
                    sp.wait_ge(used, e * 4 - n)
                    sp.dma_start(quarter(q), gate_up(0, e, q)).then_inc(land_g[q], 16)
                for q, (used, n) in enumerate(((down_used, -1), (down_used, 0), (gate_used, 1), (gate_used, 2))):
                    sp.wait_ge(used, e * 4 + n)
                    sp.dma_start(quarter((4 + q) % 6), gate_up(1, e, q)).then_inc(land_u[q], 16)
                for g, (used, n) in enumerate(((gate_used, 4), (up_used, 1), (up_used, 2), (up_used, 2))):
                    sp.wait_ge(used, e * 4 + n)
                    down(e, g)
            sp.wait_ge(up_used, 4 * NE)
            sp.wait_ge(mod_stored, 16 * 8)
            for g in range(2):
                sp.dma_start(g2b[:, g, :], mods[g, 5:6].to_broadcast((P, D))).then_inc(ld_end, 16)
            sp.dma_start(l2g, ln2_g.to_broadcast((P, D))).then_inc(ld_end, 16)
            sp.dma_start(l2b, ln2_b.to_broadcast((P, D))).then_inc(ld_end, 16)
            for t in range(T):
                sp.wait_ge(f_ready, t + 1)
                dst = y_prompt[0] if t == 0 else y_sample[0, (t - 1) * P:t * P, :]
                sp.dma_start(dst, x_r[:, t, :]).then_inc(stored, 16)
            sp.wait_ge(stored, 16 * T)
            sp.wait_ge(kv_stored, 32)
            sp.wait_ge(gla_st, 16 * 2 * GH)

        @block.gpsimd
        def _(pool):
            pool.memset(cT[:], 0.0).then_inc(zeroed, 1)
            pool.memset(wal, 0.0).then_inc(zeroed, 1)
            for j in range(4):
                src = b_mod.rearrange("o (b j n) -> o j b n", b=3, j=4)[:, j]
                pool.dma_start(bmod[32 * j:32 * j + 32], src.to_broadcast((32, 3, BANK))).then_inc(ld_bm, 16)
            pool.dma_start(wab, w_in[0].rearrange("(k p) n -> p k n", p=P)[:, :, C_AB:C_AB + 2 * RANK]).then_inc(ld_ab, 16)
            pool.wait_ge(zeroed, 2)
            pool.dma_start(wal[0:RANK, 0:GH * DK], w_alpha_f[0]).then_inc(ld_ab, 16)
            pool.dma_start(wal[RANK:2 * RANK, GH * DK:2 * GH * DK], w_alpha_b[0]).then_inc(ld_ab, 16)
            pool.dma_start(s("balpha", 0, 4), b_alpha_f[0].rearrange("(h p) -> p h", p=P)).then_inc(ld_small, 16)
            pool.dma_start(s("balpha", 4, 8), b_alpha_b[0].rearrange("(h p) -> p h", p=P)).then_inc(ld_small, 16)
            pool.dma_start(resetm, k_r[0:1].to_broadcast((P, NT))).then_inc(ld_small, 16)
            pool.dma_start(km[:], k_m).then_inc(ld_small, 16)
            pool.dma_start(s("gla_g"), gla_g[0].rearrange("(a p) -> p a", p=P)).then_inc(ld_small, 16)
            pool.dma_start(s("sub_g"), sub_g[0].rearrange("(a p) -> p a", p=P)).then_inc(ld_small, 16)
            for i, v in enumerate((lq1, lk1, lq2, lk2)):
                pool.dma_start(lamv[:, i * DH:(i + 1) * DH], v.to_broadcast((P, DH))).then_inc(ld_small, 16)
            for w, st in enumerate((st_f, st_b)):
                pool.dma_start(S0[:, w], st[0, 0].rearrange("h k v -> k h v")).then_inc(ld_s0, 16)
            for b in (1, 2):
                pool.wait_ge(job_out["v"], copied_before(J_MOD[b], "v") + 1)
                for j in range(4):
                    q, half = divmod(4 * b + j, 2)
                    pool.dma_start(mods[:, q, half * BANK:(half + 1) * BANK],
                                   modrow[32 * j:32 * j + 2, b, :]).then_inc(mod_stored, 16)
            for h in range(GH):
                i = 2 * h
                pool.wait_ge(gla_s, 10 * h + 4)
                for w, dst in enumerate((new_f, new_b)):
                    pool.dma_start(dst[0, 0, h], SV[i % 2][:, 2 * w + 1, :]).then_inc(gla_st, 16)
            for j in (J_KD[0], J_KD[3]):
                wait_job_copied(pool, j)
            pool.dma_start(new_k[0, 0].rearrange("t h c d -> t (h c d)"), kd[:, 0, :]).then_inc(kv_stored, 16)
            pool.wait_ge(gla_o, len(GLA_ITEMS))
            pool.dma_start(kc, cache_k[0, 0].rearrange("t h c d -> t (h c d)")).then_inc(ld_cache, 16)
            pool.dma_start(vc, cache_v[0, 0].rearrange("t h d -> t (h d)")).then_inc(ld_cache, 16)
            n = 0
            for t in (1, 2):
                for src in (qd, kd):
                    v = src[:, t, :].rearrange("p (g a w i) -> p g a w i", a=2, w=2, i=ROPE_HALF)
                    if n == 0:
                        for j in (J_QD[-1], J_KD[-1]):
                            wait_job_copied(pool, j)
                    cs = ropec[:, t - 1][:, None].to_broadcast((P, 16, 2, ROPE_HALF))
                    sn = ropes[:, t - 1][:, None].to_broadcast((P, 16, 2, ROPE_HALF))
                    tmp = [Dm[:, i * 512:(i + 1) * 512].rearrange("p (g a i) -> p g a i", a=2, i=ROPE_HALF)
                           for i in range(4)]
                    if n:
                        pool.wait_ge(rope_done, 2 * n)
                    for i, (half, tab) in enumerate(((0, cs), (1, sn), (0, sn), (1, cs))):
                        pool.tensor_tensor(tmp[i], v[:, :, :, half, :], tab, ALU.mult).then_inc(rope_tmp, 1)
                    pool.wait_ge(rope_tmp, 4 * (n + 1))
                    pool.tensor_tensor(v[:, :, :, 0, :], tmp[0], tmp[1], ALU.subtract).then_inc(rope_done, 1)
                    pool.tensor_tensor(v[:, :, :, 1, :], tmp[2], tmp[3], ALU.add).then_inc(rope_done, 1)
                    n += 1
            for j in (J_VD[0], J_VD[3]):
                wait_job_copied(pool, j)
            pool.dma_start(new_v[0, 0].rearrange("t h d -> t (h d)"), vd[:, 0, :]).then_inc(kv_stored, 16)
            pool.wait_ge(mod_stored, 16 * 8)
            pool.wait_ge(kv_stored, 32)
            pool.wait_ge(tb_done, 8 * (F_OD + 1))
            for g in range(2):
                pool.dma_start(g1b[:, g, :], mods[g, 2:3].to_broadcast((P, D))).then_inc(bc_loaded, 16)
                pool.dma_start(sh2b[:, g, :], mods[g, 3:4].to_broadcast((P, D))).then_inc(bc_loaded, 16)
                pool.dma_start(sc2b[:, g, :], mods[g, 4:5].to_broadcast((P, D))).then_inc(bc_loaded, 16)
            pool.dma_start(l1g, ln1_g.to_broadcast((P, D))).then_inc(bc_loaded, 16)
            pool.dma_start(l1b, ln1_b.to_broadcast((P, D))).then_inc(bc_loaded, 16)
            pool.dma_start(wr, w_router[0].rearrange("(k p) e -> p k e", p=P)).then_inc(bc_loaded, 16)
            pool.dma_start(iota_r, k_r[1:2].to_broadcast((P, NT))).then_inc(bc_loaded, 16)
            pool.wait_ge(rt_slots, 1)
            pool.dma_start(slot_tokens, slots[:, 0:SLOT]).then_inc(rt_stored, 16)
            pool.wait_ge(rt_stored, 16)
            pool.dma_start(slot_bc, slot_tokens.rearrange("e s -> (e s)")[None].to_broadcast((P, NE * SLOT))).then_inc(rt_bc, 16)

        @block.tensor
        def _(pe):
            turned = [0]

            def batch(srcs):
                b = turned[0]
                if b >= 2:
                    pe.wait_ge(tb_out[b % 2], (b - 2) // 2 + 1)
                for i, src in enumerate(srcs):
                    x = pe.transpose(banks[:, 2 + b % 2, i * P:(i + 1) * P], src, ident)
                x.then_inc(tb_done, 1)
                turned[0] += 1

            def job(j):
                kind, chunk, i, _ = JOBS[j]
                if j >= 2:
                    wait_job_copied(pe, j - 2)
                out = banks[:, j % 2, :]

                def weights(n):
                    pe.wait_ge(wsem[n % WSLOTS], 16 * (n // WSLOTS + 1))
                    return wslot[n % WSLOTS]

                if kind == "mod":
                    ws = [weights(CHUNK_OF["mod", 4 * chunk + q]) for q in range(4)]
                    for k in range(KT):
                        for q in range(4):
                            x = pe.matmul(out[32 * q:32 * q + 32, :], cT[:, k, :], ws[q][:, k, :],
                                          start=(k == 0), stop=(k == KT - 1))
                elif kind in ("qa", "ka"):
                    w = weights(chunk)
                    for k in range(KT):
                        x = pe.matmul(out[:, 0:NT], w[:, k, i * P:(i + 1) * P], hT[:, k, :],
                                      start=(k == 0), stop=(k == KT - 1))
                elif kind == "ab":
                    pe.wait_ge(ld_ab, 48)
                    for k in range(KT):
                        x = pe.matmul(out[0:32, 0:NT], wab[:, k, :], hT[:, k, :], start=(k == 0), stop=(k == KT - 1))
                elif kind == "al":
                    if i == 0:
                        wait_job_copied(pe, J_AB[0])
                    x = pe.matmul(out[:, 0:NT], wal[:, i * P:(i + 1) * P], abT, start=True, stop=True)
                else:
                    w = weights(chunk)
                    src = {"pa": oaT, "pb": odT, "wo": mT}.get(kind, hT)
                    for k in range(KT):
                        x = pe.matmul(out, src[:, k, i * P:(i + 1) * P], w[:, k, :], start=(k == 0), stop=(k == KT - 1))
                x.then_inc(job_done, 1)

            pe.wait_ge(ld_k, 16)
            pe.wait_ge(c_silu, 1)
            pe.transpose(banks[:, 4, 0:16], crow_s, ident[0:16, 0:16]).then_inc(c_turned, 1)
            pe.wait_ge(c_ready, 1)
            job(J_MOD[0])
            wait_job_copied(pe, J_MOD[0])
            for i in range(4):
                x = pe.transpose(banks[:, 5, i * P:(i + 1) * P], modrow[:, 0, i * P:(i + 1) * P], ident)
            x.then_inc(mod_turned, 1)
            pe.wait_ge(xn_ready, T)
            for k in range(KT):
                batch([xn[:, t, k * P:(k + 1) * P] for t in range(T)])
            wait_family(pe, F_HT)
            for j in J_QA + J_KA + J_AB + J_AL + J_VA:
                job(j)
            job(J_MOD[1])
            job(J_MOD[2])

            def gla_turn(i):
                h, q = GLA_ITEMS[i]
                if i:
                    pe.wait_ge(gla_kcp, i)
                    pe.wait_ge(gla_msk, 3 * i)
                for a, t in enumerate(GLA_TILES[q]):
                    for w in range(2):
                        pe.transpose(banks[:, 2, (2 * a + w) * P:(2 * a + w + 1) * P],
                                     heads(KD)[:, w, h, t * P:(t + 1) * P], ident)
                for a, t in enumerate(GLA_TILES[q]):
                    for w in range(2):
                        x = pe.matmul(banks[:, 3, (2 * a + w) * P:(2 * a + w + 1) * P],
                                      heads(KE)[:, w, h, t * P:(t + 1) * P], heads(QE)[:, w, h, t * P:(t + 1) * P],
                                      start=True, stop=True)
                x.then_inc(gla_kt, 1)

            def gla_update(i):
                h, q = GLA_ITEMS[i]
                pe.wait_ge(gla_kcp, i + 1)
                if i == 0:
                    for j in J_VA[-2:]:
                        wait_job_copied(pe, j)
                if i:
                    pe.wait_ge(gla_s, 10 * (i // 2) + (4 if i % 2 else 0))
                for u, (w, ch) in enumerate(GLA_UPD[q]):
                    t, r = divmod(ch, 2)
                    a = t - GLA_TILES[q][0]
                    x = pe.matmul(banks[:, 4 + u // 2, (u % 2) * DV:(u % 2 + 1) * DV],
                                  kdn[i % 2][:, a, w, r, :], va[:, t, h * DV:(h + 1) * DV], start=True, stop=True)
                x.then_inc(gla_u, 1)

            def gla_state(i, w, ch):
                h, q = GLA_ITEMS[i]
                if q == 0:
                    return SV[i % 2][:, 2 * w, :] if ch == 1 - w else None
                step = ch - 2 if w == 0 else 5 - ch
                return S0[:, w, h, :] if step == 0 else SV[i % 2][:, 3 * w + step - 1, :]

            def gla_out(i):
                h, q = GLA_ITEMS[i]
                pe.wait_ge(gla_msk, 3 * (i + 1))
                pe.wait_ge(gla_s, 10 * (i // 2) + (10 if i % 2 else 4))
                if i == 0:
                    pe.wait_ge(ld_s0, 32)
                if i:
                    pe.wait_ge(gla_ocp, i)
                for a, t in enumerate(GLA_TILES[q]):
                    out = banks[:, 7, a * DV:(a + 1) * DV]
                    terms = [(r, w, gla_state(i, w, 2 * t + r)) for r in range(2) for w in range(2)]
                    terms = [x for x in terms if x[2] is not None]
                    pe.matmul(out, AS[i % 2][:, a, :], va[:, t, h * DV:(h + 1) * DV], start=True, stop=False,
                              skip_group_check=True)
                    for r, w, st in terms:
                        c0 = t * P + r * 64
                        x = pe.matmul(out[64 * r:64 * r + 64, :], heads(QE)[:, w, h, c0:c0 + 64], st,
                                      start=False, stop=True, skip_group_check=True)
                x.then_inc(gla_o, 1)

            pe.wait_ge(gla_in, 3)
            pe.wait_ge(mod_ready, 2)
            more = list(J_QD + J_KD)
            for i in range(len(GLA_ITEMS)):
                gla_turn(i)
                job(more.pop(0))
                gla_update(i)
                if i % 2:
                    job(more.pop(0))
                gla_out(i)
            for j in J_VD:
                job(j)
            pe.wait_ge(gla_kcp, len(GLA_ITEMS))
            pe.wait_ge(gla_msk, 3 * len(GLA_ITEMS))
            pe.wait_ge(gla_ocp, len(GLA_ITEMS))
            pe.wait_ge(rope_done, 8)
            pe.wait_ge(ld_cache, 32)
            for h in range(AH):
                batch([qd[:, t, h * P:(h + 1) * P] for t in range(T)])
            for h in range(AH):
                batch([kd[:, t, h * P:(h + 1) * P] for t in range(T)] + [kc[:, h * P:(h + 1) * P]])
            wait_family(pe, F_KT)

            def keys(t):
                return (0, SEQ) if t == 0 else (SEQ, NKEY)

            def att_scores(i):
                t, h = ATT_ITEMS[i]
                a, b = keys(t)
                if i >= 2:
                    pe.wait_ge(att_e, 2 * (i - 1))
                for q in range(2):
                    x = pe.matmul(banks[:, 2 + 2 * (i % 2) + q, 0:b - a], qT[64 * q:64 * q + 64, h, t * P:(t + 1) * P],
                                  kT[64 * q:64 * q + 64, h, a:b], start=True, stop=True)
                x.then_inc(att_s, 1)

            def att_turn(i):
                t, h = ATT_ITEMS[i]
                pe.wait_ge(att_pd, i + 1)
                if i:
                    pe.wait_ge(att_tcp, i)
                for n in range(1 if t == 0 else 3):
                    x = pe.transpose(banks[:, 6, n * P:(n + 1) * P], pp[i % 2][2][:, n * P:(n + 1) * P], ident)
                x.then_inc(att_t, 1)

            def att_out(i):
                t, h = ATT_ITEMS[i]
                pe.wait_ge(att_tcp, i + 1)
                if i:
                    pe.wait_ge(att_ocp, i)
                vs = [vd[:, 0, :]] if t == 0 else [vd[:, 1, :], vd[:, 2, :], vc]
                for n, v in enumerate(vs):
                    x = pe.matmul(banks[:, 7, 0:P], pp[i % 2][3][:, n * P:(n + 1) * P], v[:, h * P:(h + 1) * P],
                                  start=(n == 0), stop=(n == len(vs) - 1))
                x.then_inc(att_o, 1)

            for j in J_VD[-2:]:
                wait_job_copied(pe, j)
            n = len(ATT_ITEMS)
            for i in range(n + 2):
                if i < n:
                    att_scores(i)
                if i % 2 == 0 and i // 2 < len(J_RA + J_GA):
                    job((J_RA + J_GA)[i // 2])
                if 1 <= i <= n:
                    att_turn(i - 1)
                if i >= 2:
                    att_out(i - 2)
            for j in J_GB:
                job(j)
            pe.wait_ge(oa_g, T)
            for k in range(KT):
                batch([o_a[:, t, k * P:(k + 1) * P] for t in range(T)])
            pe.wait_ge(od_g, T)
            for k in range(KT):
                batch([o_d[:, t, k * P:(k + 1) * P] for t in range(T)])
            wait_family(pe, F_OD)
            for j in J_PA + J_PB:
                job(j)
            wait_job_copied(pe, J_PB[-1])
            for k in range(KT):
                batch([merged[:, t, k * P:(k + 1) * P] for t in range(T)])
            wait_family(pe, F_M)
            for j in J_WO:
                job(j)
            pe.wait_ge(h2_ready, T)
            for k in range(KT):
                batch([h2[:, t, k * P:(k + 1) * P] for t in range(T)])
            wait_family(pe, F_H2)
            for t in range(T):
                for k in range(KT):
                    x = pe.matmul(banks[:, 4, t * NE:(t + 1) * NE], h2T[:, k, t * P:(t + 1) * P], wr[:, k, :],
                                  start=(k == 0), stop=(k == KT - 1))
            x.then_inc(rt_log, 1)
            pe.wait_ge(rt_aff, 1)
            for t in range(T):
                x = pe.transpose(banks[0:NE, 5, t * P:(t + 1) * P], aff[:, t, :], ident)
            x.then_inc(rt_tr, 1)
            pe.wait_ge(rt_slots, 2)
            pe.transpose(banks[:, 6, 0:NE], slots, ident[0:NE, 0:NE])
            pe.transpose(banks[:, 6, NE:2 * NE], gates, ident[0:NE, 0:NE]).then_inc(rt_tt, 1)

            pe.wait_ge(rt_cols, 2)
            with pe.Fori(0, NE) as e:
                pe.wait_ge(sel_ready, e * T + T)
                pe.wait_ge(acc_done, e * 6 + 6)
                for t in range(T):
                    for w in range(2):
                        x = pe.matmul(banks[64 * w:64 * w + 64, 3, :], sel[:, t, :], h2[:, t, w * BANK:(w + 1) * BANK],
                                      start=(t == 0), stop=(t == T - 1))
                x.then_inc(xe_done, 1)
                pe.wait_ge(xe_cp, e + 1)
                for i in range(4):
                    x = pe.transpose(banks[:, 4, i * P:(i + 1) * P], xe[:, i * P:(i + 1) * P], ident)
                x.then_inc(xet_done, 1)
                pe.wait_ge(xet_cp, e + 1)
                for m, (land, used) in enumerate(((land_g, gate_used), (land_u, up_used))):
                    for q in range(4):
                        pe.wait_ge(land[q], e * 16 + 16)
                        w4 = reg(((4 * m + q) % 6) * QUARTER, QUARTER).rearrange("p (k i w n) -> p k i w n", k=2, w=2, n=P)
                        for kk in range(2):
                            k = 2 * q + kk
                            for b, (i0, i1) in enumerate(FCH):
                                for w in range(2):
                                    x = pe.matmul(banks[64 * w:64 * w + 64, 3 * m + b, 0:(i1 - i0) * P],
                                                  xeT[:, k % 4, 64 * (k // 4):64 * (k // 4) + 64],
                                                  w4[:, kk, i0:i1, w, :], start=(k == 0), stop=(k == KT - 1))
                        x.then_inc(used, 1)
                for b, (i0, i1) in enumerate(FCH):
                    pe.wait_ge(hid_done, e * 3 + b + 1)
                    for i in range(i0, i1):
                        x = pe.transpose(banks[:, b, (i - i0) * P:(i - i0 + 1) * P], hid[:, i * P:(i + 1) * P], ident)
                    x.then_inc(hidt_done, 1)
                pe.wait_ge(hidt_cp, e * 3 + 3)
                wd = reg(DOWN0, FF // P * D).rearrange("p (i w d) -> p i w d", w=2, d=D)
                for g, (i0, i1) in enumerate(DOWN_GROUPS):
                    pe.wait_ge(land_d[g], e * 16 + 16)
                    for i in range(i0, i1):
                        for dc in range(2):
                            for w in range(2):
                                x = pe.matmul(banks[64 * w:64 * w + 64, 6 + dc, :], hidT[:, i, 64 * w:64 * w + 64],
                                              wd[:, i, w, dc * BANK:(dc + 1) * BANK], start=(i == 0), stop=(i == FT - 1))
                    x.then_inc(down_used, 1)
                pe.wait_ge(selT_ready, e + 1)
                pe.wait_ge(y_cp[0], e + 1)
                pe.wait_ge(y_cp[1], e + 1)
                for t in range(T):
                    for dc in range(2):
                        pe.matmul(banks[:, 2 * t + dc, :], selT[:, t * P:(t + 1) * P], yrow[:, dc * BANK:(dc + 1) * BANK],
                                  start=True, stop=True).then_inc(comb_done, 1)

        def wait_turned(eng, b):
            eng.wait_ge(tb_done, b + 1)

        def family_copies(eng, f, copy, parity):
            for k in range(parity, KT, 2):
                wait_turned(eng, 8 * f + k)
                copy(k, banks[:, 2 + k % 2, :]).then_inc(tb_out[parity], 1)

        @block.scalar
        def _(act):
            steps = [0]

            def link(x):
                steps[0] += 1
                x.then_inc(a_chain, 1)
                act.wait_ge(a_chain, steps[0])

            def cp(out, in_, scale=1.0):
                return act.activation(out, in_, ACT.Copy, scale=scale)

            def job_copy(j):
                kind, chunk, i, who = JOBS[j]
                assert who == "a"
                act.wait_ge(job_done, j + 1)
                b = banks[:, j % 2, :]
                half = 0 if chunk is None else (chunk - 4) % 2
                if kind == "qa":
                    x = cp(qkT[:, 0, i, :], b[:, 0:NT], DK ** -0.5)
                else:
                    dst = {"va": va, "qd": qd, "kd": kd, "vd": vd, "ra": ra, "ga": ga, "gb": gb}[kind]
                    x = cp(dst[:, i, half * BANK:(half + 1) * BANK], b)
                x.then_inc(job_out["a"], 1)

            act.wait_ge(ld_c, 32)
            act.activation(crow_s, crow, ACT.Silu).then_inc(c_silu, 1)
            act.wait_ge(ln_var, T)
            act.activation(s("std"), s("mv").rearrange("p (t w) -> p t w", w=2)[:, :, 1], ACT.Sqrt,
                           bias=s("eps")).then_inc(ln_std, 1)

            act.wait_ge(mod_ready, 2)

            def modulated(k, b):
                sc = s("sc1").rearrange("p (k g) -> p k g", g=2)
                sh = s("sh1").rearrange("p (k g) -> p k g", g=2)
                act.activation(hT[:, k, 0:P], b[:, 0:P], ACT.Identity, scale=sc[:, k, 0:1], bias=sh[:, k, 0:1])
                return act.activation(hT[:, k, P:NT], b[:, P:NT], ACT.Identity, scale=sc[:, k, 1:2], bias=sh[:, k, 1:2])

            family_copies(act, F_HT, modulated, 0)
            for j in J_QA:
                job_copy(j)
            wait_job_copied(act, J_AL[-1])
            link(act.activation(QE, B, ACT.Abs))
            link(act.activation(QE, QE, ACT.Exp, scale=-1.0))
            act.activation(QE, QE, ACT.Ln, bias=s("one")).then_inc(lg_soft, 1)
            for j in J_VA:
                job_copy(j)
            act.wait_ge(lg_sum, 2)
            act.activation(KD, KD, ACT.Exp).then_inc(lg_exp, 1)
            act.activation(QE, B, ACT.Exp).then_inc(lg_exp, 1)
            act.activation(KE, B, ACT.Exp, scale=-1.0).then_inc(lg_exp, 1)
            ebv = eb.rearrange("p w (h c) -> p w h c", h=GH)
            act.activation(eb[:, 0, :], LGc[:, 0, :, CHUNK - 1], ACT.Exp)
            act.activation(eb[:, 1, :], LGc[:, 1, :, 0], ACT.Exp).then_inc(lg_exp, 1)
            act.wait_ge(dot_done, 2)
            act.activation(s("edots"), s("dots"), ACT.Exp).then_inc(dot_exp, 1)

            more = list(J_QD + J_KD)
            act.wait_ge(gla_in, 3)
            act.wait_ge(mod_stored, 16 * 8)
            for i, (h, q) in enumerate(GLA_ITEMS):
                nt = len(GLA_TILES[q])
                act.wait_ge(gla_kt, i + 1)
                if i == 0:
                    act.wait_ge(gla_kz, 1)
                for r in range(2):
                    rs = slice(CHUNK * r, CHUNK * r + CHUNK)
                    x = cp(kdn[i % 2][rs, 0:nt, :, r], banks[rs, 2, 0:nt * 2 * P].rearrange("p (a w n) -> p a w n", w=2, n=P))
                x.then_inc(gla_kcp, 1)
                job_copy(more.pop(0))
                if i % 2:
                    job_copy(more.pop(0))
                act.wait_ge(gla_o, i + 1)
                t0 = GLA_TILES[q][0]
                cp(o_a[:, t0:t0 + nt, h * DV:(h + 1) * DV],
                   banks[:, 7, 0:nt * DV].rearrange("p (a v) -> p a v", v=DV)).then_inc(gla_ocp, 1)
            act.wait_ge(gla_ocp, len(GLA_ITEMS))
            for n in range(T * GH):
                t, h = divmod(n, GH)
                link(act.activation(junk, o_a[:, t, h * DV:(h + 1) * DV], ACT.Square, accum_out=s("msa", n, n + 1)))
            act.activation(s("msa"), s("msa"), ACT.Sqrt, scale=1.0 / DV, bias=s("eps")).then_inc(oa_sq, 1)
            for j in J_VD:
                if JOBS[j][3] == "a":
                    job_copy(j)
            family_copies(act, F_QT, lambda h, b: cp(qT[:, h, :], b[:, 0:NT]), 0)
            family_copies(act, F_KT, lambda h, b: cp(kT[:, h, :], b), 0)

            def exps(i):
                t, h = ATT_ITEMS[i]
                nk = SEQ if t == 0 else NKEY - SEQ
                act.wait_ge(att_nb, i + 1)
                if i >= 2:
                    act.wait_ge(att_pd, i - 1)
                for q in range(2):
                    m = 2 * (i % 2) + q
                    act.activation(pp[i % 2][q][:, 0:nk], banks[:, 2 + m, 0:nk], ACT.Exp, scale=DH ** -0.5,
                                   bias=s("nb", m, m + 1), accum_out=s("sum", m, m + 1)).then_inc(att_e, 1)

            n = len(ATT_ITEMS)
            for i in range(n + 2):
                if i < n:
                    exps(i)
                if i % 2 == 0 and i // 2 < len(J_RA + J_GA):
                    j = (J_RA + J_GA)[i // 2]
                    if JOBS[j][3] == "a":
                        job_copy(j)
                if 1 <= i <= n:
                    nk = 1 if ATT_ITEMS[i - 1][0] == 0 else 3
                    act.wait_ge(att_t, i)
                    cp(pp[(i - 1) % 2][3][:, 0:nk * P], banks[:, 6, 0:nk * P]).then_inc(att_tcp, 1)
                if i >= 2:
                    t, h = ATT_ITEMS[i - 2]
                    act.wait_ge(att_o, i - 1)
                    cp(o_d[:, t, h * P:(h + 1) * P], banks[:, 7, 0:P]).then_inc(att_ocp, 1)
            act.wait_ge(att_ocp, n)
            for m in range(T * AH):
                t, h = divmod(m, AH)
                link(act.activation(junk[:, 0:P], o_d[:, t, h * P:(h + 1) * P], ACT.Square, accum_out=s("eb", m, m + 1)))
            act.activation(s("eb", 24, 48), s("eb", 0, 24), ACT.Sqrt, scale=1.0 / (2 * DH), bias=s("eps")).then_inc(od_sq, 1)
            for j in (J_RA[-1], J_RA[-2]):
                wait_job_copied(act, j)
            act.activation(E, E, ACT.Silu).then_inc(gates_on, 1)
            for j in (J_GA[-1], J_GA[-2]):
                wait_job_copied(act, j)
            act.activation(O4[:], O4[:], ACT.Sigmoid).then_inc(gates_on, 1)
            for j in J_GB:
                job_copy(j)
            wait_job_copied(act, J_GB[-1])
            act.activation(A, A, ACT.Sigmoid).then_inc(gates_on, 1)
            family_copies(act, F_OA, lambda k, b: act.activation(oaT[:, k, :], b[:, 0:NT], ACT.Copy, scale=s("gla_g", k % 2, k % 2 + 1)), 0)
            family_copies(act, F_OD, lambda k, b: act.activation(odT[:, k, :], b[:, 0:NT], ACT.Copy, scale=s("sub_g")), 0)
            family_copies(act, F_M, lambda k, b: cp(mT[:, k, :], b[:, 0:NT]), 0)
            for m in range(2):
                act.wait_ge(x1_var, T * (m + 1))
                act.activation(s("std"), s("mv").rearrange("p (t w) -> p t w", w=2)[:, :, 1], ACT.Sqrt,
                               bias=s("eps")).then_inc(x1_std, 1)
            family_copies(act, F_H2, lambda k, b: cp(h2T[:, k, :], b[:, 0:NT]), 0)
            act.wait_ge(rt_max, 1)
            for t in range(T):
                act.activation(aff[:, t, :], banks[:, 4, t * NE:(t + 1) * NE], ACT.Exp, bias=rst[:, 3 + t:4 + t],
                               accum_out=rst[:, 6 + t:7 + t]).then_inc(rt_exp, 1)

            with act.Fori(0, NE) as e:
                act.wait_ge(xe_done, e + 1)
                act.activation(xe, banks[:, 3, :], ACT.Copy).then_inc(xe_cp, 1)
                act.wait_ge(gate_used, e * 4 + 4)
                for b, (i0, i1) in enumerate(FCH):
                    act.activation(hid[:, i0 * P:i1 * P], banks[:, b, 0:(i1 - i0) * P], ACT.Silu).then_inc(silu_done, 1)
                for b, (i0, i1) in enumerate(FCH):
                    act.wait_ge(hidt_done, e * 3 + b + 1)
                    act.activation(hidT[:, i0:i1, :], banks[:, b, 0:(i1 - i0) * P].rearrange("p (i n) -> p i n", n=P),
                                   ACT.Copy).then_inc(hidt_cp, 1)
                act.wait_ge(down_used, e * 4 + 4)
                act.activation(yrow[:, 0:BANK], banks[:, 6, :], ACT.Copy).then_inc(y_cp[0], 1)
            act.wait_ge(f_var, T)
            act.activation(s("std"), s("mv").rearrange("p (t w) -> p t w", w=2)[:, :, 1], ACT.Sqrt,
                           bias=s("eps")).then_inc(f_std, 1)

        @block.vector
        def _(dve):
            steps = [0]

            def note(x):
                steps[0] += 1
                return x.then_inc(v_chain, 1)

            def settle():
                dve.wait_ge(v_chain, steps[0])

            def link(x):
                note(x)
                settle()

            def stats(src):
                bn = s("bn").rearrange("p (t w n) -> p t w n", t=T, n=6)
                for t in range(T):
                    for w in range(2):
                        note(dve.bn_stats(bn[:, t, w, :], src[:, t, w * BANK:(w + 1) * BANK]))
                settle()
                return [dve.bn_aggr(s("mv", 2 * t, 2 * t + 2), bn[:, t].rearrange("p w n -> p (w n)")) for t in range(T)]

            def normalise(dst, src, t):
                return dve.tensor_scalar(dst[:, t, :], src[:, t, :], s("mv", 2 * t, 2 * t + 1), s("rstd", t, t + 1),
                                         ALU.subtract, ALU.mult)

            def job_copy(j):
                kind, chunk, i, who = JOBS[j]
                assert who == "v"
                dve.wait_ge(job_done, j + 1)
                b = banks[:, j % 2, :]
                half = 0 if chunk is None else (chunk - 4) % 2
                cs = slice(half * BANK, (half + 1) * BANK)
                g = min(i, 1)
                if kind == "mod":
                    if chunk == 0:
                        dve.wait_ge(ld_bm, 64)
                    x = dve.tensor_tensor(modrow[:, chunk, :], b, bmod[:, chunk, :], ALU.add)
                elif kind == "ka":
                    x = dve.tensor_copy(qkT[:, 1, i, :], b[:, 0:NT])
                elif kind == "ab":
                    x = dve.tensor_copy(abT, b[0:32, 0:NT])
                elif kind == "al":
                    if i == 0:
                        dve.wait_ge(ld_small, 160)
                    x = dve.tensor_scalar(LG4[:, i // GH, i % GH, :], b[:, 0:NT], s("balpha", i, i + 1), None, ALU.add)
                elif kind == "pa":
                    x = dve.tensor_tensor(merged[:, i, cs], b, ga[:, i, cs], ALU.mult)
                elif kind == "pb":
                    link(dve.tensor_tensor(pbtmp, b, gb[:, i, cs], ALU.mult))
                    x = dve.tensor_tensor(merged[:, i, cs], merged[:, i, cs], pbtmp, ALU.add)
                elif kind == "wo":
                    link(dve.tensor_tensor(wotmp, b, g1b[:, g, cs], ALU.mult))
                    x = dve.scalar_tensor_tensor(out=x_r[:, i, cs], in0=x_r[:, i, cs], scalar=ALPHA, in1=wotmp,
                                                 op0=ALU.mult, op1=ALU.add)
                else:
                    dst = {"vd": vd, "ra": ra, "ga": ga}[kind]
                    x = dve.tensor_copy(dst[:, i, cs], b)
                x.then_inc(job_out["v"], 1)
                if kind in ("pb", "wo"):
                    dve.wait_ge(job_out["v"], copied_before(j, "v") + 1)

            note(dve.memset(s("eps"), EPS))
            note(dve.memset(s("one"), 1.0))
            dve.wait_ge(ld_x, 32)
            for x in stats(x_r):
                x.then_inc(ln_var, 1)
            dve.wait_ge(ln_std, 1)
            link(dve.reciprocal(s("rstd"), s("std")))
            for t in range(T):
                normalise(xn, x_r, t).then_inc(xn_ready, 1)
            dve.wait_ge(zeroed, 1)
            dve.wait_ge(c_turned, 1)
            dve.tensor_copy(cT[:, :, 0:2], banks[:, 4, 0:16].rearrange("p (g k) -> p k g", g=2)).then_inc(c_ready, 1)
            job_copy(J_MOD[0])
            dve.wait_ge(mod_turned, 1)
            mt = banks[:, 5, :].rearrange("p (i j g) -> p i j g", i=4, j=4)
            dve.tensor_copy(s("sh1").rearrange("p (j i g) -> p i j g", j=2, g=2), mt[:, :, 0:2, 0:2]).then_inc(mod_ready, 1)
            dve.tensor_scalar(s("sc1").rearrange("p (j i g) -> p i j g", j=2, g=2), mt[:, :, 2:4, 0:2], 1.0, None,
                              ALU.add).then_inc(mod_ready, 1)
            dve.wait_ge(mod_ready, 2)

            def modulated(k, b):
                sc = s("sc1").rearrange("p (k g) -> p k g", g=2)
                sh = s("sh1").rearrange("p (k g) -> p k g", g=2)
                dve.tensor_scalar(hT[:, k, 0:P], b[:, 0:P], sc[:, k, 0:1], sh[:, k, 0:1], ALU.mult, ALU.add)
                return dve.tensor_scalar(hT[:, k, P:NT], b[:, P:NT], sc[:, k, 1:2], sh[:, k, 1:2], ALU.mult, ALU.add)

            family_copies(dve, F_HT, modulated, 1)
            for j in J_KA + J_AB + J_AL:
                job_copy(j)
            dve.wait_ge(job_out["v"], copied_before(J_AL[-1], "v") + 1)
            for w in range(2):
                note(dve.tensor_tensor(lprod[:, w * DH:(w + 1) * DH], lamv[:, 2 * w * DH:(2 * w + 1) * DH],
                                       lamv[:, (2 * w + 1) * DH:(2 * w + 2) * DH], ALU.mult))
            settle()
            for w in range(2):
                dve.tensor_reduce(s("dots", w, w + 1), lprod[:, w * DH:(w + 1) * DH], AX.X, ALU.add).then_inc(dot_done, 1)
            dve.wait_ge(lg_soft, 1)
            link(dve.scalar_tensor_tensor(out=B, in0=B, scalar=0.0, in1=QE, op0=ALU.min, op1=ALU.subtract))
            link(dve.tensor_scalar(B, B, 1.0 / GLA_TAU, None, ALU.mult))
            for h in range(GH):
                note(dve.tensor_tensor_scan(heads(QE)[:, 1, h, :], resetm, LG4[:, 1, h, :], 0.0, ALU.mult, ALU.add))
                note(dve.tensor_tensor_scan(heads(QE)[:, 0, h, :], resetm, LG4[:, 0, h, :], 0.0, ALU.mult, ALU.add))
            settle()
            QEc = QE.rearrange("p (w c j) -> p w c j", w=2, j=CHUNK)
            KDc = KD.rearrange("p (w c j) -> p w c j", w=2, j=CHUNK)
            full = (P, GH * NCH, CHUNK)
            note(dve.tensor_copy(LG[:, 0, :], QE[:, 0:GH * NT]))
            link(dve.tensor_tensor(LG[:, 1, :], LG[:, 1, :], QE[:, GH * NT:], ALU.subtract))
            link(dve.tensor_tensor(LGc[:, 1], LGc[:, 1], QEc[:, 1, :, CHUNK - 1:CHUNK].to_broadcast(full), ALU.add))
            dve.tensor_tensor(KDc[:, 0], LGc[:, 0, :, CHUNK - 1:CHUNK].to_broadcast(full), LGc[:, 0], ALU.subtract).then_inc(lg_sum, 1)
            dve.tensor_tensor(KDc[:, 1], LGc[:, 1, :, 0:1].to_broadcast(full), LGc[:, 1], ALU.subtract).then_inc(lg_sum, 1)
            both = (P, 2, GH * NT)
            for n, (dst, w) in enumerate(((KD, 1), (QE, 0), (KE, 1))):
                dve.wait_ge(lg_exp, n + 1)
                v = dst.rearrange("p (w m) -> p w m", w=2)
                src = A[:, w * GH * NT:(w + 1) * GH * NT]
                dve.tensor_tensor(v, v, src[:, None].to_broadcast(both), ALU.mult).then_inc(gla_in, 1)
            dve.wait_ge(lg_exp, 4)
            dve.wait_ge(gla_in, 3)
            job_copy(J_MOD[1])
            job_copy(J_MOD[2])
            dve.wait_ge(dot_exp, 1)
            link(dve.tensor_tensor(s("nlam"), s("edots", 1, 2), s("edots", 0, 1), ALU.subtract))
            note(dve.tensor_scalar(s("nlam"), s("nlam"), LAM_INIT, None, ALU.subtract))
            note(dve.tensor_scalar(s("sub_g"), s("sub_g"), 1.0 - LAM_INIT, None, ALU.mult))
            dve.memset(A[:, 0:2048], 0.0).then_inc(gla_kz, 1)
            note(dve.memset(AF, 0.0))
            note(dve.memset(AB, 0.0))
            settle()
            for i, (h, q) in enumerate(GLA_ITEMS):
                nt = len(GLA_TILES[q])
                dve.wait_ge(gla_kt, i + 1)
                sc = banks[:, 3, 0:nt * 2 * P].rearrange("p (a w n) -> p a w n", w=2, n=P)
                for w, dst in enumerate((AF, AB)):
                    for a in range(nt):
                        x = dve.copy_predicated(dst[:, a, :], km[:, w * P:(w + 1) * P], sc[:, a, w, :])
                    x.then_inc(gla_msk, 1)
                dve.wait_ge(gla_msk, 3 * i + 2)
                dve.tensor_tensor(AS[i % 2][:, 0:nt], AF[:, 0:nt], AB[:, 0:nt], ALU.add).then_inc(gla_msk, 1)
                dve.wait_ge(gla_u, i + 1)
                if q == 0 and i >= 2:
                    dve.wait_ge(gla_st, 16 * i)
                if q == 1 and i == 1:
                    dve.wait_ge(ld_s0, 32)
                base = 10 * (i // 2) + (4 if q else 0)
                for u, (w, ch) in enumerate(GLA_UPD[q]):
                    up = banks[:, 4 + u // 2, (u % 2) * DV:(u % 2 + 1) * DV]
                    dst = SV[i % 2][:, u, :]
                    first = u % len([x for x in GLA_UPD[q] if x[0] == w]) == 0
                    if q == 0 and first:
                        dve.tensor_copy(dst, up).then_inc(gla_s, 1)
                        continue
                    prev = S0[:, w, h, :] if first else SV[i % 2][:, u - 1, :]
                    if not first:
                        dve.wait_ge(gla_s, base + u)
                    c0 = h * NCH + ch
                    dve.scalar_tensor_tensor(out=dst, in0=prev, scalar=eb[:, w, c0:c0 + 1], in1=up,
                                             op0=ALU.mult, op1=ALU.add).then_inc(gla_s, 1)
            for j in J_VD:
                if JOBS[j][3] == "v":
                    job_copy(j)
            dve.wait_ge(oa_sq, 1)
            link(dve.reciprocal(s("rsa"), s("msa")))
            for t in range(T):
                v = o_a[:, t, :].rearrange("p (h v) -> p h v", h=GH)
                dve.tensor_tensor(v, v, s("rsa", GH * t, GH * t + GH)[:, :, None].to_broadcast((P, GH, DV)), ALU.mult).then_inc(oa_n, 1)
            family_copies(dve, F_QT, lambda h, b: dve.tensor_copy(qT[:, h, :], b[:, 0:NT]), 1)
            family_copies(dve, F_KT, lambda h, b: dve.tensor_copy(kT[:, h, :], b), 1)

            def neg_max(i):
                t, h = ATT_ITEMS[i]
                nk = SEQ if t == 0 else NKEY - SEQ
                m = 2 * (i % 2)
                dve.wait_ge(att_s, i + 1)
                link(dve.tensor_reduce(s("mx", m, m + 2), banks[:, 2 + m:4 + m, 0:nk], AX.X, ALU.max))
                if i >= 2:
                    dve.wait_ge(att_e, 2 * (i - 1))
                dve.tensor_scalar(s("nb", m, m + 2), s("mx", m, m + 2), -DH ** -0.5, None, ALU.mult).then_inc(att_nb, 1)

            def difference(i):
                t, h = ATT_ITEMS[i]
                nk = SEQ if t == 0 else NKEY - SEQ
                m = 2 * (i % 2)
                p0, p1, pd, _ = (x[:, 0:nk] for x in pp[i % 2])
                dve.wait_ge(att_e, 2 * (i + 1))
                link(dve.reciprocal(s("rs", m, m + 2), s("sum", m, m + 2)))
                note(dve.tensor_scalar(p1, p1, s("rs", m + 1, m + 2), s("nlam"), ALU.mult, ALU.mult))
                settle()
                if i >= 2:
                    dve.wait_ge(att_t, i - 1)
                dve.scalar_tensor_tensor(out=pd, in0=p0, scalar=s("rs", m, m + 1), in1=p1, op0=ALU.mult,
                                         op1=ALU.add).then_inc(att_pd, 1)

            n = len(ATT_ITEMS)
            for i in range(n + 2):
                if i < n:
                    neg_max(i)
                if i % 2 == 0 and i // 2 < len(J_RA + J_GA):
                    j = (J_RA + J_GA)[i // 2]
                    if JOBS[j][3] == "v":
                        job_copy(j)
                if 1 <= i <= n:
                    difference(i - 1)
            dve.wait_ge(oa_n, T)
            dve.wait_ge(gates_on, 1)
            for t in range(T):
                dve.tensor_tensor(o_a[:, t, :], o_a[:, t, :], ra[:, t, :], ALU.mult).then_inc(oa_g, 1)
            dve.wait_ge(od_sq, 1)
            link(dve.reciprocal(s("eb", 0, 24), s("eb", 24, 48)))
            for t in range(T):
                v = o_d[:, t, :].rearrange("p (h v) -> p h v", h=AH)
                dve.tensor_tensor(v, v, s("eb", AH * t, AH * t + AH)[:, :, None].to_broadcast((P, AH, P)), ALU.mult).then_inc(od_g, 1)
            family_copies(dve, F_OA, lambda k, b: dve.tensor_scalar(oaT[:, k, :], b[:, 0:NT], s("gla_g", k % 2, k % 2 + 1), None, ALU.mult), 1)
            family_copies(dve, F_OD, lambda k, b: dve.tensor_scalar(odT[:, k, :], b[:, 0:NT], s("sub_g"), None, ALU.mult), 1)
            dve.wait_ge(gates_on, 3)
            for j in J_PA + J_PB:
                if j == J_PB[0]:
                    wait_job_copied(dve, J_PA[-1])
                job_copy(j)
            family_copies(dve, F_M, lambda k, b: dve.tensor_copy(mT[:, k, :], b[:, 0:NT]), 1)
            dve.wait_ge(bc_loaded, 160)
            for j in J_WO:
                job_copy(j)
            for x in stats(x_r):
                x.then_inc(x1_var, 1)
            dve.wait_ge(x1_std, 1)
            link(dve.reciprocal(s("rstd"), s("std")))
            for t in range(T):
                link(normalise(x_r, x_r, t))
                link(dve.tensor_tensor(x_r[:, t, :], x_r[:, t, :], l1g, ALU.mult))
                link(dve.tensor_tensor(x_r[:, t, :], x_r[:, t, :], l1b, ALU.add))
            for x in stats(x_r):
                x.then_inc(x1_var, 1)
            dve.wait_ge(x1_std, 2)
            link(dve.reciprocal(s("rstd"), s("std")))
            for t in range(T):
                g = min(t, 1)
                link(normalise(h2, x_r, t))
                link(dve.scalar_tensor_tensor(out=h2[:, t, :], in0=sc2b[:, g, :], scalar=1.0, in1=h2[:, t, :],
                                              op0=ALU.add, op1=ALU.mult))
                dve.tensor_tensor(h2[:, t, :], h2[:, t, :], sh2b[:, g, :], ALU.add).then_inc(h2_ready, 1)
            family_copies(dve, F_H2, lambda k, b: dve.tensor_copy(h2T[:, k, :], b[:, 0:NT]), 1)
            dve.wait_ge(rt_log, 1)
            link(dve.tensor_reduce(rst[:, 0:3], banks[:, 4, 0:T * NE].rearrange("p (t e) -> p t e", t=T), AX.X, ALU.max))
            dve.tensor_scalar(rst[:, 3:6], rst[:, 0:3], -1.0, None, ALU.mult).then_inc(rt_max, 1)
            dve.wait_ge(rt_exp, T)
            link(dve.reciprocal(rst[:, 9:12], rst[:, 6:9]))
            dve.tensor_tensor(aff, aff, rst[:, 9:12][:, :, None].to_broadcast((P, T, NE)), ALU.mult).then_inc(rt_aff, 1)
            dve.wait_ge(rt_tr, 1)
            note(dve.tensor_copy(affT, banks[0:NE, 5, 0:NT]))
            note(dve.memset(slots, -1.0))
            link(dve.memset(gates, 0.0))
            for a, b, s0, cap in ((0, SEQ, CTX0, CAP_C), (SEQ, NT, LAT0, CAP_L)):
                for r in range(cap // 8):
                    v = gates[:, s0 + 8 * r:s0 + 8 * r + 8]
                    link(dve.max(v, affT[:, a:b]))
                    note(dve.max_index(idxu[:, s0 + 8 * r:s0 + 8 * r + 8], v, affT[:, a:b]))
                    if r < cap // 8 - 1:
                        settle()
                        link(dve.match_replace(affT[:, a:b], v, affT[:, a:b], -1.0))
            settle()
            note(dve.tensor_scalar(slots[:, LAT0:LAT0 + CAP_L], idxu[:, LAT0:LAT0 + CAP_L], float(SEQ), None, ALU.add))
            link(dve.tensor_copy(slots[:, CTX0:CTX0 + CAP_C], idxu[:, CTX0:CTX0 + CAP_C]))
            link(dve.tensor_copy(slots[:, SLOT:2 * SLOT], slots[:, 0:SLOT]))
            dve.tensor_copy(slots[:, 0:1], slots[:, 0:1]).then_inc(rt_slots, 1)
            dve.tensor_copy(gates[:, SLOT:2 * SLOT], gates[:, 0:SLOT]).then_inc(rt_slots, 1)
            dve.memset(O1[:], 0.0).then_inc(acc_done, 6)
            dve.wait_ge(acc_done, 6)
            dve.wait_ge(rt_tt, 1)
            dve.tensor_copy(idxT, banks[:, 6, 0:NE]).then_inc(rt_cols, 1)
            dve.tensor_copy(gateT, banks[:, 6, NE:2 * NE]).then_inc(rt_cols, 1)
            dve.wait_ge(rt_cols, 2)
            dve.wait_ge(rt_bc, 16)

            with dve.Fori(0, NE) as e:
                for t in range(T):
                    dve.tensor_scalar(sel[:, t, :], slot_bc[:, bass.ds(e, 1), :].rearrange("p e s -> p (e s)"),
                                      iota_c[:, t:t + 1], None, ALU.is_equal).then_inc(sel_ready, 1)
                dve.tensor_scalar(selT, iota_r, idxT[:, bass.ds(e, 1)], gateT[:, bass.ds(e, 1)],
                                  ALU.is_equal, ALU.mult).then_inc(selT_ready, 1)
                dve.wait_ge(xet_done, e + 1)
                dve.tensor_copy(xeT, banks[:, 4, :].rearrange("p (i n) -> p i n", n=P)).then_inc(xet_cp, 1)
                dve.wait_ge(up_used, e * 4 + 4)
                for b, (i0, i1) in enumerate(FCH):
                    dve.wait_ge(silu_done, e * 3 + b + 1)
                    dve.tensor_tensor(hid[:, i0 * P:i1 * P], hid[:, i0 * P:i1 * P], banks[:, 3 + b, 0:(i1 - i0) * P],
                                      ALU.mult).then_inc(hid_done, 1)
                dve.wait_ge(down_used, e * 4 + 4)
                dve.tensor_copy(yrow[:, BANK:2 * BANK], banks[:, 7, :]).then_inc(y_cp[1], 1)
                for t in range(T):
                    for dc in range(2):
                        n = 2 * t + dc
                        dve.wait_ge(comb_done, e * 6 + n + 1)
                        dst = acc[:, t, dc * BANK:(dc + 1) * BANK]
                        dve.tensor_tensor(dst, dst, banks[:, n, :], ALU.add).then_inc(acc_done, 1)

            dve.wait_ge(acc_done, 6 * NE + 6)
            dve.wait_ge(ld_end, 64)
            for t in range(T):
                link(dve.tensor_tensor(acc[:, t, :], acc[:, t, :], g2b[:, min(t, 1), :], ALU.mult))
                link(dve.scalar_tensor_tensor(out=x_r[:, t, :], in0=x_r[:, t, :], scalar=ALPHA, in1=acc[:, t, :],
                                              op0=ALU.mult, op1=ALU.add))
            for x in stats(x_r):
                x.then_inc(f_var, 1)
            dve.wait_ge(f_std, 1)
            link(dve.reciprocal(s("rstd"), s("std")))
            for t in range(T):
                link(normalise(x_r, x_r, t))
                link(dve.tensor_tensor(x_r[:, t, :], x_r[:, t, :], l2g, ALU.mult))
                dve.tensor_tensor(x_r[:, t, :], x_r[:, t, :], l2b, ALU.add).then_inc(f_ready, 1)


_INS = ["x_prompt", "x_sample", "cache_diff_k", "cache_diff_v", "state_gla_fwd", "state_gla_bwd", "c", "c_ctx",
        "w_mod", "b_mod", "w_in", "w_alpha_f", "b_alpha_f", "w_alpha_b", "b_alpha_b", "gla_norm_g", "w_proj_a",
        "lambda_q1", "lambda_k1", "lambda_q2", "lambda_k2", "subln_g", "w_proj_b", "w_out", "ln1_g", "ln1_b",
        "w_router", "w_exp_gate", "w_exp_up", "w_exp_down", "ln2_g", "ln2_b"]
_OUTS = [(1, SEQ, D), (1, DEC, D), (1, 1, SEQ, AH, 2, DH), (1, 1, SEQ, AH, 2 * DH), (1, 1, GH, DK, DV), (1, 1, GH, DK, DV)]


def kernel(**inputs):
    import concourse.bacc as _bacc
    from concourse.bass_utils import run_bass_kernel_spmd as _run

    nc = _bacc.Bacc("TRN2", target_bir_lowering=False, num_devices=1)
    arrays, args = {}, []
    given = [(n, np.ascontiguousarray(inputs[n])) for n in _INS]
    given += list(zip(("const_f", "const_m", "const_r"), host_constants()))
    for name, a in given:
        arrays[f"in_{name}"] = a
        args.append(nc.dram_tensor(f"in_{name}", a.shape, mybir.dt.from_np(a.dtype), kind="ExternalInput").ap())
    for i, shape in enumerate(_OUTS):
        args.append(nc.dram_tensor(f"out_{i}", shape, F32, kind="ExternalOutput").ap())
    trunk_layer(nc, *args)
    r = _run(nc, [arrays], core_ids=[0])
    return tuple(r.results[0][f"out_{i}"] for i in range(len(_OUTS)))
```

```python
from collections import namedtuple
from contextlib import ExitStack

import numpy as np
import concourse.bass as bass
from concourse import mybir

ALU = mybir.AluOpType
ACT = mybir.ActivationFunctionType
AX = mybir.AxisListType
F32 = mybir.dt.float32
I32 = mybir.dt.int32
U32 = mybir.dt.uint32

P = 128
D = 1024
KT = D // P
SEQ, DEC, PAST = 128, 256, 128
T = (SEQ + DEC) // P
NT = T * P
BANK = 512
GRID_W = 64

GH, DK, DV, RANK, CHUNK = 4, 128, 256, 16, 64
NCH = NT // CHUNK
GLA_TAU = 16.0
AH, DH = 8, 64
NKEY = NT + PAST
LAM_INIT = 0.8 - 0.6
ROPE_HALF = DH // 4
NE, FF = 16, 2816
CAP_C, CAP_L = 2 * SEQ // NE, 2 * DEC // NE
SLOT = 64
LAT0, CTX0, END0 = 0, CAP_L, CAP_L + CAP_C
ALPHA = 2.0 ** 0.25
EPS = 1e-6

C_QA, C_KA, C_VA, C_RA = 0, 512, 1024, 2048
C_AB = 3072
C_QD = C_AB + 2 * RANK
C_KD, C_VD, C_GA, C_GB = C_QD + D, C_QD + 2 * D, C_QD + 3 * D, C_QD + 4 * D

WCHUNKS = ([("mod", (0, ks)) for ks in range(4)] + [("in", C_QA), ("in", C_KA), ("in", C_VA), ("in", C_VA + BANK)]
           + [("in", c0 + h * BANK) for c0 in (C_QD, C_KD, C_VD) for h in range(2)])
for _n, _c in enumerate((C_RA, C_RA + BANK, C_GA, C_GA + BANK)):
    WCHUNKS += [("in", _c)] + [("mod", (1 + _n // 2, 2 * (_n % 2) + ks)) for ks in range(2)]
WCHUNKS += [("in", C_GB), ("in", C_GB + BANK)] + [(w, h * BANK) for w in ("pa", "pb", "out") for h in range(2)]
WSLOTS = 4
CHUNK_OF = {c: n for n, c in enumerate(WCHUNKS)}

Job = namedtuple("Job", "kind chunk i half engine")
JOBS = []


def _job(kind, chunk, i, half, engine):
    JOBS.append(Job(kind, chunk, i, half, engine))
    return len(JOBS) - 1


def _in_jobs(kind, c0, engines):
    return [_job(kind, CHUNK_OF["in", c0 + h * BANK], t, h, engines[(h * T + t) % len(engines)])
            for h in range(2) for t in range(T)]


def _out_jobs(kind, w, tile_major):
    order = [(t, h) for t in range(T) for h in range(2)] if tile_major else [(t, h) for h in range(2) for t in range(T)]
    return [_job(kind, CHUNK_OF[w, h * BANK], t, h, "v") for t, h in order]


J_MOD0 = _job("mod", 0, 0, 0, "v")
J_AB = _job("ab", None, 0, 0, "v")
J_QA, J_AL = [], []
for _h in range(GH):
    J_QA.append(_job("qa", CHUNK_OF["in", C_QA], _h, 0, "a"))
    J_AL += [_job("al", None, 2 * _h + _i, 0, "v") for _i in range(2)]
J_KA = [_job("ka", CHUNK_OF["in", C_KA], _h, 0, "v") for _h in range(GH)]
J_VA = _in_jobs("va", C_VA, "a")
J_QD = _in_jobs("qd", C_QD, "a")
J_KD = _in_jobs("kd", C_KD, "a")
J_VD = _in_jobs("vd", C_VD, "av")
ATT_JOBS, J_RA, J_GA, J_MOD = [], [], [], {1: [], 2: []}
for _n in range(4 * T):
    _kind, _c0, _to = ("ra", C_RA, J_RA) if _n < 2 * T else ("ga", C_GA, J_GA)
    _h, _t = divmod(_n % (2 * T), T)
    _to.append(_job(_kind, CHUNK_OF["in", _c0 + _h * BANK], _t, _h, "av"[_n % 2]))
    ATT_JOBS.append([_to[-1]])
    if _t < 2:
        _b, _ks = 1 + _n // (2 * T), 2 * _h + _t
        J_MOD[_b].append(_job("mod", CHUNK_OF["mod", (_b, _ks)], _b, _ks, "v"))
        ATT_JOBS[-1].append(J_MOD[_b][-1])
J_GB = _in_jobs("gb", C_GB, "a")
J_PA = _out_jobs("pa", "pa", False)
J_PB = _out_jobs("pb", "pb", True)
J_WO = _out_jobs("wo", "out", True)


def copied_before(j, engine):
    return sum(1 for job in JOBS[:j] if job.engine == engine)


def last_job_of(chunk):
    return J_MOD0 if chunk < 4 else max(j for j, job in enumerate(JOBS) if job.chunk == chunk)


GLA_ITEMS = [(h, s) for h in range(GH) for s in range(2)]
GLA_TILES = {0: [0], 1: [1, 2]}
GLA_UPD = {0: [(0, 0), (0, 1), (1, 1), (1, 0)], 1: [(0, 2), (0, 3), (0, 4), (1, 5), (1, 4), (1, 3)]}

ATT_ITEMS = [(t, h) for t in range(T) for h in range(AH)]

F_HT, F_QT, F_KT, F_OA, F_OD = ((KT * f, KT) for f in range(5))
F_M, F_H2 = ((5 * KT + 2 * T * f, 2 * T) for f in range(2))

SM = {}
_at = 0
for _name, _n in (("sc1", 16), ("sh1", 16), ("bn", 36), ("mv", 6), ("std", 3), ("rstd", 3), ("eps", 1), ("one", 1),
                  ("eb", 48), ("balpha", 8), ("gla_g", 2), ("sub_g", 1), ("dots", 2), ("edots", 2),
                  ("nlam", 1), ("mx", 4), ("nb", 4), ("sum", 4), ("rs", 4), ("msa", 12), ("rsa", 12)):
    SM[_name] = (_at, _at + _n)
    _at += _n
SM_N = _at


def host_constants():
    pos = np.arange(DEC)
    inv = (10000.0 ** (-np.arange(ROPE_HALF, dtype=np.float32) / ROPE_HALF)).astype(np.float32)
    ang = np.stack([(pos // GRID_W).astype(np.float32)[:, None] * inv,
                    (pos % GRID_W).astype(np.float32)[:, None] * inv], 1)
    ang = ang.reshape(2, P, 2 * ROPE_HALF).transpose(1, 0, 2).reshape(P, -1)
    f = np.concatenate([np.eye(P), np.cos(ang), np.sin(ang),
                        np.arange(P)[:, None] + P * np.arange(T)[None]], 1).astype(np.float32)
    j, i = np.arange(P)[:, None], np.arange(P)[None]
    same = (j // CHUNK) == (i // CHUNK)
    m = np.concatenate([same & (j <= i), same & (j >= i)], 1).astype(np.int32)
    r = np.stack([(np.arange(NT) % CHUNK != 0), np.arange(NT)]).astype(np.float32)
    return f, m, r


CF_N = P + 4 * ROPE_HALF * 2 + T

QUARTER = 2 * FF
RING = 6 * QUARTER
FT = FF // (2 * P)
DOWN_GROUPS = [(0, 3), (3, 6), (6, 9), (9, 11)]
DOWN0 = 2 * QUARTER
HALF = FF // 2
FCH = [(0, 4), (4, 8), (8, 11)]

UNIT = T * D
WS0 = RING - WSLOTS * KT * BANK


def trunk_layer(nc, x_prompt, x_sample, cache_k, cache_v, st_f, st_b, c, c_ctx, w_mod, b_mod, w_in,
                w_alpha_f, b_alpha_f, w_alpha_b, b_alpha_b, gla_g, w_pa, lq1, lk1, lq2, lk2, sub_g, w_pb,
                w_out, ln1_g, ln1_b, w_router, w_gate, w_up, w_down, ln2_g, ln2_b, k_f, k_m, k_r,
                y_prompt, y_sample, new_k, new_v, new_f, new_b):
    mods = nc.dram_tensor("mods", (2, 6, D), F32, kind="Internal").ap()
    slot_tokens = nc.dram_tensor("slot_tokens", (NE, SLOT), F32, kind="Internal").ap()
    with ExitStack() as ctx:
        ctx.enter_context(nc.allow_non_contiguous_dma(reason="a few short vectors, one value per partition"))

        def sb(name, shape, dt=F32):
            return ctx.enter_context(nc.sbuf_tensor(name, shape, dt))

        def sem(name):
            return ctx.enter_context(nc.semaphore(name))

        ring = sb("ring", [P, RING])
        X, H, O1, O2, O3, O4 = (sb(n, [P, UNIT]) for n in ("X", "H", "O1", "O2", "O3", "O4"))
        kf = sb("kf", [P, CF_N])
        km = sb("km", [P, 2 * P], I32)
        cT = sb("cT", [P, KT, 32])
        sm = sb("sm", [P, SM_N])
        banks = ctx.enter_context(nc.psum_tensor("banks", [P, 8, BANK], F32))

        ident = kf[:, 0:P]
        ropec = kf[:, P:P + 64].rearrange("p (t a i) -> p t a i", t=2, a=2)
        ropes = kf[:, P + 64:P + 128].rearrange("p (t a i) -> p t a i", t=2, a=2)
        iota_c = kf[:, P + 128:P + 128 + T]

        def s(name, a=0, b=None):
            lo, hi = SM[name]
            return sm[:, lo + a:(lo + b if b is not None else hi)]

        def rows(t):
            return t.rearrange("p (t d) -> p t d", t=T)

        def cols(t):
            return t.rearrange("p (k n) -> p k n", n=NT)

        def reg(a, n):
            return ring[:, a:a + n]

        wslot = [reg(WS0 + i * KT * BANK, KT * BANK).rearrange("p (k n) -> p k n", k=KT) for i in range(WSLOTS)]
        A, B, C = reg(0, UNIT), reg(UNIT, UNIT), reg(2 * UNIT, UNIT)
        Dm, E = reg(3 * UNIT, UNIT), reg(4 * UNIT, UNIT)
        spare = reg(5 * UNIT, 2048)
        hT = cols(H[:])
        x_r, xn = rows(X[:]), rows(O2[:])
        wab = O3[:, 0:256].rearrange("p (k n) -> p k n", k=KT)
        wal = O3[0:32, 256:1280]
        abT = O3[0:32, 1280:1280 + NT]
        lamv = O3[:, 1664:1920]
        crow = O3[0:16, 1920:2048]
        crow_s = O3[0:16, 2048:2176]
        lprod = O3[:, 2176:2304]
        modrow0, bmod0 = O1[:, 0:BANK], O1[:, BANK:2 * BANK]
        resetm = O4[:, 0:NT]
        qkT = A.rearrange("p (w h n) -> p w h n", w=2, h=GH)
        LG = B.rearrange("p (w m) -> p w m", w=2)
        LG4 = B.rearrange("p (w h n) -> p w h n", w=2, h=GH)
        LGc = B.rearrange("p (w c j) -> p w c j", w=2, j=CHUNK)
        QE, KE, KD = Dm, E, O2[:]

        def heads(t):
            return t.rearrange("p (w h n) -> p w h n", w=2, h=GH)

        va = rows(C)
        kdn = [A[:, i * 1024:(i + 1) * 1024].rearrange("p (a w r n) -> p a w r n", w=2, r=2, n=P) for i in range(2)]
        AF = A[:, 2048:2304].rearrange("p (a n) -> p a n", n=P)
        AB = A[:, 2304:2560].rearrange("p (a n) -> p a n", n=P)
        AS = [A[:, 2560 + 256 * i:2816 + 256 * i].rearrange("p (a n) -> p a n", n=P) for i in range(2)]
        S0 = spare.rearrange("p (w h v) -> p w h v", w=2, h=GH)
        SV = [B[:, i * 1536:(i + 1) * 1536].rearrange("p (u v) -> p u v", v=DV) for i in range(2)]
        eb = s("eb").rearrange("p (w c) -> p w c", w=2)
        o_a = rows(O1[:])
        modrow = spare[:, 0:2 * BANK].rearrange("p (b n) -> p b n", b=2)
        bmod = spare[:, 2 * BANK:4 * BANK].rearrange("p (b n) -> p b n", b=2)
        qd, kd, vd = rows(O3[:]), rows(O4[:]), rows(O2[:])
        qT = cols(reg(0, UNIT))
        kT = reg(UNIT, AH * NKEY).rearrange("p (h n) -> p h n", n=NKEY)
        vc = reg(7168, D)
        kc = reg(8192, D)
        qz = [reg(8192 + 256 * i, 256).rearrange("p (q n) -> p q n", q=2) for i in range(2)]
        rope_q = [Dm[:, i * 512:(i + 1) * 512] for i in range(4)]
        rope_k = [A[:, i * 512:(i + 1) * 512] for i in range(4)]
        pp = [[Dm[:, (i * 4 + q) * 384:(i * 4 + q + 1) * 384] for q in range(4)] for i in range(2)]
        o_d = rows(O3[:])
        ra, ga, gb = rows(E), rows(O4[:]), rows(reg(0, UNIT))
        merged = rows(reg(UNIT, UNIT))
        oaT, odT = cols(reg(2 * UNIT, UNIT)), cols(Dm)
        pbtmp = spare[:, 2 * BANK:3 * BANK]
        mT = cols(H[:])
        wotmp = reg(WS0 - BANK, BANK)
        g1b = O1[:, 0:2 * D].rearrange("p (g d) -> p g d", g=2)
        l1g, l1b = O1[:, 2 * D:3 * D], O2[:, 0:D]
        sh2b = O2[:, D:3 * D].rearrange("p (g d) -> p g d", g=2)
        sc2b = O3[:, 0:2 * D].rearrange("p (g d) -> p g d", g=2)
        wr = O3[:, 2 * D:2 * D + KT * NE].rearrange("p (k e) -> p k e", k=KT)
        iota_r = O3[:, 2560:2560 + NT]
        h2 = rows(O4[:])
        h2T = cols(H[:])
        r0 = 2 * D + KT * NE
        aff = O3[:, r0:r0 + T * NE].rearrange("p (t e) -> p t e", t=T)
        rst = O3[:, r0 + 48:r0 + 64]
        affT = O1[0:NE, D:D + NT]
        slots = O1[0:NE, D + 384:D + 512]
        gates = O1[0:NE, D + 512:D + 640]
        idxu = O1[0:NE, D + 640:D + 704].bitcast(U32)
        idxT, gateT = H[:, 704:720], H[:, 720:736]
        slot_bc = H[:, 1024:1024 + NE * SLOT].rearrange("p (e s) -> p e s", e=NE)
        g2s, l2g, l2b = (O1[:, i * D:(i + 1) * D] for i in range(3))
        hid = O2[:, 0:HALF]
        hidT = O2[:, HALF:2 * HALF].rearrange("p (i n) -> p i n", n=P)
        sel = O2[:, 2 * HALF:2 * HALF + T * SLOT].rearrange("p (t s) -> p t s", t=T)
        xe = O3[:, 0:BANK]
        xeT = O3[:, BANK:2 * BANK].rearrange("p (i n) -> p i n", n=P)
        yrow = O3[:, 2 * BANK:4 * BANK]
        selT = O3[:, 4 * BANK:4 * BANK + NT]
        def bank(i, n=BANK):
            return banks[:, i, 0:n]

        ld_x = [sem("x_context_loaded"), sem("x_latent_loaded")]
        ld_c = sem("conditioning_loaded")
        ld_k = sem("constants_loaded")
        ld_bm = sem("mod_bias_loaded")
        ld_ab = sem("decay_weights_loaded")
        ld_small = sem("small_vectors_loaded")
        ld_s0 = sem("cached_states_loaded")
        ld_cache = sem("cached_kv_loaded")
        wsem = [sem(f"weight_slot{i}_loaded") for i in range(WSLOTS)]
        zeroed = sem("zeroed_by_gpsimd")
        v_chain = sem("vector_steps")
        a_chain = sem("scalar_steps")
        g_chain = sem("gpsimd_steps")
        c_silu = sem("c_silu")
        c_turned = sem("c_turned")
        c_ready = sem("c_ready")
        ln_var = sem("ln_variances")
        ln_std = sem("ln_deviations")
        xn_ready = sem("x_normalised")
        mod_turned = sem("mod_turned")
        mod_ready = sem("mod_columns_ready")
        ht_out = [sem("modulated_by_scalar"), sem("modulated_by_vector")]
        mod_stored = sem("mod_rows_stored")
        job_done = sem("job_done")
        job_out = {"a": sem("job_copied_by_scalar"), "v": sem("job_copied_by_vector")}
        tb_done = sem("turned")
        tb_out = [sem("turned_copied_by_scalar"), sem("turned_copied_by_vector")]
        lg_soft = sem("gate_softplus")
        lg_sum = sem("decay_sums")
        lg_exp = sem("decay_exps")
        gla_in = sem("gla_operands")
        gla_kt = sem("gla_turned_and_scores")
        gla_kz = sem("gla_keys_zeroed")
        gla_kcp = sem("gla_keys_copied")
        gla_msk = sem("gla_scores_masked")
        gla_u = sem("gla_updates")
        gla_s = sem("gla_states")
        gla_st = sem("gla_states_stored")
        gla_o = sem("gla_outputs")
        gla_ocp = sem("gla_outputs_copied")
        oa_sq = sem("gla_deviations")
        oa_n = sem("gla_normalised")
        dot_done = sem("lambda_dots")
        dot_exp = sem("lambda_exps")
        rope_done = {"q": sem("rope_queries_done"), "k": sem("rope_keys_done")}
        rope_tmp = {"q": sem("rope_query_products"), "k": sem("rope_key_products")}
        q_zero = sem("padded_queries_zeroed")
        q_pad = sem("queries_padded")
        kv_stored = sem("new_kv_stored")
        att_s = sem("att_scores")
        att_nb = sem("att_neg_max")
        att_e = sem("att_exps")
        att_pd = sem("att_diff_probs")
        att_t = sem("att_probs_turned")
        att_tcp = sem("att_probs_turned_copied")
        att_o = sem("att_outputs")
        att_ocp = sem("att_outputs_copied")
        od_sq = sem("att_deviations")
        gates_on = sem("gates_on")
        oa_g = sem("gla_gated")
        od_g = sem("att_normalised")
        bc_loaded = sem("broadcast_rows_loaded")
        x1_var = [sem("x1_variances"), sem("h2_variances")]
        x1_std = [sem("x1_deviations"), sem("h2_deviations")]
        h2_ready = sem("h2_ready")
        rt_log = sem("router_logits")
        rt_max = sem("router_neg_max")
        rt_exp = sem("router_exps")
        rt_aff = sem("router_probs")
        rt_tr = sem("router_probs_turned")
        rt_slots = sem("slots_ready")
        rt_stored = sem("slots_stored")
        rt_bc = sem("slots_broadcast")
        rt_tt = sem("slots_turned")
        rt_cols = sem("slot_columns_ready")
        land_g = [sem(f"gate_quarter{i}_loaded") for i in range(4)]
        land_u = [sem(f"up_quarter{i}_loaded") for i in range(4)]
        land_d = [sem(f"down_group{i}_loaded") for i in range(4)]
        gate_used = sem("gate_quarters_used")
        up_used = sem("up_quarters_used")
        down_used = sem("down_groups_used")
        sel_ready = sem("selection_ready")
        selT_ready = sem("combination_ready")
        xe_done = sem("expert_rows_done")
        xe_cp = sem("expert_rows_copied")
        xet_done = sem("expert_columns_done")
        xet_cp = sem("expert_columns_copied")
        silu_done = sem("gate_silu")
        hid_done = sem("hidden_ready")
        hidt_done = sem("hidden_turned")
        hidt_cp = sem("hidden_turned_copied")
        y_cp = sem("expert_out_copied")
        comb_done = sem("combined")
        acc_done = sem("accumulated")
        ld_g2 = sem("gate_rows_loaded")
        ld_end = sem("last_rows_loaded")
        f_var = sem("final_variances")
        f_std = sem("final_deviations")
        f_ready = sem("final_rows")
        stored = sem("outputs_stored")

        block = ctx.enter_context(nc.Block())

        def wait_job_copied(eng, j):
            who = JOBS[j].engine
            eng.wait_ge(job_out[who], copied_before(j, who) + 1)

        def wait_family(eng, f):
            for out in tb_out:
                eng.wait_ge(out, (f[0] + f[1]) // 2)

        def wait_tile(eng, f, t):
            for out in tb_out:
                eng.wait_ge(out, f[0] // 2 + t + 1)

        def rope(eng, key, src, t, tmp, n):
            v = src[:, t, :].rearrange("p (g a w i) -> p g a w i", a=2, w=2, i=ROPE_HALF)
            cs = ropec[:, t - 1][:, None].to_broadcast((P, 16, 2, ROPE_HALF))
            sn = ropes[:, t - 1][:, None].to_broadcast((P, 16, 2, ROPE_HALF))
            tmp = [x.rearrange("p (g a i) -> p g a i", a=2, i=ROPE_HALF) for x in tmp]
            if n:
                eng.wait_ge(rope_done[key], 2 * n)
            for i, (half, tab) in enumerate(((0, cs), (1, sn), (0, sn), (1, cs))):
                eng.tensor_tensor(tmp[i], v[:, :, :, half, :], tab, ALU.mult).then_inc(rope_tmp[key], 1)
            eng.wait_ge(rope_tmp[key], 4 * (n + 1))
            eng.tensor_tensor(v[:, :, :, 0, :], tmp[0], tmp[1], ALU.subtract).then_inc(rope_done[key], 1)
            eng.tensor_tensor(v[:, :, :, 1, :], tmp[2], tmp[3], ALU.add).then_inc(rope_done[key], 1)

        def w_chunk(n):
            kind, c0 = WCHUNKS[n]
            if kind == "mod":
                b, ks = c0
                return w_mod[0].rearrange("(k p) n -> p k n", p=P)[:, 2 * ks:2 * ks + 2, 4 * BANK * b:4 * BANK * (b + 1)]
            w = {"in": w_in, "pa": w_pa, "pb": w_pb, "out": w_out}[kind]
            return w[0].rearrange("(k p) n -> p k n", p=P)[:, :, c0:c0 + BANK]

        def w_slot(n):
            if WCHUNKS[n][0] == "mod":
                return wslot[n % WSLOTS].rearrange("p k n -> p (k n)").rearrange("p (k n) -> p k n", k=2)
            return wslot[n % WSLOTS]

        gate_v = [w_gate[0], w_up[0]]

        @block.sync
        def _(sp):
            sp.dma_start(crow[0:8, :], c_ctx.rearrange("(k p) -> k p", p=P)).then_inc(ld_c, 16)
            sp.dma_start(crow[8:16, :], c.rearrange("b (k p) -> (b k) p", p=P)).then_inc(ld_c, 16)
            sp.dma_start(kf[:], k_f).then_inc(ld_k, 16)
            sp.dma_start(x_r[:, 0, :], x_prompt[0]).then_inc(ld_x[0], 16)
            sp.dma_start(x_r[:, 1:3, :], x_sample[0].rearrange("(t p) d -> p t d", p=P)).then_inc(ld_x[1], 16)
            for n in range(len(WCHUNKS)):
                if n >= WSLOTS:
                    sp.wait_ge(job_done, last_job_of(n - WSLOTS) + 1)
                sp.dma_start(w_slot(n), w_chunk(n)).then_inc(wsem[n % WSLOTS], 16)

            def gate_up(w, e, q):
                return gate_v[w][e].rearrange("(k p) f -> p k f", p=P)[:, 2 * q:2 * q + 2, :]

            def quarter(i):
                return reg(i * QUARTER, QUARTER).rearrange("p (k f) -> p k f", k=2)

            def down(e, g):
                a, b = DOWN_GROUPS[g]
                sp.dma_start(reg(DOWN0 + 2 * a * D, 2 * (b - a) * D).rearrange("p (i d) -> p i d", d=D),
                             w_down[0][e].rearrange("(i p) d -> p i d", p=P)[:, 2 * a:2 * b, :]).then_inc(land_d[g], 16)

            wait_family(sp, F_M)
            for q in range(4):
                if q == 3:
                    wait_job_copied(sp, J_WO[-1])
                sp.dma_start(quarter(q), gate_up(0, 0, q)).then_inc(land_g[q], 16)
            for q in range(4):
                if q >= 2:
                    sp.wait_ge(gate_used, q - 1)
                sp.dma_start(quarter((4 + q) % 6), gate_up(1, 0, q)).then_inc(land_u[q], 16)
            for g in range(4):
                if g == 0:
                    sp.wait_ge(gate_used, 4)
                else:
                    sp.wait_ge(up_used, min(g, 2))
                down(0, g)
            with sp.Fori(1, NE) as e:
                for q, (used, n) in enumerate(((up_used, 1), (up_used, 0), (down_used, 3), (down_used, 2))):
                    sp.wait_ge(used, e * 4 - n)
                    sp.dma_start(quarter(q), gate_up(0, e, q)).then_inc(land_g[q], 16)
                for q, (used, n) in enumerate(((down_used, -1), (down_used, 0), (gate_used, 1), (gate_used, 2))):
                    sp.wait_ge(used, e * 4 + n)
                    sp.dma_start(quarter((4 + q) % 6), gate_up(1, e, q)).then_inc(land_u[q], 16)
                for g, (used, n) in enumerate(((gate_used, 4), (up_used, 1), (up_used, 2), (up_used, 2))):
                    sp.wait_ge(used, e * 4 + n)
                    down(e, g)
            for t in range(T):
                sp.wait_ge(f_ready, t + 1)
                dst = y_prompt[0] if t == 0 else y_sample[0, (t - 1) * P:t * P, :]
                sp.dma_start(dst, x_r[:, t, :]).then_inc(stored, 16)
            sp.wait_ge(stored, 16 * T)
            sp.wait_ge(kv_stored, 32)
            sp.wait_ge(gla_st, 16 * 2 * GH)

        @block.gpsimd
        def _(pool):
            pool.memset(cT[:], 0.0).then_inc(zeroed, 1)
            pool.memset(wal, 0.0).then_inc(zeroed, 1)
            for j in range(4):
                pool.dma_start(bmod0[32 * j:32 * j + 32], b_mod[:, j * BANK:(j + 1) * BANK].to_broadcast((32, BANK))).then_inc(ld_bm, 16)
            pool.dma_start(wab, w_in[0].rearrange("(k p) n -> p k n", p=P)[:, :, C_AB:C_AB + 2 * RANK]).then_inc(ld_ab, 16)
            pool.wait_ge(zeroed, 2)
            pool.dma_start(wal[0:RANK, 0:GH * DK], w_alpha_f[0]).then_inc(ld_ab, 16)
            pool.dma_start(wal[RANK:2 * RANK, GH * DK:2 * GH * DK], w_alpha_b[0]).then_inc(ld_ab, 16)
            pool.dma_start(s("balpha", 0, 4), b_alpha_f[0].rearrange("(h p) -> p h", p=P)).then_inc(ld_small, 16)
            pool.dma_start(s("balpha", 4, 8), b_alpha_b[0].rearrange("(h p) -> p h", p=P)).then_inc(ld_small, 16)
            pool.dma_start(resetm, k_r[0:1].to_broadcast((P, NT))).then_inc(ld_small, 16)
            pool.dma_start(km[:], k_m).then_inc(ld_small, 16)
            pool.dma_start(s("gla_g"), gla_g[0].rearrange("(a p) -> p a", p=P)).then_inc(ld_small, 16)
            pool.dma_start(s("sub_g"), sub_g[0].rearrange("(a p) -> p a", p=P)).then_inc(ld_small, 16)
            for i, v in enumerate((lq1, lk1, lq2, lk2)):
                pool.dma_start(lamv[:, i * DH:(i + 1) * DH], v.to_broadcast((P, DH))).then_inc(ld_small, 16)
            for w, st in enumerate((st_f, st_b)):
                pool.dma_start(S0[:, w], st[0, 0].rearrange("h k v -> k h v")).then_inc(ld_s0, 16)
            for h in range(GH):
                i = 2 * h
                pool.wait_ge(gla_s, 10 * h + 4)
                for w, dst in enumerate((new_f, new_b)):
                    pool.dma_start(dst[0, 0, h], SV[i % 2][:, 2 * w + 1, :]).then_inc(gla_st, 16)
            for j in (J_KD[0], J_KD[3]):
                wait_job_copied(pool, j)
            pool.dma_start(new_k[0, 0].rearrange("t h c d -> t (h c d)"), kd[:, 0, :]).then_inc(kv_stored, 16)
            pool.wait_ge(gla_o, len(GLA_ITEMS))
            pool.dma_start(kc, cache_k[0, 0].rearrange("t h c d -> t (h c d)")).then_inc(ld_cache, 16)
            pool.dma_start(vc, cache_v[0, 0].rearrange("t h d -> t (h d)")).then_inc(ld_cache, 16)
            for j in range(4):
                src = b_mod.rearrange("o (b j n) -> o j b n", b=3, j=4)[:, j, 1:3]
                pool.dma_start(bmod[32 * j:32 * j + 32], src.to_broadcast((32, 2, BANK))).then_inc(ld_bm, 16)
            for j in J_QD[-2:]:
                wait_job_copied(pool, j)
            for t in (1, 2):
                rope(pool, "q", qd, t, rope_q, t - 1)
            for j in (J_VD[0], J_VD[3]):
                wait_job_copied(pool, j)
            pool.dma_start(new_v[0, 0].rearrange("t h d -> t (h d)"), vd[:, 0, :]).then_inc(kv_stored, 16)
            pool.wait_ge(tb_done, F_KT[0] + F_KT[1])
            wait_family(pool, F_QT)
            for i in range(2):
                pool.memset(qz[i], 0.0).then_inc(q_zero, 1)
            pool.wait_ge(q_zero, 2)
            for i, (t, h) in enumerate(ATT_ITEMS):
                if i >= 2:
                    pool.wait_ge(att_s, i - 1)
                for q in range(2):
                    ps = slice(DH * q, DH * q + DH)
                    pool.tensor_copy(qz[i % 2][ps, q, :], qT[ps, h, t * P:(t + 1) * P]).then_inc(q_pad, 1)
            for b in (1, 2):
                wait_job_copied(pool, J_MOD[b][-1])
                for j in range(4):
                    q, half = divmod(4 * b + j, 2)
                    pool.dma_start(mods[:, q, half * BANK:(half + 1) * BANK],
                                   modrow[32 * j:32 * j + 2, b - 1, :]).then_inc(mod_stored, 16)
            pool.wait_ge(mod_stored, 16 * 8)
            pool.wait_ge(kv_stored, 32)
            pool.wait_ge(tb_done, F_OD[0] + F_OD[1])
            for g in range(2):
                pool.dma_start(g1b[:, g, :], mods[g, 2:3].to_broadcast((P, D))).then_inc(bc_loaded, 16)
                pool.dma_start(sh2b[:, g, :], mods[g, 3:4].to_broadcast((P, D))).then_inc(bc_loaded, 16)
                pool.dma_start(sc2b[:, g, :], mods[g, 4:5].to_broadcast((P, D))).then_inc(bc_loaded, 16)
            pool.dma_start(l1g, ln1_g.to_broadcast((P, D))).then_inc(bc_loaded, 16)
            pool.dma_start(l1b, ln1_b.to_broadcast((P, D))).then_inc(bc_loaded, 16)
            pool.dma_start(wr, w_router[0].rearrange("(k p) e -> p k e", p=P)).then_inc(bc_loaded, 16)
            pool.dma_start(iota_r, k_r[1:2].to_broadcast((P, NT))).then_inc(bc_loaded, 16)
            wait_job_copied(pool, J_WO[-1])
            for p0, g in ((0, 1), (CAP_L, 0), (SLOT, 1), (SLOT + CAP_L, 0)):
                pool.dma_start(g2s[p0:p0 + 32], mods[g, 5:6].to_broadcast((32, D))).then_inc(ld_g2, 16)
            pool.wait_ge(rt_slots, 1)
            pool.dma_start(slot_tokens, slots[:, 0:SLOT]).then_inc(rt_stored, 16)
            pool.wait_ge(rt_stored, 16)
            pool.dma_start(slot_bc, slot_tokens.rearrange("e s -> (e s)")[None].to_broadcast((P, NE * SLOT))).then_inc(rt_bc, 16)
            pool.wait_ge(rt_tt, 1)
            pool.dma_start(l2g, ln2_g.to_broadcast((P, D))).then_inc(ld_end, 16)
            pool.dma_start(l2b, ln2_b.to_broadcast((P, D))).then_inc(ld_end, 16)

        @block.tensor
        def _(pe):
            turned = [0]

            def batch(srcs):
                b = turned[0]
                if b >= 2:
                    pe.wait_ge(tb_out[b % 2], (b - 2) // 2 + 1)
                for i, src in enumerate(srcs):
                    x = pe.transpose(banks[:, 2 + b % 2, i * P:(i + 1) * P], src, ident)
                x.then_inc(tb_done, 1)
                turned[0] += 1

            def job(j, k0=0, k1=KT):
                kind, chunk, i, _, _ = JOBS[j]
                if j >= 2 and k0 == 0:
                    wait_job_copied(pe, j - 2)
                out = banks[:, j % 2, :]

                def weights(n):
                    pe.wait_ge(wsem[n % WSLOTS], 16 * (n // WSLOTS + 1))
                    return w_slot(n)

                if kind == "mod":
                    pairs = range(4) if j == J_MOD0 else (JOBS[j].half,)
                    for n, ks in enumerate(pairs):
                        w = weights(chunk + n)
                        for kk in range(2):
                            for q in range(4):
                                x = pe.matmul(out[32 * q:32 * q + 32, :], cT[:, 2 * ks + kk, :],
                                              w[:, kk, q * BANK:(q + 1) * BANK], start=(n == 0 and kk == 0),
                                              stop=(n == len(pairs) - 1 and kk == 1))
                elif kind in ("qa", "ka"):
                    w = weights(chunk)
                    for k in range(KT):
                        x = pe.matmul(out[:, 0:NT], w[:, k, i * P:(i + 1) * P], hT[:, k, :],
                                      start=(k == 0), stop=(k == KT - 1))
                elif kind == "ab":
                    pe.wait_ge(ld_ab, 48)
                    for k in range(KT):
                        pe.wait_ge(ht_out[k % 2], k // 2 + 1)
                        x = pe.matmul(out[0:32, 0:NT], wab[:, k, :], hT[:, k, :], start=(k == 0), stop=(k == KT - 1))
                elif kind == "al":
                    if i == 0:
                        wait_job_copied(pe, J_AB)
                    x = pe.matmul(out[:, 0:NT], wal[:, i * P:(i + 1) * P], abT, start=True, stop=True)
                else:
                    w = weights(chunk)
                    src = {"pa": oaT, "pb": odT, "wo": mT}.get(kind, hT)
                    for k in range(k0, k1):
                        x = pe.matmul(out, src[:, k, i * P:(i + 1) * P], w[:, k, :], start=(k == 0), stop=(k == KT - 1))
                if k1 == KT:
                    x.then_inc(job_done, 1)

            pe.wait_ge(ld_k, 16)
            pe.wait_ge(c_silu, 1)
            pe.transpose(banks[:, 4, 0:16], crow_s, ident[0:16, 0:16]).then_inc(c_turned, 1)
            pe.wait_ge(xn_ready, T)
            for k in range(KT):
                batch([xn[:, t, k * P:(k + 1) * P] for t in range(T)])
            pe.wait_ge(c_ready, 1)
            job(J_MOD0)
            wait_job_copied(pe, J_MOD0)
            for i in range(4):
                x = pe.transpose(banks[:, 5, i * P:(i + 1) * P], modrow0[:, i * P:(i + 1) * P], ident)
            x.then_inc(mod_turned, 1)
            for j in range(J_AB, J_VA[-1] + 1):
                job(j)

            def gla_turn(i):
                h, q = GLA_ITEMS[i]
                if i:
                    pe.wait_ge(gla_kcp, i)
                    pe.wait_ge(gla_msk, 3 * i)
                for a, t in enumerate(GLA_TILES[q]):
                    for w in range(2):
                        pe.transpose(banks[:, 2, (2 * a + w) * P:(2 * a + w + 1) * P],
                                     heads(KD)[:, w, h, t * P:(t + 1) * P], ident)
                for a, t in enumerate(GLA_TILES[q]):
                    for w in range(2):
                        x = pe.matmul(banks[:, 3, (2 * a + w) * P:(2 * a + w + 1) * P],
                                      heads(KE)[:, w, h, t * P:(t + 1) * P], heads(QE)[:, w, h, t * P:(t + 1) * P],
                                      start=True, stop=True)
                x.then_inc(gla_kt, 1)

            def gla_update(i):
                h, q = GLA_ITEMS[i]
                pe.wait_ge(gla_kcp, i + 1)
                if i == 0:
                    for j in J_VA[-2:]:
                        wait_job_copied(pe, j)
                if i:
                    pe.wait_ge(gla_s, 10 * (i // 2) + (4 if i % 2 else 0))
                for u, (w, ch) in enumerate(GLA_UPD[q]):
                    t, r = divmod(ch, 2)
                    a = t - GLA_TILES[q][0]
                    x = pe.matmul(banks[:, 4 + u // 2, (u % 2) * DV:(u % 2 + 1) * DV],
                                  kdn[i % 2][:, a, w, r, :], va[:, t, h * DV:(h + 1) * DV], start=True, stop=True)
                x.then_inc(gla_u, 1)

            def gla_state(i, w, ch):
                h, q = GLA_ITEMS[i]
                if q == 0:
                    return SV[i % 2][:, 2 * w, :] if ch == 1 - w else None
                step = ch - 2 if w == 0 else 5 - ch
                return S0[:, w, h, :] if step == 0 else SV[i % 2][:, 3 * w + step - 1, :]

            def gla_out(i):
                h, q = GLA_ITEMS[i]
                pe.wait_ge(gla_msk, 3 * (i + 1))
                pe.wait_ge(gla_s, 10 * (i // 2) + (10 if i % 2 else 4))
                if i == 0:
                    pe.wait_ge(ld_s0, 32)
                if i:
                    pe.wait_ge(gla_ocp, i)
                for a, t in enumerate(GLA_TILES[q]):
                    out = banks[:, 7, a * DV:(a + 1) * DV]
                    terms = [(r, w, gla_state(i, w, 2 * t + r)) for r in range(2) for w in range(2)]
                    terms = [x for x in terms if x[2] is not None]
                    pe.matmul(out, AS[i % 2][:, a, :], va[:, t, h * DV:(h + 1) * DV], start=True, stop=False,
                              skip_group_check=True)
                    for r, w, st in terms:
                        c0 = t * P + r * 64
                        x = pe.matmul(out[64 * r:64 * r + 64, :], heads(QE)[:, w, h, c0:c0 + 64], st,
                                      start=False, stop=True, skip_group_check=True)
                x.then_inc(gla_o, 1)

            pe.wait_ge(gla_in, 3)
            more = list(J_QD + J_KD)
            for i in range(len(GLA_ITEMS)):
                gla_turn(i)
                job(more.pop(0))
                gla_update(i)
                if i % 2:
                    job(more.pop(0))
                gla_out(i)
            for j in J_VD[:4]:
                job(j)
            pe.wait_ge(gla_kcp, len(GLA_ITEMS))
            pe.wait_ge(gla_msk, 3 * len(GLA_ITEMS))
            pe.wait_ge(gla_ocp, len(GLA_ITEMS))
            pe.wait_ge(rope_done["q"], 4)
            for h in range(AH):
                batch([qd[:, t, h * P:(h + 1) * P] for t in range(T)])
                job(J_VD[4], h, h + 1)
            pe.wait_ge(rope_done["k"], 4)
            pe.wait_ge(ld_cache, 32)
            for h in range(AH):
                batch([kd[:, t, h * P:(h + 1) * P] for t in range(T)] + [kc[:, h * P:(h + 1) * P]])
                job(J_VD[5], h, h + 1)
            wait_family(pe, F_KT)

            def keys(t):
                return (0, SEQ) if t == 0 else (SEQ, NKEY)

            def att_scores(i):
                t, h = ATT_ITEMS[i]
                a, b = keys(t)
                if i >= 2:
                    pe.wait_ge(att_e, 2 * (i - 1))
                pe.wait_ge(q_pad, 2 * (i + 1))
                for q in range(2):
                    x = pe.matmul(banks[:, 2 + 2 * (i % 2) + q, 0:b - a], qz[i % 2][:, q, :], kT[:, h, a:b],
                                  start=True, stop=True)
                x.then_inc(att_s, 1)

            def att_turn(i):
                t, h = ATT_ITEMS[i]
                pe.wait_ge(att_pd, i + 1)
                if i:
                    pe.wait_ge(att_tcp, i)
                for n in range(1 if t == 0 else 3):
                    x = pe.transpose(banks[:, 6, n * P:(n + 1) * P], pp[i % 2][2][:, n * P:(n + 1) * P], ident)
                x.then_inc(att_t, 1)

            def att_out(i):
                t, h = ATT_ITEMS[i]
                pe.wait_ge(att_tcp, i + 1)
                if i:
                    pe.wait_ge(att_ocp, i)
                vs = [vd[:, 0, :]] if t == 0 else [vd[:, 1, :], vd[:, 2, :], vc]
                for n, v in enumerate(vs):
                    x = pe.matmul(banks[:, 7, 0:P], pp[i % 2][3][:, n * P:(n + 1) * P], v[:, h * P:(h + 1) * P],
                                  start=(n == 0), stop=(n == len(vs) - 1))
                x.then_inc(att_o, 1)

            for j in J_VD[-2:]:
                wait_job_copied(pe, j)
            n = len(ATT_ITEMS)
            for i in range(n + 2):
                if i < n:
                    att_scores(i)
                if i < n:
                    job(ATT_JOBS[i // 2][0], KT // 2 * (i % 2), KT // 2 * (i % 2 + 1))
                    if i % 2:
                        for j in ATT_JOBS[i // 2][1:]:
                            job(j)
                if 1 <= i <= n:
                    att_turn(i - 1)
                if i >= 2:
                    att_out(i - 2)
            for j in J_GB[:2]:
                job(j)
            pe.wait_ge(oa_g, T)
            for k in range(KT):
                batch([o_a[:, t, k * P:(k + 1) * P] for t in range(T)])
                job(J_GB[2], k, k + 1)
            pe.wait_ge(od_g, T)
            for k in range(KT):
                batch([o_d[:, t, k * P:(k + 1) * P] for t in range(T)])
                job(J_GB[3], k, k + 1)
            for j in J_GB[4:]:
                job(j)
            wait_family(pe, F_OD)
            for j in J_PA:
                job(j)

            def turn_tile(src, t):
                for b in range(2):
                    batch([src[:, t, k * P:(k + 1) * P] for k in range(4 * b, 4 * b + 4)])

            for n, j in enumerate(J_PB):
                job(j)
                if n % 2 == 0 and n:
                    wait_job_copied(pe, J_PB[n - 1])
                    turn_tile(merged, n // 2 - 1)

            def logits(t):
                wait_tile(pe, F_H2, t)
                for k in range(KT):
                    x = pe.matmul(banks[:, 4 + t, 0:NE], h2T[:, k, t * P:(t + 1) * P], wr[:, k, :],
                                  start=(k == 0), stop=(k == KT - 1))
                x.then_inc(rt_log, 1)

            def turn_probs(t):
                pe.wait_ge(rt_aff, t + 1)
                pe.transpose(banks[0:NE, 4 + t, 0:P], aff[:, t, :], ident).then_inc(rt_tr, 1)

            wait_tile(pe, F_M, 0)
            job(J_WO[0])
            wait_job_copied(pe, J_PB[-1])
            turn_tile(merged, 2)
            job(J_WO[1])
            wait_tile(pe, F_M, 1)
            job(J_WO[2])
            job(J_WO[3])
            pe.wait_ge(h2_ready, 1)
            turn_tile(h2, 0)
            wait_tile(pe, F_M, 2)
            job(J_WO[4])
            logits(0)
            job(J_WO[5])
            pe.wait_ge(h2_ready, 2)
            turn_tile(h2, 1)
            turn_probs(0)
            logits(1)
            pe.wait_ge(h2_ready, 3)
            turn_tile(h2, 2)
            logits(2)
            turn_probs(1)
            turn_probs(2)
            pe.wait_ge(rt_slots, 2)
            pe.transpose(banks[:, 7, 0:NE], slots, ident[0:NE, 0:NE])
            pe.transpose(banks[:, 7, NE:2 * NE], gates, ident[0:NE, 0:NE]).then_inc(rt_tt, 1)

            pe.wait_ge(rt_cols, 2)
            with pe.Fori(0, NE) as e:
                pe.wait_ge(sel_ready, e * T + T)
                pe.wait_ge(acc_done, e * 6 + 6)
                for t in range(T):
                    for w in range(2):
                        x = pe.matmul(banks[64 * w:64 * w + 64, 3, :], sel[:, t, :], h2[:, t, w * BANK:(w + 1) * BANK],
                                      start=(t == 0), stop=(t == T - 1))
                x.then_inc(xe_done, 1)
                pe.wait_ge(xe_cp, e + 1)
                for i in range(4):
                    x = pe.transpose(banks[:, 4, i * P:(i + 1) * P], xe[:, i * P:(i + 1) * P], ident)
                x.then_inc(xet_done, 1)
                pe.wait_ge(xet_cp, e + 1)
                for m, (land, used) in enumerate(((land_g, gate_used), (land_u, up_used))):
                    for q in range(4):
                        pe.wait_ge(land[q], e * 16 + 16)
                        w4 = reg(((4 * m + q) % 6) * QUARTER, QUARTER).rearrange("p (k i w n) -> p k i w n", k=2, w=2, n=P)
                        for kk in range(2):
                            k = 2 * q + kk
                            for b, (i0, i1) in enumerate(FCH):
                                for w in range(2):
                                    x = pe.matmul(banks[64 * w:64 * w + 64, 3 * m + b, 0:(i1 - i0) * P],
                                                  xeT[:, k % 4, 64 * (k // 4):64 * (k // 4) + 64],
                                                  w4[:, kk, i0:i1, w, :], start=(k == 0), stop=(k == KT - 1))
                        x.then_inc(used, 1)
                for b, (i0, i1) in enumerate(FCH):
                    pe.wait_ge(hid_done, e * 3 + b + 1)
                    for i in range(i0, i1):
                        x = pe.transpose(banks[:, b, (i - i0) * P:(i - i0 + 1) * P], hid[:, i * P:(i + 1) * P], ident)
                    x.then_inc(hidt_done, 1)
                pe.wait_ge(hidt_cp, e * 3 + 3)
                wd = reg(DOWN0, FF // P * D).rearrange("p (i w d) -> p i w d", w=2, d=D)
                for g, (i0, i1) in enumerate(DOWN_GROUPS):
                    pe.wait_ge(land_d[g], e * 16 + 16)
                    for i in range(i0, i1):
                        for dc in range(2):
                            for w in range(2):
                                x = pe.matmul(banks[64 * w:64 * w + 64, 6 + dc, :], hidT[:, i, 64 * w:64 * w + 64],
                                              wd[:, i, w, dc * BANK:(dc + 1) * BANK], start=(i == 0), stop=(i == FT - 1))
                    x.then_inc(down_used, 1)
                pe.wait_ge(selT_ready, e + 1)
                pe.wait_ge(y_cp, e * 2 + 2)
                for t in range(T):
                    for dc in range(2):
                        pe.matmul(banks[:, 2 * t + dc, :], selT[:, t * P:(t + 1) * P], yrow[:, dc * BANK:(dc + 1) * BANK],
                                  start=True, stop=True).then_inc(comb_done, 1)

        def wait_turned(eng, b):
            eng.wait_ge(tb_done, b + 1)

        def family_copies(eng, f, copy, parity):
            for k in range(parity, KT, 2):
                wait_turned(eng, f[0] + k)
                copy(k, banks[:, 2 + k % 2, :]).then_inc(tb_out[parity], 1)

        def tile_copy(eng, f, t, dst, copy, parity):
            wait_turned(eng, f[0] + 2 * t + parity)
            copy(dst[:, 4 * parity:4 * parity + 4, t * P:(t + 1) * P],
                 banks[:, 2 + parity, :].rearrange("p (k n) -> p k n", n=P)).then_inc(tb_out[parity], 1)

        @block.scalar
        def _(act):
            steps = [0]

            def link(x):
                steps[0] += 1
                x.then_inc(a_chain, 1)
                act.wait_ge(a_chain, steps[0])

            def cp(out, in_, scale=1.0):
                return act.activation(out, in_, ACT.Copy, scale=scale)

            def job_copy(j):
                kind, chunk, i, half, who = JOBS[j]
                assert who == "a"
                act.wait_ge(job_done, j + 1)
                b = banks[:, j % 2, :]
                if kind == "qa":
                    x = cp(qkT[:, 0, i, :], b[:, 0:NT], DK ** -0.5)
                else:
                    dst = {"va": va, "qd": qd, "kd": kd, "vd": vd, "ra": ra, "ga": ga, "gb": gb}[kind]
                    if j == J_GA[0]:
                        act.wait_ge(kv_stored, 32)
                    x = act.activation(dst[:, i, half * BANK:(half + 1) * BANK], b,
                                       ACT.Sigmoid if kind == "gb" else ACT.Copy)
                x.then_inc(job_out["a"], 1)

            act.wait_ge(ld_c, 32)
            act.activation(crow_s, crow, ACT.Silu).then_inc(c_silu, 1)
            act.wait_ge(ln_var, T)
            act.activation(s("std"), s("mv").rearrange("p (t w) -> p t w", w=2)[:, :, 1], ACT.Sqrt,
                           bias=s("eps")).then_inc(ln_std, 1)

            family_copies(act, F_HT, lambda k, b: cp(hT[:, k, :], b[:, 0:NT]), 0)
            act.wait_ge(tb_out[0], F_HT[1] // 2)
            act.wait_ge(mod_ready, 2)
            sc, sh = (s(x).rearrange("p (k g) -> p k g", g=2) for x in ("sc1", "sh1"))
            for k in range(0, KT, 2):
                for g, ns in enumerate((slice(0, P), slice(P, NT))):
                    x = act.activation(hT[:, k, ns], hT[:, k, ns], ACT.Identity, scale=sc[:, k, g:g + 1], bias=sh[:, k, g:g + 1])
                x.then_inc(ht_out[0], 1)
            for j in J_QA:
                job_copy(j)
            wait_job_copied(act, J_AL[-1])
            link(act.activation(QE, B, ACT.Abs))
            link(act.activation(QE, QE, ACT.Exp, scale=-1.0))
            act.activation(QE, QE, ACT.Ln, bias=s("one")).then_inc(lg_soft, 1)
            for j in J_VA:
                job_copy(j)
            act.wait_ge(lg_sum, 2)
            act.activation(KD, KD, ACT.Exp).then_inc(lg_exp, 1)
            act.activation(QE, B, ACT.Exp).then_inc(lg_exp, 1)
            act.activation(KE, B, ACT.Exp, scale=-1.0).then_inc(lg_exp, 1)
            ebv = eb.rearrange("p w (h c) -> p w h c", h=GH)
            act.activation(eb[:, 0, :], LGc[:, 0, :, CHUNK - 1], ACT.Exp)
            act.activation(eb[:, 1, :], LGc[:, 1, :, 0], ACT.Exp).then_inc(lg_exp, 1)
            act.wait_ge(dot_done, 2)
            act.activation(s("edots"), s("dots"), ACT.Exp).then_inc(dot_exp, 1)

            more = list(J_QD + J_KD)
            act.wait_ge(gla_in, 3)
            for i, (h, q) in enumerate(GLA_ITEMS):
                nt = len(GLA_TILES[q])
                act.wait_ge(gla_kt, i + 1)
                if i == 0:
                    act.wait_ge(gla_kz, 1)
                for r in range(2):
                    rs = slice(CHUNK * r, CHUNK * r + CHUNK)
                    x = cp(kdn[i % 2][rs, 0:nt, :, r], banks[rs, 2, 0:nt * 2 * P].rearrange("p (a w n) -> p a w n", w=2, n=P))
                x.then_inc(gla_kcp, 1)
                job_copy(more.pop(0))
                if i % 2:
                    job_copy(more.pop(0))
                act.wait_ge(gla_o, i + 1)
                t0 = GLA_TILES[q][0]
                link(cp(o_a[:, t0:t0 + nt, h * DV:(h + 1) * DV], banks[:, 7, 0:nt * DV].rearrange("p (a v) -> p a v", v=DV)))
                for a in range(nt):
                    b = banks[:, 7, a * DV:(a + 1) * DV]
                    n = GH * (t0 + a) + h
                    x = act.activation(b, b, ACT.Square, accum_out=s("msa", n, n + 1))
                x.then_inc(gla_ocp, 1)
            act.wait_ge(gla_ocp, len(GLA_ITEMS))
            act.activation(s("msa"), s("msa"), ACT.Sqrt, scale=1.0 / DV, bias=s("eps")).then_inc(oa_sq, 1)
            for j in (J_VD[0], J_VD[2]):
                job_copy(j)
            family_copies(act, F_QT, lambda h, b: cp(qT[:, h, :], b[:, 0:NT]), 0)
            job_copy(J_VD[4])
            family_copies(act, F_KT, lambda h, b: cp(kT[:, h, :], b), 0)

            def exps(i):
                t, h = ATT_ITEMS[i]
                nk = SEQ if t == 0 else NKEY - SEQ
                act.wait_ge(att_nb, i + 1)
                if i >= 2:
                    act.wait_ge(att_pd, i - 1)
                for q in range(2):
                    m = 2 * (i % 2) + q
                    act.activation(pp[i % 2][q][:, 0:nk], banks[:, 2 + m, 0:nk], ACT.Exp, scale=DH ** -0.5,
                                   bias=s("nb", m, m + 1), accum_out=s("sum", m, m + 1)).then_inc(att_e, 1)

            n = len(ATT_ITEMS)
            for i in range(n + 2):
                if i < n:
                    exps(i)
                if 1 <= i <= n:
                    nk = 1 if ATT_ITEMS[i - 1][0] == 0 else 3
                    act.wait_ge(att_t, i)
                    cp(pp[(i - 1) % 2][3][:, 0:nk * P], banks[:, 6, 0:nk * P]).then_inc(att_tcp, 1)
                if i >= 2:
                    t, h = ATT_ITEMS[i - 2]
                    act.wait_ge(att_o, i - 1)
                    b = banks[:, 7, 0:P]
                    link(cp(o_d[:, t, h * P:(h + 1) * P], b))
                    act.activation(b, b, ACT.Square, accum_out=s("eb", i - 2, i - 1)).then_inc(att_ocp, 1)
                if i < n and i % 2 and JOBS[ATT_JOBS[i // 2][0]].engine == "a":
                    job_copy(ATT_JOBS[i // 2][0])
            act.wait_ge(att_ocp, n)
            act.activation(s("eb", 24, 48), s("eb", 0, 24), ACT.Sqrt, scale=1.0 / (2 * DH), bias=s("eps")).then_inc(od_sq, 1)
            for j in (J_RA[-1], J_RA[-2]):
                wait_job_copied(act, j)
            act.activation(E, E, ACT.Silu).then_inc(gates_on, 1)
            for j in J_GB[:2]:
                job_copy(j)
            for j in (J_GA[-1], J_GA[-2]):
                wait_job_copied(act, j)
            act.activation(O4[:], O4[:], ACT.Sigmoid).then_inc(gates_on, 1)
            family_copies(act, F_OA, lambda k, b: act.activation(oaT[:, k, :], b[:, 0:NT], ACT.Copy, scale=s("gla_g", k % 2, k % 2 + 1)), 0)
            job_copy(J_GB[2])
            family_copies(act, F_OD, lambda k, b: act.activation(odT[:, k, :], b[:, 0:NT], ACT.Copy, scale=s("sub_g")), 0)
            for j in J_GB[3:]:
                job_copy(j)
            for t in range(T):
                tile_copy(act, F_M, t, mT, cp, 0)

            def router_exps(t):
                act.wait_ge(rt_max, t + 1)
                act.activation(aff[:, t, :], banks[:, 4 + t, 0:NE], ACT.Exp, bias=rst[:, 3 + t:4 + t],
                               accum_out=rst[:, 6 + t:7 + t]).then_inc(rt_exp, 1)

            def times_alpha(t):
                act.wait_ge(h2_ready, t + 1)
                act.activation(x_r[:, t, :], x_r[:, t, :], ACT.Copy, scale=ALPHA).then_inc(acc_done, 2)

            def x1_dev(t, m):
                act.wait_ge(x1_var[m], t + 1)
                act.activation(s("std", t, t + 1), s("mv", 2 * t + 1, 2 * t + 2), ACT.Sqrt, bias=s("eps")).then_inc(x1_std[m], 1)

            for t in range(T):
                x1_dev(t, 0)
                x1_dev(t, 1)
                if t == 1:
                    times_alpha(0)
                    router_exps(0)
                if t < 2:
                    tile_copy(act, F_H2, t, h2T, cp, 0)
            times_alpha(1)
            router_exps(1)
            tile_copy(act, F_H2, 2, h2T, cp, 0)
            router_exps(2)
            times_alpha(2)

            with act.Fori(0, NE) as e:
                act.wait_ge(xe_done, e + 1)
                act.activation(xe, banks[:, 3, :], ACT.Copy).then_inc(xe_cp, 1)
                act.wait_ge(gate_used, e * 4 + 4)
                for b, (i0, i1) in enumerate(FCH):
                    act.activation(hid[:, i0 * P:i1 * P], banks[:, b, 0:(i1 - i0) * P], ACT.Silu).then_inc(silu_done, 1)
                for b, (i0, i1) in enumerate(FCH):
                    act.wait_ge(hidt_done, e * 3 + b + 1)
                    act.activation(hidT[:, i0:i1, :], banks[:, b, 0:(i1 - i0) * P].rearrange("p (i n) -> p i n", n=P),
                                   ACT.Copy).then_inc(hidt_cp, 1)
            for t in range(T):
                act.wait_ge(f_var, t + 1)
                act.activation(s("std", t, t + 1), s("mv", 2 * t + 1, 2 * t + 2), ACT.Sqrt, bias=s("eps")).then_inc(f_std, 1)

        @block.vector
        def _(dve):
            steps = [0]

            def note(x):
                steps[0] += 1
                return x.then_inc(v_chain, 1)

            def settle():
                dve.wait_ge(v_chain, steps[0])

            def link(x):
                note(x)
                settle()

            def stats(t):
                bn = s("bn").rearrange("p (t w n) -> p t w n", t=T, n=6)
                for w in range(2):
                    note(dve.bn_stats(bn[:, t, w, :], x_r[:, t, w * BANK:(w + 1) * BANK]))
                settle()
                return dve.bn_aggr(s("mv", 2 * t, 2 * t + 2), bn[:, t].rearrange("p w n -> p (w n)"))

            def affine(dst, t, g, b):
                link(dve.reciprocal(s("rstd", t, t + 1), s("std", t, t + 1)))
                link(dve.scalar_tensor_tensor(out=dst[:, t, :], in0=x_r[:, t, :], scalar=s("mv", 2 * t, 2 * t + 1), in1=g,
                                              op0=ALU.subtract, op1=ALU.mult))
                return dve.scalar_tensor_tensor(out=dst[:, t, :], in0=dst[:, t, :], scalar=s("rstd", t, t + 1), in1=b,
                                                op0=ALU.mult, op1=ALU.add)

            def job_copy(j):
                kind, chunk, i, half, who = JOBS[j]
                assert who == "v"
                dve.wait_ge(job_done, j + 1)
                b = banks[:, j % 2, :]
                cs = slice(half * BANK, (half + 1) * BANK)
                g = min(i, 1)
                if j == J_MOD0:
                    dve.wait_ge(ld_bm, 64)
                    x = dve.tensor_tensor(modrow0, b, bmod0, ALU.add)
                elif kind == "mod":
                    if half == 0:
                        dve.wait_ge(ld_bm, 128)
                    else:
                        dve.wait_ge(job_out["v"], copied_before(J_MOD[i][half - 1], "v") + 1)
                    x = dve.tensor_tensor(modrow[:, i - 1, :], b, modrow[:, i - 1, :] if half else bmod[:, i - 1, :], ALU.add)
                elif kind == "ka":
                    x = dve.tensor_copy(qkT[:, 1, i, :], b[:, 0:NT])
                elif kind == "ab":
                    x = dve.tensor_copy(abT, b[0:32, 0:NT])
                elif kind == "al":
                    if i == 0:
                        dve.wait_ge(ld_small, 160)
                    x = dve.tensor_scalar(LG4[:, i // GH, i % GH, :], b[:, 0:NT], s("balpha", i, i + 1), None, ALU.add)
                elif kind == "pa":
                    x = dve.tensor_tensor(merged[:, i, cs], b, ga[:, i, cs], ALU.mult)
                elif kind == "pb":
                    link(dve.tensor_tensor(pbtmp, b, gb[:, i, cs], ALU.mult))
                    x = dve.tensor_tensor(merged[:, i, cs], merged[:, i, cs], pbtmp, ALU.add)
                elif kind == "wo":
                    link(dve.tensor_tensor(wotmp, b, g1b[:, g, cs], ALU.mult))
                    x = dve.scalar_tensor_tensor(out=x_r[:, i, cs], in0=x_r[:, i, cs], scalar=ALPHA, in1=wotmp,
                                                 op0=ALU.mult, op1=ALU.add)
                else:
                    if kind == "ga":
                        dve.wait_ge(kv_stored, 32)
                    dst = {"vd": vd, "ra": ra, "ga": ga}[kind]
                    x = dve.tensor_copy(dst[:, i, cs], b)
                x.then_inc(job_out["v"], 1)
                if kind in ("pb", "wo"):
                    dve.wait_ge(job_out["v"], copied_before(j, "v") + 1)

            note(dve.memset(s("eps"), EPS))
            note(dve.memset(s("one"), 1.0))
            dve.wait_ge(zeroed, 1)
            dve.wait_ge(c_turned, 1)
            dve.tensor_copy(cT[:, :, 0:2], banks[:, 4, 0:16].rearrange("p (g k) -> p k g", g=2)).then_inc(c_ready, 1)
            for t in range(T):
                dve.wait_ge(ld_x[min(t, 1)], 16)
                stats(t).then_inc(ln_var, 1)
            dve.wait_ge(ln_std, 1)
            link(dve.reciprocal(s("rstd"), s("std")))
            for t in range(T):
                dve.tensor_scalar(xn[:, t, :], x_r[:, t, :], s("mv", 2 * t, 2 * t + 1), s("rstd", t, t + 1),
                                  ALU.subtract, ALU.mult).then_inc(xn_ready, 1)
            family_copies(dve, F_HT, lambda k, b: dve.tensor_copy(hT[:, k, :], b[:, 0:NT]), 1)
            job_copy(J_MOD0)
            dve.wait_ge(mod_turned, 1)
            mt = banks[:, 5, :].rearrange("p (i j g) -> p i j g", i=4, j=4)
            dve.tensor_copy(s("sh1").rearrange("p (j i g) -> p i j g", j=2, g=2), mt[:, :, 0:2, 0:2]).then_inc(mod_ready, 1)
            dve.tensor_scalar(s("sc1").rearrange("p (j i g) -> p i j g", j=2, g=2), mt[:, :, 2:4, 0:2], 1.0, None,
                              ALU.add).then_inc(mod_ready, 1)
            dve.wait_ge(tb_out[1], F_HT[1] // 2)
            dve.wait_ge(mod_ready, 2)
            sc, sh = (s(x).rearrange("p (k g) -> p k g", g=2) for x in ("sc1", "sh1"))
            for k in range(1, KT, 2):
                for g, ns in enumerate((slice(0, P), slice(P, NT))):
                    x = dve.tensor_scalar(hT[:, k, ns], hT[:, k, ns], sc[:, k, g:g + 1], sh[:, k, g:g + 1], ALU.mult, ALU.add)
                x.then_inc(ht_out[1], 1)
            for j in [J_AB] + J_AL:
                job_copy(j)
            dve.wait_ge(job_out["v"], copied_before(J_AL[-1], "v") + 1)
            for w in range(2):
                note(dve.tensor_tensor(lprod[:, w * DH:(w + 1) * DH], lamv[:, 2 * w * DH:(2 * w + 1) * DH],
                                       lamv[:, (2 * w + 1) * DH:(2 * w + 2) * DH], ALU.mult))
            settle()
            for w in range(2):
                dve.tensor_reduce(s("dots", w, w + 1), lprod[:, w * DH:(w + 1) * DH], AX.X, ALU.add).then_inc(dot_done, 1)
            dve.wait_ge(lg_soft, 1)
            link(dve.scalar_tensor_tensor(out=B, in0=B, scalar=0.0, in1=QE, op0=ALU.min, op1=ALU.subtract))
            link(dve.tensor_scalar(B, B, 1.0 / GLA_TAU, None, ALU.mult))
            for h in range(GH):
                note(dve.tensor_tensor_scan(heads(QE)[:, 1, h, :], resetm, LG4[:, 1, h, :], 0.0, ALU.mult, ALU.add))
                note(dve.tensor_tensor_scan(heads(QE)[:, 0, h, :], resetm, LG4[:, 0, h, :], 0.0, ALU.mult, ALU.add))
            settle()
            QEc = QE.rearrange("p (w c j) -> p w c j", w=2, j=CHUNK)
            KDc = KD.rearrange("p (w c j) -> p w c j", w=2, j=CHUNK)
            full = (P, GH * NCH, CHUNK)
            note(dve.tensor_copy(LG[:, 0, :], QE[:, 0:GH * NT]))
            link(dve.tensor_tensor(LG[:, 1, :], LG[:, 1, :], QE[:, GH * NT:], ALU.subtract))
            link(dve.tensor_tensor(LGc[:, 1], LGc[:, 1], QEc[:, 1, :, CHUNK - 1:CHUNK].to_broadcast(full), ALU.add))
            dve.tensor_tensor(KDc[:, 0], LGc[:, 0, :, CHUNK - 1:CHUNK].to_broadcast(full), LGc[:, 0], ALU.subtract).then_inc(lg_sum, 1)
            dve.tensor_tensor(KDc[:, 1], LGc[:, 1, :, 0:1].to_broadcast(full), LGc[:, 1], ALU.subtract).then_inc(lg_sum, 1)
            for j in J_KA:
                job_copy(j)
            wait_job_copied(dve, J_KA[-1])
            wait_job_copied(dve, J_QA[-1])
            both = (P, 2, GH * NT)
            for n, (dst, w) in enumerate(((KD, 1), (QE, 0), (KE, 1))):
                dve.wait_ge(lg_exp, n + 1)
                v = dst.rearrange("p (w m) -> p w m", w=2)
                src = A[:, w * GH * NT:(w + 1) * GH * NT]
                dve.tensor_tensor(v, v, src[:, None].to_broadcast(both), ALU.mult).then_inc(gla_in, 1)
            dve.wait_ge(lg_exp, 4)
            dve.wait_ge(gla_in, 3)
            dve.wait_ge(dot_exp, 1)
            link(dve.tensor_tensor(s("nlam"), s("edots", 1, 2), s("edots", 0, 1), ALU.subtract))
            note(dve.tensor_scalar(s("nlam"), s("nlam"), LAM_INIT, None, ALU.subtract))
            note(dve.tensor_scalar(s("sub_g"), s("sub_g"), 1.0 - LAM_INIT, None, ALU.mult))
            dve.memset(A[:, 0:2048], 0.0).then_inc(gla_kz, 1)
            note(dve.memset(AF, 0.0))
            note(dve.memset(AB, 0.0))
            settle()
            for i, (h, q) in enumerate(GLA_ITEMS):
                nt = len(GLA_TILES[q])
                dve.wait_ge(gla_kt, i + 1)
                sc = banks[:, 3, 0:nt * 2 * P].rearrange("p (a w n) -> p a w n", w=2, n=P)
                for w, dst in enumerate((AF, AB)):
                    for a in range(nt):
                        x = dve.copy_predicated(dst[:, a, :], km[:, w * P:(w + 1) * P], sc[:, a, w, :])
                    x.then_inc(gla_msk, 1)
                dve.wait_ge(gla_msk, 3 * i + 2)
                dve.tensor_tensor(AS[i % 2][:, 0:nt], AF[:, 0:nt], AB[:, 0:nt], ALU.add).then_inc(gla_msk, 1)
                dve.wait_ge(gla_u, i + 1)
                if q == 0 and i >= 2:
                    dve.wait_ge(gla_st, 16 * i)
                if q == 1 and i == 1:
                    dve.wait_ge(ld_s0, 32)
                base = 10 * (i // 2) + (4 if q else 0)
                for u, (w, ch) in enumerate(GLA_UPD[q]):
                    up = banks[:, 4 + u // 2, (u % 2) * DV:(u % 2 + 1) * DV]
                    dst = SV[i % 2][:, u, :]
                    first = u % len([x for x in GLA_UPD[q] if x[0] == w]) == 0
                    if q == 0 and first:
                        dve.tensor_copy(dst, up).then_inc(gla_s, 1)
                        continue
                    prev = S0[:, w, h, :] if first else SV[i % 2][:, u - 1, :]
                    if not first:
                        dve.wait_ge(gla_s, base + u)
                    c0 = h * NCH + ch
                    dve.scalar_tensor_tensor(out=dst, in0=prev, scalar=eb[:, w, c0:c0 + 1], in1=up,
                                             op0=ALU.mult, op1=ALU.add).then_inc(gla_s, 1)
            for j in J_KD[-2:]:
                wait_job_copied(dve, j)
            dve.wait_ge(gla_o, len(GLA_ITEMS))
            for t in (1, 2):
                rope(dve, "k", kd, t, rope_k, t - 1)
            for j in (J_VD[1], J_VD[3]):
                job_copy(j)
            dve.wait_ge(oa_sq, 1)
            link(dve.reciprocal(s("rsa"), s("msa")))
            for t in range(T):
                v = o_a[:, t, :].rearrange("p (h v) -> p h v", h=GH)
                dve.tensor_tensor(v, v, s("rsa", GH * t, GH * t + GH)[:, :, None].to_broadcast((P, GH, DV)), ALU.mult).then_inc(oa_n, 1)
            family_copies(dve, F_QT, lambda h, b: dve.tensor_copy(qT[:, h, :], b[:, 0:NT]), 1)
            family_copies(dve, F_KT, lambda h, b: dve.tensor_copy(kT[:, h, :], b), 1)
            job_copy(J_VD[5])

            def neg_max(i):
                t, h = ATT_ITEMS[i]
                nk = SEQ if t == 0 else NKEY - SEQ
                m = 2 * (i % 2)
                dve.wait_ge(att_s, i + 1)
                link(dve.tensor_reduce(s("mx", m, m + 2), banks[:, 2 + m:4 + m, 0:nk], AX.X, ALU.max))
                if i >= 2:
                    dve.wait_ge(att_e, 2 * (i - 1))
                dve.tensor_scalar(s("nb", m, m + 2), s("mx", m, m + 2), -DH ** -0.5, None, ALU.mult).then_inc(att_nb, 1)

            def difference(i):
                t, h = ATT_ITEMS[i]
                nk = SEQ if t == 0 else NKEY - SEQ
                m = 2 * (i % 2)
                p0, p1, pd, _ = (x[:, 0:nk] for x in pp[i % 2])
                dve.wait_ge(att_e, 2 * (i + 1))
                link(dve.reciprocal(s("rs", m, m + 2), s("sum", m, m + 2)))
                note(dve.tensor_scalar(p1, p1, s("rs", m + 1, m + 2), s("nlam"), ALU.mult, ALU.mult))
                settle()
                if i >= 2:
                    dve.wait_ge(att_t, i - 1)
                dve.scalar_tensor_tensor(out=pd, in0=p0, scalar=s("rs", m, m + 1), in1=p1, op0=ALU.mult,
                                         op1=ALU.add).then_inc(att_pd, 1)

            n = len(ATT_ITEMS)
            for i in range(n + 2):
                if i < n:
                    neg_max(i)
                if 1 <= i <= n:
                    difference(i - 1)
                if i < n and i % 2:
                    for j in ATT_JOBS[i // 2]:
                        if JOBS[j].engine == "v":
                            job_copy(j)
            dve.wait_ge(oa_n, T)
            dve.wait_ge(gates_on, 1)
            for t in range(T):
                dve.tensor_tensor(o_a[:, t, :], o_a[:, t, :], ra[:, t, :], ALU.mult).then_inc(oa_g, 1)
            dve.wait_ge(od_sq, 1)
            link(dve.reciprocal(s("eb", 0, 24), s("eb", 24, 48)))
            for t in range(T):
                v = o_d[:, t, :].rearrange("p (h v) -> p h v", h=AH)
                dve.tensor_tensor(v, v, s("eb", AH * t, AH * t + AH)[:, :, None].to_broadcast((P, AH, P)), ALU.mult).then_inc(od_g, 1)
            family_copies(dve, F_OA, lambda k, b: dve.tensor_scalar(oaT[:, k, :], b[:, 0:NT], s("gla_g", k % 2, k % 2 + 1), None, ALU.mult), 1)
            family_copies(dve, F_OD, lambda k, b: dve.tensor_scalar(odT[:, k, :], b[:, 0:NT], s("sub_g"), None, ALU.mult), 1)
            dve.wait_ge(gates_on, 2)
            for j in J_PA:
                job_copy(j)
            for j in J_GB[-2:]:
                wait_job_copied(dve, j)
            dve.wait_ge(mod_stored, 16 * 8)
            wait_job_copied(dve, J_PA[-1])
            for n, j in enumerate(J_PB):
                job_copy(j)
                if n % 2 == 0 and n:
                    tile_copy(dve, F_M, n // 2 - 1, mT, dve.tensor_copy, 1)
            dve.wait_ge(bc_loaded, 160)
            for g in range(2):
                note(dve.tensor_scalar(sc2b[:, g, :], sc2b[:, g, :], 1.0, None, ALU.add))

            def layer_norms(t):
                stats(t).then_inc(x1_var[0], 1)
                dve.wait_ge(x1_std[0], t + 1)
                link(affine(x_r, t, l1g, l1b))
                stats(t).then_inc(x1_var[1], 1)
                dve.wait_ge(x1_std[1], t + 1)
                g = min(t, 1)
                affine(h2, t, sc2b[:, g, :], sh2b[:, g, :]).then_inc(h2_ready, 1)

            def softmax(t):
                dve.wait_ge(rt_log, t + 1)
                link(dve.tensor_reduce(rst[:, t:t + 1], banks[:, 4 + t, 0:NE], AX.X, ALU.max))
                dve.tensor_scalar(rst[:, 3 + t:4 + t], rst[:, t:t + 1], -1.0, None, ALU.mult).then_inc(rt_max, 1)
                dve.wait_ge(rt_exp, t + 1)
                link(dve.reciprocal(rst[:, 9 + t:10 + t], rst[:, 6 + t:7 + t]))
                dve.tensor_scalar(aff[:, t, :], aff[:, t, :], rst[:, 9 + t:10 + t], None, ALU.mult).then_inc(rt_aff, 1)

            def best(a, b, s0, cap):
                for r in range(cap // 8):
                    v = gates[:, s0 + 8 * r:s0 + 8 * r + 8]
                    link(dve.max(v, affT[:, a:b]))
                    note(dve.max_index(idxu[:, s0 + 8 * r:s0 + 8 * r + 8], v, affT[:, a:b]))
                    if r < cap // 8 - 1:
                        settle()
                        link(dve.match_replace(affT[:, a:b], v, affT[:, a:b], -1.0))

            job_copy(J_WO[0])
            tile_copy(dve, F_M, 2, mT, dve.tensor_copy, 1)
            job_copy(J_WO[1])
            layer_norms(0)
            job_copy(J_WO[2])
            job_copy(J_WO[3])
            tile_copy(dve, F_H2, 0, h2T, dve.tensor_copy, 1)
            layer_norms(1)
            softmax(0)
            job_copy(J_WO[4])
            job_copy(J_WO[5])
            tile_copy(dve, F_H2, 1, h2T, dve.tensor_copy, 1)
            layer_norms(2)
            note(dve.memset(slots, -1.0))
            note(dve.memset(gates, 0.0))
            dve.wait_ge(rt_tr, 1)
            link(dve.tensor_copy(affT[:, 0:P], banks[0:NE, 4, 0:P]))
            best(0, SEQ, CTX0, CAP_C)
            softmax(1)
            tile_copy(dve, F_H2, 2, h2T, dve.tensor_copy, 1)
            softmax(2)
            for t in (1, 2):
                dve.wait_ge(rt_tr, t + 1)
                note(dve.tensor_copy(affT[:, t * P:(t + 1) * P], banks[0:NE, 4 + t, 0:P]))
            settle()
            best(SEQ, NT, LAT0, CAP_L)
            settle()
            note(dve.tensor_scalar(slots[:, LAT0:LAT0 + CAP_L], idxu[:, LAT0:LAT0 + CAP_L], float(SEQ), None, ALU.add))
            link(dve.tensor_copy(slots[:, CTX0:CTX0 + CAP_C], idxu[:, CTX0:CTX0 + CAP_C]))
            dve.tensor_copy(slots[:, SLOT:2 * SLOT], slots[:, 0:SLOT]).then_inc(rt_slots, 1)
            dve.tensor_copy(gates[:, SLOT:2 * SLOT], gates[:, 0:SLOT]).then_inc(rt_slots, 1)
            dve.wait_ge(rt_tt, 1)
            dve.tensor_copy(idxT, banks[:, 7, 0:NE]).then_inc(rt_cols, 1)
            dve.tensor_copy(gateT, banks[:, 7, NE:2 * NE]).then_inc(rt_cols, 1)
            dve.wait_ge(rt_cols, 2)
            dve.wait_ge(rt_bc, 16)
            dve.wait_ge(ld_g2, 64)
            dve.wait_ge(acc_done, 6)

            with dve.Fori(0, NE) as e:
                for t in range(T):
                    dve.tensor_scalar(sel[:, t, :], slot_bc[:, bass.ds(e, 1), :].rearrange("p e s -> p (e s)"),
                                      iota_c[:, t:t + 1], None, ALU.is_equal).then_inc(sel_ready, 1)
                dve.tensor_scalar(selT, iota_r, idxT[:, bass.ds(e, 1)], gateT[:, bass.ds(e, 1)],
                                  ALU.is_equal, ALU.mult).then_inc(selT_ready, 1)
                dve.wait_ge(xet_done, e + 1)
                dve.tensor_copy(xeT, banks[:, 4, :].rearrange("p (i n) -> p i n", n=P)).then_inc(xet_cp, 1)
                dve.wait_ge(up_used, e * 4 + 4)
                for b, (i0, i1) in enumerate(FCH):
                    dve.wait_ge(silu_done, e * 3 + b + 1)
                    dve.tensor_tensor(hid[:, i0 * P:i1 * P], hid[:, i0 * P:i1 * P], banks[:, 3 + b, 0:(i1 - i0) * P],
                                      ALU.mult).then_inc(hid_done, 1)
                dve.wait_ge(down_used, e * 4 + 4)
                for dc in range(2):
                    cs = slice(dc * BANK, (dc + 1) * BANK)
                    dve.tensor_tensor(yrow[:, cs], banks[:, 6 + dc, :], g2s[:, cs], ALU.mult).then_inc(y_cp, 1)
                for t in range(T):
                    for dc in range(2):
                        n = 2 * t + dc
                        dve.wait_ge(comb_done, e * 6 + n + 1)
                        dst = x_r[:, t, dc * BANK:(dc + 1) * BANK]
                        dve.tensor_tensor(dst, dst, banks[:, n, :], ALU.add).then_inc(acc_done, 1)

            dve.wait_ge(acc_done, 6 * NE + 6)
            dve.wait_ge(ld_end, 32)
            for t in range(T):
                stats(t).then_inc(f_var, 1)
            for t in range(T):
                dve.wait_ge(f_std, t + 1)
                affine(x_r, t, l2g, l2b).then_inc(f_ready, 1)


_INS = ["x_prompt", "x_sample", "cache_diff_k", "cache_diff_v", "state_gla_fwd", "state_gla_bwd", "c", "c_ctx",
        "w_mod", "b_mod", "w_in", "w_alpha_f", "b_alpha_f", "w_alpha_b", "b_alpha_b", "gla_norm_g", "w_proj_a",
        "lambda_q1", "lambda_k1", "lambda_q2", "lambda_k2", "subln_g", "w_proj_b", "w_out", "ln1_g", "ln1_b",
        "w_router", "w_exp_gate", "w_exp_up", "w_exp_down", "ln2_g", "ln2_b"]
_OUTS = [(1, SEQ, D), (1, DEC, D), (1, 1, SEQ, AH, 2, DH), (1, 1, SEQ, AH, 2 * DH), (1, 1, GH, DK, DV), (1, 1, GH, DK, DV)]


def kernel(**inputs):
    import concourse.bacc as _bacc
    from concourse.bass_utils import run_bass_kernel_spmd as _run

    nc = _bacc.Bacc("TRN2", target_bir_lowering=False, num_devices=1)
    arrays, args = {}, []
    given = [(n, np.ascontiguousarray(inputs[n])) for n in _INS]
    given += list(zip(("const_f", "const_m", "const_r"), host_constants()))
    for name, a in given:
        arrays[f"in_{name}"] = a
        args.append(nc.dram_tensor(f"in_{name}", a.shape, mybir.dt.from_np(a.dtype), kind="ExternalInput").ap())
    for i, shape in enumerate(_OUTS):
        args.append(nc.dram_tensor(f"out_{i}", shape, F32, kind="ExternalOutput").ap())
    trunk_layer(nc, *args)
    r = _run(nc, [arrays], core_ids=[0])
    return tuple(r.results[0][f"out_{i}"] for i in range(len(_OUTS)))
```

```python
from collections import namedtuple
from contextlib import ExitStack

import numpy as np
import concourse.bass as bass
from concourse import mybir

ALU = mybir.AluOpType
ACT = mybir.ActivationFunctionType
AX = mybir.AxisListType
F32 = mybir.dt.float32
I32 = mybir.dt.int32
U32 = mybir.dt.uint32
F32R = mybir.dt.float32r

P = 128
D = 1024
KT = D // P
SEQ, DEC, PAST = 128, 256, 128
T = (SEQ + DEC) // P
NT = T * P
BANK = 512
GRID_W = 64

GH, DK, DV, RANK, CHUNK = 4, 128, 256, 16, 64
NCH = NT // CHUNK
GLA_TAU = 16.0
AH, DH = 8, 64
NKEY = NT + PAST
LAM_INIT = 0.8 - 0.6
ROPE_HALF = DH // 4
NE, FF = 16, 2816
CAP_C, CAP_L = 2 * SEQ // NE, 2 * DEC // NE
SLOT = 64
LAT0, CTX0, END0 = 0, CAP_L, CAP_L + CAP_C
ALPHA = 2.0 ** 0.25
EPS = 1e-6

C_QA, C_KA, C_VA, C_RA = 0, 512, 1024, 2048
C_AB = 3072
C_QD = C_AB + 2 * RANK
C_KD, C_VD, C_GA, C_GB = C_QD + D, C_QD + 2 * D, C_QD + 3 * D, C_QD + 4 * D

ORDER = (1, 2, 0)

WCHUNKS = [("mod", (0, ks)) for ks in range(4)]
for _n, _c in enumerate((C_QA, C_KA, C_VA, C_VA + BANK)):
    WCHUNKS += [("in", _c)] + [("mod", (1 + _n // 2, 2 * (_n % 2) + ks)) for ks in range(2)]
SPLIT = [len(WCHUNKS) + n for n in range(12)]
WCHUNKS += [("in", c0 + h * BANK) for c0 in (C_QD, C_KD, C_VD, C_RA, C_GA, C_GB) for h in range(2)]
WCHUNKS += [(w, h * BANK) for w in ("pa", "pb", "out") for h in range(2)]
WSLOTS = 4
SLOT_OF = [n % WSLOTS for n in range(SPLIT[0] - 2)] + [3, 0] + [2 - 2 * (m % 2) for m in range(12)] + [2, 3, 0, 1, 2, 3]
HIGH_SLOT_OF = {n: SLOT_OF[n] + 1 for n in SPLIT}
CHUNK_OF = {c: n for n, c in enumerate(WCHUNKS)}

Job = namedtuple("Job", "kind chunk i half engine")
JOBS = []


def _job(kind, chunk, i, half, engine):
    JOBS.append(Job(kind, chunk, i, half, engine))
    return len(JOBS) - 1


def _in_jobs(kind, c0, engines):
    return [_job(kind, CHUNK_OF["in", c0 + h * BANK], t, h, engines[(h * T + t) % len(engines)])
            for h in range(2) for t in range(T)]


def _out_jobs(kind, w, tile_major):
    order = [(t, h) for t in ORDER for h in range(2)] if tile_major else [(t, h) for h in range(2) for t in range(T)]
    return [_job(kind, CHUNK_OF[w, h * BANK], t, h, "v") for t, h in order]


J_MOD0 = _job("mod", 0, 0, 0, "v")
J_AB = _job("ab", None, 0, 0, "v")
J_QA, J_AL, J_KA, J_VA, J_MOD = [], [], [], [], {1: [], 2: []}


def _mod_job(b, ks):
    J_MOD[b].append(_job("mod", CHUNK_OF["mod", (b, ks)], b, ks, "v"))


for _h in range(GH):
    J_QA.append(_job("qa", CHUNK_OF["in", C_QA], _h, 0, "a"))
    J_AL += [_job("al", None, 2 * _h + _i, 0, "v") for _i in range(2)]
    if _h % 2:
        _mod_job(1, _h // 2)
for _h in range(GH):
    J_KA.append(_job("ka", CHUNK_OF["in", C_KA], _h, 0, "v"))
    if _h % 2:
        _mod_job(1, 2 + _h // 2)
for _h in range(2):
    for _t in range(T):
        J_VA.append(_job("va", CHUNK_OF["in", C_VA + _h * BANK], _t, _h, "a"))
        if _t < 2:
            _mod_job(2, 2 * _h + _t)
J_QD = _in_jobs("qd", C_QD, "a")
J_KD = _in_jobs("kd", C_KD, "a")
J_VD = _in_jobs("vd", C_VD, "a")
J_RA = _in_jobs("ra", C_RA, "av")
J_GA = _in_jobs("ga", C_GA, "va")
ATT_JOBS = J_RA + J_GA
J_GB = _in_jobs("gb", C_GB, "a")
J_PA = _out_jobs("pa", "pa", False)
J_PB = _out_jobs("pb", "pb", True)
J_WO = _out_jobs("wo", "out", True)


def copied_before(j, engine):
    return sum(1 for job in JOBS[:j] if job.engine == engine)


def last_job_of(chunk):
    return J_MOD0 if chunk < 4 else max(j for j, job in enumerate(JOBS) if job.chunk == chunk)


def freed_by(slot, chunk):
    before = [n for n in range(chunk) if slot in (SLOT_OF[n], HIGH_SLOT_OF.get(n))]
    return last_job_of(before[-1]) if before else None


def loads_into(slot, chunk):
    return sum(1 for n in range(chunk + 1) if SLOT_OF[n] == slot)


GLA_ITEMS = [(h, s) for h in range(GH) for s in range(2)]
GLA_TILES = {0: [0], 1: [1, 2]}
GLA_UPD = {0: [(0, 0), (0, 1), (1, 1), (1, 0)], 1: [(0, 2), (0, 3), (0, 4), (1, 5), (1, 4), (1, 3)]}

ATT_ITEMS = [(t, h) for t in range(T) for h in range(AH)]

F_HT, F_QT, F_KT, F_OA, F_OD = ((KT * f, KT) for f in range(5))
F_M, F_H2 = ((5 * KT + 2 * T * f, 2 * T) for f in range(2))

SM = {}
_at = 0
for _name, _n in (("sc1", 16), ("sh1", 16), ("bn", 36), ("mv", 6), ("std", 3), ("rstd", 3), ("eps", 1), ("one", 1),
                  ("eb", 48), ("balpha", 8), ("gla_g", 2), ("sub_g", 1), ("dots", 2), ("edots", 2),
                  ("nlam", 1), ("mx", 4), ("nb", 4), ("sum", 4), ("rs", 4), ("msa", 12), ("rsa", 12)):
    SM[_name] = (_at, _at + _n)
    _at += _n
SM_N = _at


def host_constants():
    pos = np.arange(DEC)
    inv = (10000.0 ** (-np.arange(ROPE_HALF, dtype=np.float32) / ROPE_HALF)).astype(np.float32)
    ang = np.stack([(pos // GRID_W).astype(np.float32)[:, None] * inv,
                    (pos % GRID_W).astype(np.float32)[:, None] * inv], 1)
    ang = ang.reshape(2, P, 2 * ROPE_HALF).transpose(1, 0, 2).reshape(P, -1)
    f = np.concatenate([np.eye(P), np.cos(ang), np.sin(ang),
                        np.arange(P)[:, None] + P * np.arange(T)[None]], 1).astype(np.float32)
    j, i = np.arange(P)[:, None], np.arange(P)[None]
    same = (j // CHUNK) == (i // CHUNK)
    m = np.concatenate([same & (j <= i), same & (j >= i)], 1).astype(np.int32)
    r = np.stack([(np.arange(NT) % CHUNK != 0), np.arange(NT)]).astype(np.float32)
    return f, m, r


CF_N = P + 4 * ROPE_HALF * 2 + T

QUARTER = 2 * FF
RING = 6 * QUARTER
FT = FF // (2 * P)
DOWN_GROUPS = [(0, 3), (3, 6), (6, 9), (9, 11)]
DOWN0 = 2 * QUARTER
HALF = FF // 2
FCH = [(0, 4), (4, 8), (8, 11)]

UNIT = T * D
WS0 = RING - WSLOTS * KT * BANK


def trunk_layer(nc, x_prompt, x_sample, cache_k, cache_v, st_f, st_b, c, c_ctx, w_mod, b_mod, w_in,
                w_alpha_f, b_alpha_f, w_alpha_b, b_alpha_b, gla_g, w_pa, lq1, lk1, lq2, lk2, sub_g, w_pb,
                w_out, ln1_g, ln1_b, w_router, w_gate, w_up, w_down, ln2_g, ln2_b, k_f, k_m, k_r,
                y_prompt, y_sample, new_k, new_v, new_f, new_b):
    mods = nc.dram_tensor("mods", (2, 6, D), F32, kind="Internal").ap()
    slot_tokens = nc.dram_tensor("slot_tokens", (NE, SLOT), F32, kind="Internal").ap()
    with ExitStack() as ctx:
        ctx.enter_context(nc.allow_non_contiguous_dma(reason="a few short vectors, one value per partition"))

        def sb(name, shape, dt=F32):
            return ctx.enter_context(nc.sbuf_tensor(name, shape, dt))

        def sem(name):
            return ctx.enter_context(nc.semaphore(name))

        with ExitStack() as parts:
            parts.enter_context(nc.sbuf_tensor("below_slots", [P, WS0], F32))
            slots_r = [parts.enter_context(nc.sbuf_tensor(f"slot{i}_parts", [P, KT * BANK], F32R)) for i in range(WSLOTS)]
            X_r, H_r = (parts.enter_context(nc.sbuf_tensor(n, [P, UNIT], F32R)) for n in ("X_parts", "H_parts"))
        ring = sb("ring", [P, RING])
        X, H, O1, O2, O3, O4 = (sb(n, [P, UNIT]) for n in ("X", "H", "O1", "O2", "O3", "O4"))
        kf = sb("kf", [P, CF_N])
        km = sb("km", [P, 2 * P], I32)
        cT = sb("cT", [P, KT, 32])
        sm = sb("sm", [P, SM_N])
        banks = ctx.enter_context(nc.psum_tensor("banks", [P, 8, BANK], F32))

        ident = kf[:, 0:P]
        ropec = kf[:, P:P + 64].rearrange("p (t a i) -> p t a i", t=2, a=2)
        ropes = kf[:, P + 64:P + 128].rearrange("p (t a i) -> p t a i", t=2, a=2)
        iota_c = kf[:, P + 128:P + 128 + T]

        def s(name, a=0, b=None):
            lo, hi = SM[name]
            return sm[:, lo + a:(lo + b if b is not None else hi)]

        def rows(t):
            return t.rearrange("p (t d) -> p t d", t=T)

        def cols(t):
            return t.rearrange("p (k n) -> p k n", n=NT)

        def reg(a, n):
            return ring[:, a:a + n]

        wslot = [reg(WS0 + i * KT * BANK, KT * BANK).rearrange("p (k n) -> p k n", k=KT) for i in range(WSLOTS)]
        wpart = [x[:].rearrange("p (k n) -> p k n", k=KT) for x in slots_r]
        A, B, C = reg(0, UNIT), reg(UNIT, UNIT), reg(2 * UNIT, UNIT)
        Dm, E = reg(3 * UNIT, UNIT), reg(4 * UNIT, UNIT)
        spare = reg(5 * UNIT, 2048)
        hT = cols(H[:])
        hT_high, hT_low = cols(X_r[:]), cols(H_r[:])
        x_r, xn = rows(X[:]), rows(O2[:])
        wab = O3[:, 0:256].rearrange("p (k n) -> p k n", k=KT)
        wal = O3[0:32, 256:1280]
        abT = O3[0:32, 1280:1280 + NT]
        lamv = O3[:, 1664:1920]
        crow = O3[0:16, 1920:2048]
        crow_s = O3[0:16, 2048:2176]
        lprod = O3[:, 2176:2304]
        modrow0, bmod0 = O1[:, 0:BANK], O1[:, BANK:2 * BANK]
        modrow = O1[:, 2 * BANK:4 * BANK].rearrange("p (b n) -> p b n", b=2)
        bmod = O1[:, 4 * BANK:6 * BANK].rearrange("p (b n) -> p b n", b=2)
        resetm = O4[:, 0:NT]
        qkT = A.rearrange("p (w h n) -> p w h n", w=2, h=GH)
        LG = B.rearrange("p (w m) -> p w m", w=2)
        LG4 = B.rearrange("p (w h n) -> p w h n", w=2, h=GH)
        LGc = B.rearrange("p (w c j) -> p w c j", w=2, j=CHUNK)
        QE, KE, KD = Dm, E, O2[:]

        def heads(t):
            return t.rearrange("p (w h n) -> p w h n", w=2, h=GH)

        va = rows(C)
        kdn = [A[:, i * 1024:(i + 1) * 1024].rearrange("p (a w r n) -> p a w r n", w=2, r=2, n=P) for i in range(2)]
        AF = A[:, 2048:2304].rearrange("p (a n) -> p a n", n=P)
        AB = A[:, 2304:2560].rearrange("p (a n) -> p a n", n=P)
        AS = [A[:, 2560 + 256 * i:2816 + 256 * i].rearrange("p (a n) -> p a n", n=P) for i in range(2)]
        S0 = spare.rearrange("p (w h v) -> p w h v", w=2, h=GH)
        SV = [B[:, i * 1536:(i + 1) * 1536].rearrange("p (u v) -> p u v", v=DV) for i in range(2)]
        eb = s("eb").rearrange("p (w c) -> p w c", w=2)
        o_a = rows(O1[:])
        qd, kd, vd = rows(O3[:]), rows(O4[:]), rows(O2[:])
        qT = cols(reg(0, UNIT))
        kT = reg(UNIT, AH * NKEY).rearrange("p (h n) -> p h n", n=NKEY)
        vc = reg(7168, D)
        kc = reg(8192, D)
        qz = [reg(8192 + 256 * i, 256).rearrange("p (q n) -> p q n", q=2) for i in range(2)]
        rope_q = [Dm[:, i * 512:(i + 1) * 512] for i in range(4)]
        rope_k = [A[:, i * 512:(i + 1) * 512] for i in range(4)]
        pp = [[Dm[:, (i * 4 + q) * 384:(i * 4 + q + 1) * 384] for q in range(4)] for i in range(2)]
        o_d = rows(O3[:])
        ra, ga, gb = rows(E), rows(O4[:]), rows(reg(0, UNIT))
        merged = rows(reg(UNIT, UNIT))
        oaT, odT = cols(reg(2 * UNIT, UNIT)), cols(Dm)
        pbtmp = spare[:, 2 * BANK:3 * BANK]
        mT = cols(H[:])
        wotmp = reg(WS0 - BANK, BANK)
        g1b = O1[:, 0:2 * D].rearrange("p (g d) -> p g d", g=2)
        l1g, l1b = O1[:, 2 * D:3 * D], O2[:, 0:D]
        sh2b = O2[:, D:3 * D].rearrange("p (g d) -> p g d", g=2)
        sc2b = O3[:, 0:2 * D].rearrange("p (g d) -> p g d", g=2)
        wr = O3[:, 2 * D:2 * D + KT * NE].rearrange("p (k e) -> p k e", k=KT)
        iota_r = O3[:, 2560:2560 + NT]
        h2 = rows(O4[:])
        h2T = cols(H[:])
        r0 = 2 * D + KT * NE
        aff = O3[:, r0:r0 + T * NE].rearrange("p (t e) -> p t e", t=T)
        rst = O3[:, r0 + 48:r0 + 64]
        affT = O1[0:NE, D:D + NT]
        slots = O1[0:NE, D + 384:D + 512]
        gates = O1[0:NE, D + 512:D + 640]
        idxu = O1[0:NE, D + 640:D + 704].bitcast(U32)
        idxT, gateT = H[:, 704:720], H[:, 720:736]
        slot_bc = H[:, 1024:1024 + NE * SLOT].rearrange("p (e s) -> p e s", e=NE)
        g2s, l2g, l2b = (O1[:, i * D:(i + 1) * D] for i in range(3))
        hid = O2[:, 0:HALF]
        hidT = O2[:, HALF:2 * HALF].rearrange("p (i n) -> p i n", n=P)
        sel = O2[:, 2 * HALF:2 * HALF + T * SLOT].rearrange("p (t s) -> p t s", t=T)
        xe = O3[:, 0:BANK]
        xeT = O3[:, BANK:2 * BANK].rearrange("p (i n) -> p i n", n=P)
        yrow = O3[:, 2 * BANK:4 * BANK]
        selT = O3[:, 4 * BANK:4 * BANK + NT]
        def bank(i, n=BANK):
            return banks[:, i, 0:n]

        ld_x = [sem("x_context_loaded"), sem("x_latent_loaded")]
        ld_x2 = sem("x_loaded_again")
        h_split = sem("h_split")
        w_split = sem("weight_tiles_split")
        ld_c = sem("conditioning_loaded")
        ld_k = sem("constants_loaded")
        ld_bm = [sem("first_mod_bias_loaded"), sem("mod_bias_loaded")]
        ld_ab = sem("decay_weights_loaded")
        ld_small = sem("small_vectors_loaded")
        ld_s0 = sem("cached_states_loaded")
        ld_cache = sem("cached_kv_loaded")
        wsem = [sem(f"weight_slot{i}_loaded") for i in range(WSLOTS)]
        zeroed = sem("zeroed_by_gpsimd")
        v_chain = sem("vector_steps")
        a_chain = sem("scalar_steps")
        g_chain = sem("gpsimd_steps")
        c_silu = sem("c_silu")
        c_turned = sem("c_turned")
        c_ready = sem("c_ready")
        ln_var = sem("ln_variances")
        ln_std = sem("ln_deviations")
        xn_ready = sem("x_normalised")
        mod_turned = sem("mod_turned")
        mod_ready = sem("mod_columns_ready")
        ht_out = [sem("modulated_by_scalar"), sem("modulated_by_vector")]
        mod_stored = sem("mod_rows_stored")
        job_done = sem("job_done")
        job_out = {"a": sem("job_copied_by_scalar"), "v": sem("job_copied_by_vector")}
        tb_done = sem("turned")
        tb_out = [sem("turned_copied_by_scalar"), sem("turned_copied_by_vector")]
        lg_soft = sem("gate_softplus")
        lg_sum = sem("decay_sums")
        lg_exp = sem("decay_exps")
        gla_in = sem("gla_operands")
        gla_kt = sem("gla_turned_and_scores")
        gla_kz = sem("gla_keys_zeroed")
        gla_kcp = sem("gla_keys_copied")
        gla_msk = sem("gla_scores_masked")
        gla_u = sem("gla_updates")
        gla_s = sem("gla_states")
        gla_st = sem("gla_states_stored")
        gla_o = sem("gla_outputs")
        gla_ocp = sem("gla_outputs_copied")
        oa_sq = sem("gla_deviations")
        oa_rs = sem("gla_norms")
        oa_n = sem("gla_normalised")
        dot_done = sem("lambda_dots")
        dot_exp = sem("lambda_exps")
        rope_done = {"q": sem("rope_queries_done"), "k": sem("rope_keys_done")}
        rope_tmp = {"q": sem("rope_query_products"), "k": sem("rope_key_products")}
        q_zero = sem("padded_queries_zeroed")
        q_pad = sem("queries_padded")
        kv_stored = sem("new_kv_stored")
        att_s = sem("att_scores")
        att_nb = sem("att_neg_max")
        att_e = sem("att_exps")
        att_pd = sem("att_diff_probs")
        att_t = sem("att_probs_turned")
        att_tcp = sem("att_probs_turned_copied")
        att_o = sem("att_outputs")
        att_ocp = sem("att_outputs_copied")
        od_sq = sem("att_deviations")
        gates_on = sem("gates_on")
        oa_g = sem("gla_gated")
        od_g = sem("att_normalised")
        bc_loaded = sem("broadcast_rows_loaded")
        x1_var = [sem("x1_variances"), sem("h2_variances")]
        x1_std = [sem("x1_deviations"), sem("h2_deviations")]
        h2_ready = sem("h2_ready")
        rt_log = sem("router_logits")
        rt_max = sem("router_neg_max")
        rt_exp = sem("router_exps")
        rt_aff = sem("router_probs")
        rt_tr = sem("router_probs_turned")
        rt_slots = sem("slots_ready")
        rt_stored = sem("slots_stored")
        rt_bc = sem("slots_broadcast")
        rt_tt = sem("slots_turned")
        rt_cols = sem("slot_columns_ready")
        land_g = [sem(f"gate_quarter{i}_loaded") for i in range(4)]
        land_u = [sem(f"up_quarter{i}_loaded") for i in range(4)]
        land_d = [sem(f"down_group{i}_loaded") for i in range(4)]
        gate_used = sem("gate_quarters_used")
        up_used = sem("up_quarters_used")
        down_used = sem("down_groups_used")
        sel_ready = sem("selection_ready")
        sel0_rows = sem("first_selection_rows")
        sel0_turned = sem("first_selection_turned")
        selT_ready = sem("combination_ready")
        xe_done = sem("expert_rows_done")
        xe_cp = sem("expert_rows_copied")
        xet_done = sem("expert_columns_done")
        xet_cp = sem("expert_columns_copied")
        silu_done = sem("gate_silu")
        hid_done = sem("hidden_ready")
        hidt_done = sem("hidden_turned")
        hidt_cp = sem("hidden_turned_copied")
        y_cp = sem("expert_out_copied")
        comb_done = sem("combined")
        acc_done = sem("accumulated")
        ld_g2 = sem("gate_rows_loaded")
        ld_end = sem("last_rows_loaded")
        f_var = sem("final_variances")
        f_std = sem("final_deviations")
        f_ready = sem("final_rows")
        stored = sem("outputs_stored")

        block = ctx.enter_context(nc.Block())

        def wait_job_copied(eng, j):
            who = JOBS[j].engine
            eng.wait_ge(job_out[who], copied_before(j, who) + 1)

        def wait_family(eng, f):
            for out in tb_out:
                eng.wait_ge(out, (f[0] + f[1]) // 2)

        def wait_tile(eng, f, n):
            for out in tb_out:
                eng.wait_ge(out, f[0] // 2 + n + 1)

        def rope(eng, key, src, t, tmp, n):
            v = src[:, t, :].rearrange("p (g a w i) -> p g a w i", a=2, w=2, i=ROPE_HALF)
            cs = ropec[:, t - 1][:, None].to_broadcast((P, 16, 2, ROPE_HALF))
            sn = ropes[:, t - 1][:, None].to_broadcast((P, 16, 2, ROPE_HALF))
            tmp = [x.rearrange("p (g a i) -> p g a i", a=2, i=ROPE_HALF) for x in tmp]
            if n:
                eng.wait_ge(rope_done[key], 2 * n)
            for i, (half, tab) in enumerate(((0, cs), (1, sn), (0, sn), (1, cs))):
                eng.tensor_tensor(tmp[i], v[:, :, :, half, :], tab, ALU.mult).then_inc(rope_tmp[key], 1)
            eng.wait_ge(rope_tmp[key], 4 * (n + 1))
            eng.tensor_tensor(v[:, :, :, 0, :], tmp[0], tmp[1], ALU.subtract).then_inc(rope_done[key], 1)
            eng.tensor_tensor(v[:, :, :, 1, :], tmp[2], tmp[3], ALU.add).then_inc(rope_done[key], 1)

        def w_chunk(n):
            kind, c0 = WCHUNKS[n]
            if kind == "mod":
                b, ks = c0
                return w_mod[0].rearrange("(k p) n -> p k n", p=P)[:, 2 * ks:2 * ks + 2, 4 * BANK * b:4 * BANK * (b + 1)]
            w = {"in": w_in, "pa": w_pa, "pb": w_pb, "out": w_out}[kind]
            return w[0].rearrange("(k p) n -> p k n", p=P)[:, :, c0:c0 + BANK]

        def w_slot(n):
            if WCHUNKS[n][0] == "mod":
                return wslot[SLOT_OF[n]].rearrange("p k n -> p (k n)").rearrange("p (k n) -> p k n", k=2)
            return wslot[SLOT_OF[n]]

        def wait_loaded(eng, n):
            eng.wait_ge(wsem[SLOT_OF[n]], 16 * loads_into(SLOT_OF[n], n))

        gate_v = [w_gate[0], w_up[0]]

        @block.sync
        def _(sp):
            sp.dma_start(crow[0:8, :], c_ctx.rearrange("(k p) -> k p", p=P)).then_inc(ld_c, 16)
            sp.dma_start(crow[8:16, :], c.rearrange("b (k p) -> (b k) p", p=P)).then_inc(ld_c, 16)
            sp.dma_start(kf[:], k_f).then_inc(ld_k, 16)
            sp.dma_start(x_r[:, 0, :], x_prompt[0]).then_inc(ld_x[0], 16)
            sp.dma_start(x_r[:, 1:3, :], x_sample[0].rearrange("(t p) d -> p t d", p=P)).then_inc(ld_x[1], 16)
            for n in range(len(WCHUNKS)):
                j = freed_by(SLOT_OF[n], n)
                if j is not None:
                    sp.wait_ge(job_done, j + 1)
                sp.dma_start(w_slot(n), w_chunk(n)).then_inc(wsem[SLOT_OF[n]], 16)
            sp.wait_ge(job_done, J_GB[-1] + 1)
            sp.dma_start(x_r[:, 0, :], x_prompt[0]).then_inc(ld_x2, 16)
            sp.dma_start(x_r[:, 1:3, :], x_sample[0].rearrange("(t p) d -> p t d", p=P)).then_inc(ld_x2, 16)

            def gate_up(w, e, q):
                return gate_v[w][e].rearrange("(k p) f -> p k f", p=P)[:, 2 * q:2 * q + 2, :]

            def quarter(i):
                return reg(i * QUARTER, QUARTER).rearrange("p (k f) -> p k f", k=2)

            def down(e, g):
                a, b = DOWN_GROUPS[g]
                sp.dma_start(reg(DOWN0 + 2 * a * D, 2 * (b - a) * D).rearrange("p (i d) -> p i d", d=D),
                             w_down[0][e].rearrange("(i p) d -> p i d", p=P)[:, 2 * a:2 * b, :]).then_inc(land_d[g], 16)

            wait_family(sp, F_M)
            for q in range(4):
                if q == 3:
                    wait_job_copied(sp, J_WO[-1])
                sp.dma_start(quarter(q), gate_up(0, 0, q)).then_inc(land_g[q], 16)
            for q in range(4):
                if q >= 2:
                    sp.wait_ge(gate_used, q - 1)
                sp.dma_start(quarter((4 + q) % 6), gate_up(1, 0, q)).then_inc(land_u[q], 16)
            for g in range(4):
                if g == 0:
                    sp.wait_ge(gate_used, 4)
                else:
                    sp.wait_ge(up_used, min(g, 2))
                down(0, g)
            with sp.Fori(1, NE) as e:
                for q, (used, n) in enumerate(((up_used, 1), (up_used, 0), (down_used, 3), (down_used, 2))):
                    sp.wait_ge(used, e * 4 - n)
                    sp.dma_start(quarter(q), gate_up(0, e, q)).then_inc(land_g[q], 16)
                for q, (used, n) in enumerate(((down_used, -1), (down_used, 0), (gate_used, 1), (gate_used, 2))):
                    sp.wait_ge(used, e * 4 + n)
                    sp.dma_start(quarter((4 + q) % 6), gate_up(1, e, q)).then_inc(land_u[q], 16)
                for g, (used, n) in enumerate(((gate_used, 4), (up_used, 1), (up_used, 2), (up_used, 2))):
                    sp.wait_ge(used, e * 4 + n)
                    down(e, g)
            for t in range(T):
                sp.wait_ge(f_ready, t + 1)
                dst = y_prompt[0] if t == 0 else y_sample[0, (t - 1) * P:t * P, :]
                sp.dma_start(dst, x_r[:, t, :]).then_inc(stored, 16)
            sp.wait_ge(stored, 16 * T)
            sp.wait_ge(kv_stored, 32)
            sp.wait_ge(gla_st, 16 * 2 * GH)

        @block.gpsimd
        def _(pool):
            pool.memset(cT[:], 0.0).then_inc(zeroed, 1)
            pool.memset(wal, 0.0).then_inc(zeroed, 1)
            for j in range(4):
                pool.dma_start(bmod0[32 * j:32 * j + 32], b_mod[:, j * BANK:(j + 1) * BANK].to_broadcast((32, BANK))).then_inc(ld_bm[0], 16)
            pool.dma_start(wab, w_in[0].rearrange("(k p) n -> p k n", p=P)[:, :, C_AB:C_AB + 2 * RANK]).then_inc(ld_ab, 16)
            pool.wait_ge(zeroed, 2)
            pool.dma_start(wal[0:RANK, 0:GH * DK], w_alpha_f[0]).then_inc(ld_ab, 16)
            pool.dma_start(wal[RANK:2 * RANK, GH * DK:2 * GH * DK], w_alpha_b[0]).then_inc(ld_ab, 16)
            pool.dma_start(s("balpha", 0, 4), b_alpha_f[0].rearrange("(h p) -> p h", p=P)).then_inc(ld_small, 16)
            pool.dma_start(s("balpha", 4, 8), b_alpha_b[0].rearrange("(h p) -> p h", p=P)).then_inc(ld_small, 16)
            pool.dma_start(resetm, k_r[0:1].to_broadcast((P, NT))).then_inc(ld_small, 16)
            pool.dma_start(km[:], k_m).then_inc(ld_small, 16)
            pool.dma_start(s("gla_g"), gla_g[0].rearrange("(a p) -> p a", p=P)).then_inc(ld_small, 16)
            pool.dma_start(s("sub_g"), sub_g[0].rearrange("(a p) -> p a", p=P)).then_inc(ld_small, 16)
            for i, v in enumerate((lq1, lk1, lq2, lk2)):
                pool.dma_start(lamv[:, i * DH:(i + 1) * DH], v.to_broadcast((P, DH))).then_inc(ld_small, 16)
            pool.wait_ge(job_done, J_MOD0 + 1)
            for j in range(4):
                src = b_mod.rearrange("o (b j n) -> o j b n", b=3, j=4)[:, j, 1:3]
                pool.dma_start(bmod[32 * j:32 * j + 32], src.to_broadcast((32, 2, BANK))).then_inc(ld_bm[1], 16)
            for w, st in enumerate((st_f, st_b)):
                pool.dma_start(S0[:, w], st[0, 0].rearrange("h k v -> k h v")).then_inc(ld_s0, 16)
            for b in (1, 2):
                if b == 2:
                    pool.wait_ge(gla_in, 3)
                    pool.memset(A[:, 0:2048], 0.0).then_inc(gla_kz, 1)
                    pool.memset(A[:, 2048:2560], 0.0).then_inc(gla_kz, 1)
                wait_job_copied(pool, J_MOD[b][-1])
                for j in range(4):
                    q, half = divmod(4 * b + j, 2)
                    pool.dma_start(mods[:, q, half * BANK:(half + 1) * BANK],
                                   modrow[32 * j:32 * j + 2, b - 1, :]).then_inc(mod_stored, 16)
            for h in range(GH):
                i = 2 * h
                pool.wait_ge(gla_s, 10 * h + 4)
                for w, dst in enumerate((new_f, new_b)):
                    pool.dma_start(dst[0, 0, h], SV[i % 2][:, 2 * w + 1, :]).then_inc(gla_st, 16)
            for j in (J_KD[0], J_KD[3]):
                wait_job_copied(pool, j)
            pool.dma_start(new_k[0, 0].rearrange("t h c d -> t (h c d)"), kd[:, 0, :]).then_inc(kv_stored, 16)
            pool.wait_ge(gla_o, len(GLA_ITEMS))
            pool.dma_start(kc, cache_k[0, 0].rearrange("t h c d -> t (h c d)")).then_inc(ld_cache, 16)
            pool.dma_start(vc, cache_v[0, 0].rearrange("t h d -> t (h d)")).then_inc(ld_cache, 16)
            for j in J_QD[-2:]:
                wait_job_copied(pool, j)
            for t in (1, 2):
                rope(pool, "q", qd, t, rope_q, t - 1)
            for j in (J_VD[0], J_VD[3]):
                wait_job_copied(pool, j)
            pool.dma_start(new_v[0, 0].rearrange("t h d -> t (h d)"), vd[:, 0, :]).then_inc(kv_stored, 16)
            pool.wait_ge(tb_done, F_KT[0] + F_KT[1])
            wait_family(pool, F_QT)
            for i in range(2):
                pool.memset(qz[i], 0.0).then_inc(q_zero, 1)
            pool.wait_ge(q_zero, 2)
            for i, (t, h) in enumerate(ATT_ITEMS):
                if i >= 2:
                    pool.wait_ge(att_s, i - 1)
                for q in range(2):
                    ps = slice(DH * q, DH * q + DH)
                    pool.tensor_copy(qz[i % 2][ps, q, :], qT[ps, h, t * P:(t + 1) * P]).then_inc(q_pad, 1)
            pool.wait_ge(mod_stored, 16 * 8)
            pool.wait_ge(kv_stored, 32)
            pool.wait_ge(tb_done, F_OD[0] + F_OD[1])
            for g in range(2):
                pool.dma_start(g1b[:, g, :], mods[g, 2:3].to_broadcast((P, D))).then_inc(bc_loaded, 16)
                pool.dma_start(sh2b[:, g, :], mods[g, 3:4].to_broadcast((P, D))).then_inc(bc_loaded, 16)
                pool.dma_start(sc2b[:, g, :], mods[g, 4:5].to_broadcast((P, D))).then_inc(bc_loaded, 16)
            pool.dma_start(l1g, ln1_g.to_broadcast((P, D))).then_inc(bc_loaded, 16)
            pool.dma_start(l1b, ln1_b.to_broadcast((P, D))).then_inc(bc_loaded, 16)
            pool.dma_start(wr, w_router[0].rearrange("(k p) e -> p k e", p=P)).then_inc(bc_loaded, 16)
            pool.dma_start(iota_r, k_r[1:2].to_broadcast((P, NT))).then_inc(bc_loaded, 16)
            wait_job_copied(pool, J_WO[-1])
            for p0, g in ((0, 1), (CAP_L, 0), (SLOT, 1), (SLOT + CAP_L, 0)):
                pool.dma_start(g2s[p0:p0 + 32], mods[g, 5:6].to_broadcast((32, D))).then_inc(ld_g2, 16)
            pool.wait_ge(rt_slots, 1)
            pool.dma_start(slot_tokens, slots[:, 0:SLOT]).then_inc(rt_stored, 16)
            pool.wait_ge(rt_stored, 16)
            pool.dma_start(slot_bc, slot_tokens.rearrange("e s -> (e s)")[None].to_broadcast((P, NE * SLOT))).then_inc(rt_bc, 16)
            pool.wait_ge(rt_tt, 1)
            pool.dma_start(l2g, ln2_g.to_broadcast((P, D))).then_inc(ld_end, 16)
            pool.dma_start(l2b, ln2_b.to_broadcast((P, D))).then_inc(ld_end, 16)

        @block.tensor
        def _(pe):
            turned = [0]

            def batch(srcs):
                b = turned[0]
                if b >= 2:
                    pe.wait_ge(tb_out[b % 2], (b - 2) // 2 + 1)
                for i, src in enumerate(srcs):
                    x = pe.transpose(banks[:, 2 + b % 2, i * P:(i + 1) * P], src, ident)
                x.then_inc(tb_done, 1)
                turned[0] += 1

            def job(j, k0=0, k1=KT):
                kind, chunk, i, _, _ = JOBS[j]
                if j >= 2 and k0 == 0:
                    wait_job_copied(pe, j - 2)
                out = banks[:, j % 2, :]

                def weights(n):
                    wait_loaded(pe, n)
                    return w_slot(n)

                if kind == "mod":
                    pairs = range(4) if j == J_MOD0 else (JOBS[j].half,)
                    for n, ks in enumerate(pairs):
                        w = weights(chunk + n)
                        for kk in range(2):
                            for q in range(4):
                                x = pe.matmul(out[32 * q:32 * q + 32, :], cT[:, 2 * ks + kk, :],
                                              w[:, kk, q * BANK:(q + 1) * BANK], start=(n == 0 and kk == 0),
                                              stop=(n == len(pairs) - 1 and kk == 1))
                elif kind in ("qa", "ka"):
                    w = weights(chunk)
                    for k in range(KT):
                        x = pe.matmul(out[:, 0:NT], w[:, k, i * P:(i + 1) * P], hT[:, k, :],
                                      start=(k == 0), stop=(k == KT - 1))
                elif kind == "ab":
                    pe.wait_ge(ld_ab, 48)
                    for k in range(KT):
                        pe.wait_ge(ht_out[k % 2], k // 2 + 1)
                        x = pe.matmul(out[0:32, 0:NT], wab[:, k, :], hT[:, k, :], start=(k == 0), stop=(k == KT - 1))
                elif kind == "al":
                    if i == 0:
                        wait_job_copied(pe, J_AB)
                    x = pe.matmul(out[:, 0:NT], wal[:, i * P:(i + 1) * P], abT, start=True, stop=True)
                elif chunk in SPLIT:
                    pe.wait_ge(w_split, KT * SPLIT.index(chunk) + k1)
                    high, low = wpart[HIGH_SLOT_OF[chunk]], wpart[SLOT_OF[chunk]]
                    for n, (a, w) in enumerate(((hT_high, high), (hT_high, low), (hT_low, high))):
                        for k in range(k0, k1):
                            if n == 0 and k == k0:
                                pe.wait_ge(h_split, 1)
                            if n == 2 and k in (k0, KT // 2):
                                pe.wait_ge(h_split, 2 + k // (KT // 2))
                            x = pe.matmul(out, a[:, k, i * P:(i + 1) * P], w[:, k, :], start=(n == 0 and k == 0),
                                          stop=(n == 2 and k == KT - 1))
                else:
                    w = weights(chunk)
                    src = {"pa": oaT, "pb": odT, "wo": mT}.get(kind, hT)
                    for k in range(k0, k1):
                        x = pe.matmul(out, src[:, k, i * P:(i + 1) * P], w[:, k, :], start=(k == 0), stop=(k == KT - 1))
                if k1 == KT:
                    x.then_inc(job_done, 1)

            pe.wait_ge(ld_k, 16)
            pe.wait_ge(c_silu, 1)
            pe.transpose(banks[:, 4, 0:16], crow_s, ident[0:16, 0:16]).then_inc(c_turned, 1)
            pe.wait_ge(xn_ready, T)
            for k in range(KT):
                batch([xn[:, t, k * P:(k + 1) * P] for t in range(T)])
            pe.wait_ge(c_ready, 1)
            job(J_MOD0)
            wait_job_copied(pe, J_MOD0)
            for i in range(4):
                x = pe.transpose(banks[:, 5, i * P:(i + 1) * P], modrow0[:, i * P:(i + 1) * P], ident)
            x.then_inc(mod_turned, 1)
            for j in range(J_AB, J_VA[-1] + 1):
                job(j)

            def gla_turn(i):
                h, q = GLA_ITEMS[i]
                if i:
                    pe.wait_ge(gla_kcp, i)
                    pe.wait_ge(gla_msk, 3 * i)
                for a, t in enumerate(GLA_TILES[q]):
                    for w in range(2):
                        pe.transpose(banks[:, 2, (2 * a + w) * P:(2 * a + w + 1) * P],
                                     heads(KD)[:, w, h, t * P:(t + 1) * P], ident)
                for a, t in enumerate(GLA_TILES[q]):
                    for w in range(2):
                        x = pe.matmul(banks[:, 3, (2 * a + w) * P:(2 * a + w + 1) * P],
                                      heads(KE)[:, w, h, t * P:(t + 1) * P], heads(QE)[:, w, h, t * P:(t + 1) * P],
                                      start=True, stop=True)
                x.then_inc(gla_kt, 1)

            def gla_update(i):
                h, q = GLA_ITEMS[i]
                pe.wait_ge(gla_kcp, i + 1)
                if i == 0:
                    for j in J_VA[-2:]:
                        wait_job_copied(pe, j)
                if i:
                    pe.wait_ge(gla_s, 10 * (i // 2) + (4 if i % 2 else 0))
                for u, (w, ch) in enumerate(GLA_UPD[q]):
                    t, r = divmod(ch, 2)
                    a = t - GLA_TILES[q][0]
                    x = pe.matmul(banks[:, 4 + u // 2, (u % 2) * DV:(u % 2 + 1) * DV],
                                  kdn[i % 2][:, a, w, r, :], va[:, t, h * DV:(h + 1) * DV], start=True, stop=True)
                x.then_inc(gla_u, 1)

            def gla_state(i, w, ch):
                h, q = GLA_ITEMS[i]
                if q == 0:
                    return SV[i % 2][:, 2 * w, :] if ch == 1 - w else None
                step = ch - 2 if w == 0 else 5 - ch
                return S0[:, w, h, :] if step == 0 else SV[i % 2][:, 3 * w + step - 1, :]

            def gla_out(i):
                h, q = GLA_ITEMS[i]
                pe.wait_ge(gla_msk, 3 * (i + 1))
                pe.wait_ge(gla_s, 10 * (i // 2) + (10 if i % 2 else 4))
                if i == 0:
                    pe.wait_ge(ld_s0, 32)
                if i:
                    pe.wait_ge(gla_ocp, i)
                for a, t in enumerate(GLA_TILES[q]):
                    out = banks[:, 7, a * DV:(a + 1) * DV]
                    terms = [(r, w, gla_state(i, w, 2 * t + r)) for w in range(2) for r in range(2)]
                    terms = [x for x in terms if x[2] is not None]
                    pe.matmul(out, AS[i % 2][:, a, :], va[:, t, h * DV:(h + 1) * DV], start=True, stop=False,
                              skip_group_check=True)
                    for r, w, st in terms:
                        c0 = t * P + r * 64
                        x = pe.matmul(out[64 * r:64 * r + 64, :], heads(QE)[:, w, h, c0:c0 + 64], st,
                                      start=False, stop=True, skip_group_check=True)
                x.then_inc(gla_o, 1)

            pe.wait_ge(gla_in, 3)
            more = list(J_QD + J_KD)
            for i in range(len(GLA_ITEMS)):
                gla_turn(i)
                job(more[0], 0, KT if i % 2 else KT // 2)
                gla_update(i)
                if i % 2:
                    more.pop(0)
                job(more.pop(0), 0 if i % 2 else KT // 2, KT)
                gla_out(i)
            for j in J_VD[:4]:
                job(j)
            pe.wait_ge(gla_kcp, len(GLA_ITEMS))
            pe.wait_ge(gla_msk, 3 * len(GLA_ITEMS))
            pe.wait_ge(gla_ocp, len(GLA_ITEMS))
            pe.wait_ge(rope_done["q"], 4)
            for h in range(AH):
                batch([qd[:, t, h * P:(h + 1) * P] for t in range(T)])
                job(J_VD[4], h, h + 1)
            pe.wait_ge(rope_done["k"], 4)
            pe.wait_ge(ld_cache, 32)
            for h in range(AH):
                batch([kd[:, t, h * P:(h + 1) * P] for t in range(T)] + [kc[:, h * P:(h + 1) * P]])
                job(J_VD[5], h, h + 1)
            wait_family(pe, F_KT)

            def keys(t):
                return (0, SEQ) if t == 0 else (SEQ, NKEY)

            def att_scores(i):
                t, h = ATT_ITEMS[i]
                a, b = keys(t)
                if i >= 2:
                    pe.wait_ge(att_e, 2 * (i - 1))
                pe.wait_ge(q_pad, 2 * (i + 1))
                for q in range(2):
                    x = pe.matmul(banks[:, 2 + 2 * (i % 2) + q, 0:b - a], qz[i % 2][:, q, :], kT[:, h, a:b],
                                  start=True, stop=True)
                x.then_inc(att_s, 1)

            def att_turn(i):
                t, h = ATT_ITEMS[i]
                pe.wait_ge(att_pd, i + 1)
                if i:
                    pe.wait_ge(att_tcp, i)
                for n in range(1 if t == 0 else 3):
                    x = pe.transpose(banks[:, 6, n * P:(n + 1) * P], pp[i % 2][2][:, n * P:(n + 1) * P], ident)
                x.then_inc(att_t, 1)

            def att_out(i):
                t, h = ATT_ITEMS[i]
                pe.wait_ge(att_tcp, i + 1)
                if i:
                    pe.wait_ge(att_ocp, i)
                vs = [vd[:, 0, :]] if t == 0 else [vd[:, 1, :], vd[:, 2, :], vc]
                for n, v in enumerate(vs):
                    x = pe.matmul(banks[:, 7, 0:P], pp[i % 2][3][:, n * P:(n + 1) * P], v[:, h * P:(h + 1) * P],
                                  start=(n == 0), stop=(n == len(vs) - 1))
                x.then_inc(att_o, 1)

            for j in J_VD[-2:]:
                wait_job_copied(pe, j)
            n = len(ATT_ITEMS)
            for i in range(n + 2):
                if i < n:
                    att_scores(i)
                if i < n:
                    job(ATT_JOBS[i // 2], KT // 2 * (i % 2), KT // 2 * (i % 2 + 1))
                if 1 <= i <= n:
                    att_turn(i - 1)
                if i >= 2:
                    att_out(i - 2)
            for j in J_GB[:2]:
                job(j)
            pe.wait_ge(oa_g, T)
            for k in range(KT):
                batch([o_a[:, t, k * P:(k + 1) * P] for t in range(T)])
                job(J_GB[2], k, k + 1)
            pe.wait_ge(od_g, T)
            for k in range(KT):
                batch([o_d[:, t, k * P:(k + 1) * P] for t in range(T)])
                job(J_GB[3], k, k + 1)
            for j in J_GB[4:]:
                job(j)
            wait_family(pe, F_OD)
            for j in J_PA:
                job(j)

            def turn_tile(src, n):
                t = ORDER[n]
                for b in range(2):
                    batch([src[:, t, k * P:(k + 1) * P] for k in range(4 * b, 4 * b + 4)])

            for n, j in enumerate(J_PB):
                job(j)
                if n % 2 == 0 and n:
                    wait_job_copied(pe, J_PB[n - 1])
                    turn_tile(merged, n // 2 - 1)

            def logits(n):
                t = ORDER[n]
                for k in range(KT):
                    if k % 4 == 0:
                        pe.wait_ge(tb_out[k // 4], F_H2[0] // 2 + n + 1)
                    x = pe.matmul(banks[:, 4 + t, 0:NE], h2T[:, k, t * P:(t + 1) * P], wr[:, k, :],
                                  start=(k == 0), stop=(k == KT - 1))
                x.then_inc(rt_log, 1)

            def turn_probs(n):
                t = ORDER[n]
                pe.wait_ge(rt_aff, n + 1)
                pe.transpose(banks[0:NE, 4 + t, 0:P], aff[:, t, :], ident).then_inc(rt_tr, 1)

            wait_tile(pe, F_M, 0)
            job(J_WO[0])
            wait_job_copied(pe, J_PB[-1])
            turn_tile(merged, 2)
            job(J_WO[1])
            wait_tile(pe, F_M, 1)
            job(J_WO[2])
            job(J_WO[3])
            pe.wait_ge(h2_ready, 1)
            turn_tile(h2, 0)
            wait_tile(pe, F_M, 2)
            job(J_WO[4])
            logits(0)
            job(J_WO[5])
            pe.wait_ge(h2_ready, 2)
            turn_tile(h2, 1)
            turn_probs(0)
            logits(1)
            pe.wait_ge(h2_ready, 3)
            turn_tile(h2, 2)
            turn_probs(1)
            logits(2)
            turn_probs(2)
            pe.wait_ge(rt_slots, 2)
            pe.transpose(banks[:, 7, 0:NE], slots, ident[0:NE, 0:NE])
            pe.transpose(banks[:, 7, NE:2 * NE], gates, ident[0:NE, 0:NE]).then_inc(rt_tt, 1)
            pe.wait_ge(sel0_rows, 1)
            for t in range(T):
                x = pe.transpose(banks[:, 6, t * SLOT:(t + 1) * SLOT], selT[0:SLOT, t * P:(t + 1) * P], ident[0:SLOT, 0:SLOT])
            x.then_inc(sel0_turned, 1)

            def expert(e, last=False):
                pe.wait_ge(sel_ready, e * T + T)
                pe.wait_ge(acc_done, e * 6 + 6)
                for t in range(T):
                    for w in range(2):
                        x = pe.matmul(banks[64 * w:64 * w + 64, 3, :], sel[:, t, :], h2[:, t, w * BANK:(w + 1) * BANK],
                                      start=(t == 0), stop=(t == T - 1))
                x.then_inc(xe_done, 1)
                pe.wait_ge(xe_cp, e + 1)
                for i in range(4):
                    x = pe.transpose(banks[:, 4, i * P:(i + 1) * P], xe[:, i * P:(i + 1) * P], ident)
                x.then_inc(xet_done, 1)
                pe.wait_ge(xet_cp, e + 1)
                for m, (land, used) in enumerate(((land_g, gate_used), (land_u, up_used))):
                    for q in range(4):
                        pe.wait_ge(land[q], e * 16 + 16)
                        w4 = reg(((4 * m + q) % 6) * QUARTER, QUARTER).rearrange("p (k i w n) -> p k i w n", k=2, w=2, n=P)
                        for kk in range(2):
                            k = 2 * q + kk
                            for b, (i0, i1) in enumerate(FCH):
                                for w in range(2):
                                    x = pe.matmul(banks[64 * w:64 * w + 64, 3 * m + b, 0:(i1 - i0) * P],
                                                  xeT[:, k % 4, 64 * (k // 4):64 * (k // 4) + 64],
                                                  w4[:, kk, i0:i1, w, :], start=(k == 0), stop=(k == KT - 1))
                        x.then_inc(used, 1)
                for b, (i0, i1) in enumerate(FCH):
                    pe.wait_ge(hid_done, e * 3 + b + 1)
                    for i in range(i0, i1):
                        x = pe.transpose(banks[:, b, (i - i0) * P:(i - i0 + 1) * P], hid[:, i * P:(i + 1) * P], ident)
                    x.then_inc(hidt_done, 1)
                pe.wait_ge(hidt_cp, e * 3 + 3)
                wd = reg(DOWN0, FF // P * D).rearrange("p (i w d) -> p i w d", w=2, d=D)
                for g, (i0, i1) in enumerate(DOWN_GROUPS):
                    if last and g in (1, 2):
                        for n in range(3 * g - 3, 3 * g):
                            t, dc = divmod(n, 2)
                            pe.matmul(banks[:, n, :], ident, x_r[:, t, dc * BANK:(dc + 1) * BANK],
                                      start=True, stop=False, skip_group_check=True)
                    pe.wait_ge(land_d[g], e * 16 + 16)
                    for i in range(i0, i1):
                        for dc in range(2):
                            for w in range(2):
                                x = pe.matmul(banks[64 * w:64 * w + 64, 6 + dc, :], hidT[:, i, 64 * w:64 * w + 64],
                                              wd[:, i, w, dc * BANK:(dc + 1) * BANK], start=(i == 0), stop=(i == FT - 1))
                    x.then_inc(down_used, 1)
                pe.wait_ge(selT_ready, e + 1)
                pe.wait_ge(y_cp, e * 2 + 2)
                for t in range(T):
                    for dc in range(2):
                        pe.matmul(banks[:, 2 * t + dc, :], selT[:, t * P:(t + 1) * P], yrow[:, dc * BANK:(dc + 1) * BANK],
                                  start=not last, stop=True, skip_group_check=last).then_inc(comb_done, 1)

            with pe.Fori(0, NE - 1) as e:
                expert(e)
            expert(NE - 1, last=True)

        def wait_turned(eng, b):
            eng.wait_ge(tb_done, b + 1)

        def family_copies(eng, f, copy, parity, beside=None):
            for k in range(parity, KT, 2):
                wait_turned(eng, f[0] + k)
                copy(k, banks[:, 2 + k % 2, :]).then_inc(tb_out[parity], 1)
                if beside:
                    beside(k)

        def tile_copy(eng, f, n, dst, copy, parity):
            t = ORDER[n]
            wait_turned(eng, f[0] + 2 * n + parity)
            copy(dst[:, 4 * parity:4 * parity + 4, t * P:(t + 1) * P],
                 banks[:, 2 + parity, :].rearrange("p (k n) -> p k n", n=P)).then_inc(tb_out[parity], 1)

        @block.scalar
        def _(act):
            steps = [0]

            def link(x):
                steps[0] += 1
                x.then_inc(a_chain, 1)
                act.wait_ge(a_chain, steps[0])

            def cp(out, in_, scale=1.0):
                return act.activation(out, in_, ACT.Copy, scale=scale)

            def job_copy(j):
                kind, chunk, i, half, who = JOBS[j]
                assert who == "a"
                act.wait_ge(job_done, j + 1)
                b = banks[:, j % 2, :]
                if kind == "qa":
                    x = cp(qkT[:, 0, i, :], b[:, 0:NT], DK ** -0.5)
                else:
                    dst = {"va": va, "qd": qd, "kd": kd, "vd": vd, "ra": ra, "ga": ga, "gb": gb}[kind]
                    if kind == "ga":
                        act.wait_ge(kv_stored, 32)
                    x = act.activation(dst[:, i, half * BANK:(half + 1) * BANK], b,
                                       ACT.Sigmoid if kind == "gb" else ACT.Copy)
                x.then_inc(job_out["a"], 1)

            act.wait_ge(ld_c, 32)
            act.activation(crow_s, crow, ACT.Silu).then_inc(c_silu, 1)
            act.wait_ge(ln_var, T)
            act.activation(s("std"), s("mv").rearrange("p (t w) -> p t w", w=2)[:, :, 1], ACT.Sqrt,
                           bias=s("eps")).then_inc(ln_std, 1)

            family_copies(act, F_HT, lambda k, b: cp(hT[:, k, :], b[:, 0:NT]), 0)
            act.wait_ge(tb_out[0], F_HT[1] // 2)
            act.wait_ge(mod_ready, 2)
            sc, sh = (s(x).rearrange("p (k g) -> p k g", g=2) for x in ("sc1", "sh1"))
            for k in range(0, KT, 2):
                for g, ns in enumerate((slice(0, P), slice(P, NT))):
                    x = act.activation(hT[:, k, ns], hT[:, k, ns], ACT.Identity, scale=sc[:, k, g:g + 1], bias=sh[:, k, g:g + 1])
                x.then_inc(ht_out[0], 1)
            for j in J_QA:
                job_copy(j)
            wait_job_copied(act, J_AL[-1])
            link(act.activation(QE, B, ACT.Abs))
            link(act.activation(QE, QE, ACT.Exp, scale=-1.0))
            act.activation(QE, QE, ACT.Ln, bias=s("one")).then_inc(lg_soft, 1)
            for j in J_VA[:2]:
                job_copy(j)
            act.wait_ge(lg_sum, 2)
            act.activation(KD, KD, ACT.Exp).then_inc(lg_exp, 1)
            act.activation(QE, B, ACT.Exp).then_inc(lg_exp, 1)
            job_copy(J_VA[2])
            act.activation(KE, B, ACT.Exp, scale=-1.0).then_inc(lg_exp, 1)
            ebv = eb.rearrange("p w (h c) -> p w h c", h=GH)
            act.activation(eb[:, 0, :], LGc[:, 0, :, CHUNK - 1], ACT.Exp)
            act.activation(eb[:, 1, :], LGc[:, 1, :, 0], ACT.Exp).then_inc(lg_exp, 1)
            act.wait_ge(dot_done, 2)
            act.activation(s("edots"), s("dots"), ACT.Exp).then_inc(dot_exp, 1)
            for j in J_VA[3:]:
                job_copy(j)

            more = list(J_QD + J_KD)
            act.wait_ge(gla_in, 3)
            act.wait_ge(mod_stored, 16 * 8)
            for i, (h, q) in enumerate(GLA_ITEMS):
                nt = len(GLA_TILES[q])
                act.wait_ge(gla_kt, i + 1)
                if i == 0:
                    act.wait_ge(gla_kz, 1)
                for r in range(2):
                    rs = slice(CHUNK * r, CHUNK * r + CHUNK)
                    x = cp(kdn[i % 2][rs, 0:nt, :, r], banks[rs, 2, 0:nt * 2 * P].rearrange("p (a w n) -> p a w n", w=2, n=P))
                x.then_inc(gla_kcp, 1)
                job_copy(more.pop(0))
                if i % 2:
                    job_copy(more.pop(0))
                act.wait_ge(gla_o, i + 1)
                t0 = GLA_TILES[q][0]
                link(cp(o_a[:, t0:t0 + nt, h * DV:(h + 1) * DV], banks[:, 7, 0:nt * DV].rearrange("p (a v) -> p a v", v=DV)))
                for a in range(nt):
                    b = banks[:, 7, a * DV:(a + 1) * DV]
                    n = GH * (t0 + a) + h
                    x = act.activation(b, b, ACT.Square, accum_out=s("msa", n, n + 1))
                x.then_inc(gla_ocp, 1)
            act.wait_ge(gla_ocp, len(GLA_ITEMS))
            act.activation(s("msa"), s("msa"), ACT.Sqrt, scale=1.0 / DV, bias=s("eps")).then_inc(oa_sq, 1)
            def norms(t):
                if t == 0:
                    act.wait_ge(oa_rs, 1)
                for h in range(GH):
                    v = o_a[:, t, h * DV:(h + 1) * DV]
                    x = act.activation(v, v, ACT.Copy, scale=s("rsa", GH * t + h, GH * t + h + 1))
                x.then_inc(oa_n, 1)

            for n, j in enumerate(J_VD[:4]):
                job_copy(j)
                if n < T:
                    norms(n)
            family_copies(act, F_QT, lambda h, b: cp(qT[:, h, :], b[:, 0:NT]), 0)
            job_copy(J_VD[4])
            family_copies(act, F_KT, lambda h, b: cp(kT[:, h, :], b), 0)
            job_copy(J_VD[5])

            def exps(i):
                t, h = ATT_ITEMS[i]
                nk = SEQ if t == 0 else NKEY - SEQ
                act.wait_ge(att_nb, i + 1)
                if i >= 2:
                    act.wait_ge(att_pd, i - 1)
                for q in range(2):
                    m = 2 * (i % 2) + q
                    act.activation(pp[i % 2][q][:, 0:nk], banks[:, 2 + m, 0:nk], ACT.Exp, scale=DH ** -0.5,
                                   bias=s("nb", m, m + 1), accum_out=s("sum", m, m + 1)).then_inc(att_e, 1)

            n = len(ATT_ITEMS)
            for i in range(n + 2):
                if i < n:
                    exps(i)
                if 1 <= i <= n:
                    nk = 1 if ATT_ITEMS[i - 1][0] == 0 else 3
                    act.wait_ge(att_t, i)
                    cp(pp[(i - 1) % 2][3][:, 0:nk * P], banks[:, 6, 0:nk * P]).then_inc(att_tcp, 1)
                if i >= 2:
                    t, h = ATT_ITEMS[i - 2]
                    act.wait_ge(att_o, i - 1)
                    b = banks[:, 7, 0:P]
                    link(cp(o_d[:, t, h * P:(h + 1) * P], b))
                    act.activation(b, b, ACT.Square, accum_out=s("eb", i - 2, i - 1)).then_inc(att_ocp, 1)
                if i < n and i % 2 and JOBS[ATT_JOBS[i // 2]].engine == "a":
                    job_copy(ATT_JOBS[i // 2])
            act.wait_ge(att_ocp, n)
            act.activation(s("eb", 24, 48), s("eb", 0, 24), ACT.Sqrt, scale=1.0 / (2 * DH), bias=s("eps")).then_inc(od_sq, 1)
            for j in (J_RA[-1], J_RA[-2]):
                wait_job_copied(act, j)
            act.activation(E, E, ACT.Silu).then_inc(gates_on, 1)
            for j in J_GB[:2]:
                job_copy(j)
            family_copies(act, F_OA, lambda k, b: act.activation(oaT[:, k, :], b[:, 0:NT], ACT.Copy, scale=s("gla_g", k % 2, k % 2 + 1)), 0)
            job_copy(J_GB[2])
            family_copies(act, F_OD, lambda k, b: act.activation(odT[:, k, :], b[:, 0:NT], ACT.Copy, scale=s("sub_g")), 0)
            job_copy(J_GB[3])
            for j in (J_GA[-1], J_GA[-2]):
                wait_job_copied(act, j)
            act.activation(O4[:], O4[:], ACT.Sigmoid).then_inc(gates_on, 1)
            for j in J_GB[4:]:
                job_copy(j)
            for t in range(T):
                tile_copy(act, F_M, t, mT, cp, 0)

            def router_exps(n):
                t = ORDER[n]
                act.wait_ge(rt_max, n + 1)
                act.activation(aff[:, t, :], banks[:, 4 + t, 0:NE], ACT.Exp, bias=rst[:, 3 + t:4 + t],
                               accum_out=rst[:, 6 + t:7 + t]).then_inc(rt_exp, 1)

            def times_alpha(n):
                t = ORDER[n]
                act.wait_ge(h2_ready, n + 1)
                act.activation(x_r[:, t, :], x_r[:, t, :], ACT.Copy, scale=ALPHA).then_inc(acc_done, 2)

            def x1_dev(n, m):
                t = ORDER[n]
                act.wait_ge(x1_var[m], n + 1)
                act.activation(s("std", t, t + 1), s("mv", 2 * t + 1, 2 * t + 2), ACT.Sqrt, bias=s("eps")).then_inc(x1_std[m], 1)

            for n in range(2):
                x1_dev(n, 0)
                x1_dev(n, 1)
                if n:
                    times_alpha(0)
                    router_exps(0)
                tile_copy(act, F_H2, n, h2T, cp, 0)
            x1_dev(2, 0)
            x1_dev(2, 1)
            times_alpha(1)
            router_exps(1)
            tile_copy(act, F_H2, 2, h2T, cp, 0)
            router_exps(2)
            times_alpha(2)

            with act.Fori(0, NE) as e:
                act.wait_ge(xe_done, e + 1)
                act.activation(xe, banks[:, 3, :], ACT.Copy).then_inc(xe_cp, 1)
                act.wait_ge(gate_used, e * 4 + 4)
                for b, (i0, i1) in enumerate(FCH):
                    act.activation(hid[:, i0 * P:i1 * P], banks[:, b, 0:(i1 - i0) * P], ACT.Silu).then_inc(silu_done, 1)
                for b, (i0, i1) in enumerate(FCH):
                    act.wait_ge(hidt_done, e * 3 + b + 1)
                    act.activation(hidT[:, i0:i1, :], banks[:, b, 0:(i1 - i0) * P].rearrange("p (i n) -> p i n", n=P),
                                   ACT.Copy).then_inc(hidt_cp, 1)
            for t in range(T):
                act.wait_ge(f_var, t + 1)
                act.activation(s("std", t, t + 1), s("mv", 2 * t + 1, 2 * t + 2), ACT.Sqrt, bias=s("eps")).then_inc(f_std, 1)

        @block.vector
        def _(dve):
            steps = [0]

            def note(x):
                steps[0] += 1
                return x.then_inc(v_chain, 1)

            def settle():
                dve.wait_ge(v_chain, steps[0])

            def link(x):
                note(x)
                settle()

            def stats(t, src=x_r):
                bn = s("bn").rearrange("p (t w n) -> p t w n", t=T, n=6)
                for w in range(2):
                    note(dve.bn_stats(bn[:, t, w, :], src[:, t, w * BANK:(w + 1) * BANK]))
                settle()
                return dve.bn_aggr(s("mv", 2 * t, 2 * t + 2), bn[:, t].rearrange("p w n -> p (w n)"))

            def affine(dst, t, g, b, src=x_r):
                link(dve.reciprocal(s("rstd", t, t + 1), s("std", t, t + 1)))
                link(dve.scalar_tensor_tensor(out=dst[:, t, :], in0=src[:, t, :], scalar=s("mv", 2 * t, 2 * t + 1), in1=g,
                                              op0=ALU.subtract, op1=ALU.mult))
                return dve.scalar_tensor_tensor(out=dst[:, t, :], in0=dst[:, t, :], scalar=s("rstd", t, t + 1), in1=b,
                                                op0=ALU.mult, op1=ALU.add)

            def job_copy(j):
                kind, chunk, i, half, who = JOBS[j]
                assert who == "v"
                dve.wait_ge(job_done, j + 1)
                b = banks[:, j % 2, :]
                cs = slice(half * BANK, (half + 1) * BANK)
                g = min(i, 1)
                if j == J_MOD0:
                    dve.wait_ge(ld_bm[0], 64)
                    x = dve.tensor_tensor(modrow0, b, bmod0, ALU.add)
                elif kind == "mod":
                    if half == 0:
                        dve.wait_ge(ld_bm[1], 64)
                    else:
                        dve.wait_ge(job_out["v"], copied_before(J_MOD[i][half - 1], "v") + 1)
                    x = dve.tensor_tensor(modrow[:, i - 1, :], b, modrow[:, i - 1, :] if half else bmod[:, i - 1, :], ALU.add)
                elif kind == "ka":
                    x = dve.tensor_copy(qkT[:, 1, i, :], b[:, 0:NT])
                elif kind == "ab":
                    x = dve.tensor_copy(abT, b[0:32, 0:NT])
                elif kind == "al":
                    if i == 0:
                        dve.wait_ge(ld_small, 160)
                    x = dve.tensor_scalar(LG4[:, i // GH, i % GH, :], b[:, 0:NT], s("balpha", i, i + 1), None, ALU.add)
                elif kind == "pa":
                    x = dve.tensor_tensor(merged[:, i, cs], b, ga[:, i, cs], ALU.mult)
                elif kind == "pb":
                    link(dve.tensor_tensor(pbtmp, b, gb[:, i, cs], ALU.mult))
                    x = dve.tensor_tensor(merged[:, i, cs], merged[:, i, cs], pbtmp, ALU.add)
                elif kind == "wo":
                    link(dve.tensor_tensor(wotmp, b, g1b[:, g, cs], ALU.mult))
                    x = dve.scalar_tensor_tensor(out=x_r[:, i, cs], in0=x_r[:, i, cs], scalar=ALPHA, in1=wotmp,
                                                 op0=ALU.mult, op1=ALU.add)
                else:
                    if kind == "ga":
                        dve.wait_ge(kv_stored, 32)
                    dst = {"vd": vd, "ra": ra, "ga": ga}[kind]
                    x = dve.tensor_copy(dst[:, i, cs], b)
                x.then_inc(job_out["v"], 1)
                if kind in ("pb", "wo"):
                    dve.wait_ge(job_out["v"], copied_before(j, "v") + 1)

            note(dve.memset(s("eps"), EPS))
            note(dve.memset(s("one"), 1.0))
            dve.wait_ge(zeroed, 1)
            dve.wait_ge(c_turned, 1)
            dve.tensor_copy(cT[:, :, 0:2], banks[:, 4, 0:16].rearrange("p (g k) -> p k g", g=2)).then_inc(c_ready, 1)
            for t in range(T):
                dve.wait_ge(ld_x[min(t, 1)], 16)
                stats(t).then_inc(ln_var, 1)
            dve.wait_ge(ln_std, 1)
            link(dve.reciprocal(s("rstd"), s("std")))
            for t in range(T):
                dve.tensor_scalar(xn[:, t, :], x_r[:, t, :], s("mv", 2 * t, 2 * t + 1), s("rstd", t, t + 1),
                                  ALU.subtract, ALU.mult).then_inc(xn_ready, 1)
            family_copies(dve, F_HT, lambda k, b: dve.tensor_copy(hT[:, k, :], b[:, 0:NT]), 1)
            job_copy(J_MOD0)
            dve.wait_ge(mod_turned, 1)
            mt = banks[:, 5, :].rearrange("p (i j g) -> p i j g", i=4, j=4)
            dve.tensor_copy(s("sh1").rearrange("p (j i g) -> p i j g", j=2, g=2), mt[:, :, 0:2, 0:2]).then_inc(mod_ready, 1)
            dve.tensor_scalar(s("sc1").rearrange("p (j i g) -> p i j g", j=2, g=2), mt[:, :, 2:4, 0:2], 1.0, None,
                              ALU.add).then_inc(mod_ready, 1)
            dve.wait_ge(tb_out[1], F_HT[1] // 2)
            dve.wait_ge(mod_ready, 2)
            sc, sh = (s(x).rearrange("p (k g) -> p k g", g=2) for x in ("sc1", "sh1"))
            for k in range(1, KT, 2):
                for g, ns in enumerate((slice(0, P), slice(P, NT))):
                    x = dve.tensor_scalar(hT[:, k, ns], hT[:, k, ns], sc[:, k, g:g + 1], sh[:, k, g:g + 1], ALU.mult, ALU.add)
                x.then_inc(ht_out[1], 1)
            for j in range(J_AB, J_AL[-1] + 1):
                if JOBS[j].engine == "v":
                    job_copy(j)
            dve.wait_ge(job_out["v"], copied_before(J_AL[-1], "v") + 1)
            for w in range(2):
                note(dve.tensor_tensor(lprod[:, w * DH:(w + 1) * DH], lamv[:, 2 * w * DH:(2 * w + 1) * DH],
                                       lamv[:, (2 * w + 1) * DH:(2 * w + 2) * DH], ALU.mult))
            settle()
            for w in range(2):
                dve.tensor_reduce(s("dots", w, w + 1), lprod[:, w * DH:(w + 1) * DH], AX.X, ALU.add).then_inc(dot_done, 1)
            for j in range(J_AL[-1] + 1, J_VA[0]):
                job_copy(j)
            dve.wait_ge(lg_soft, 1)
            link(dve.scalar_tensor_tensor(out=B, in0=B, scalar=0.0, in1=QE, op0=ALU.min, op1=ALU.subtract))
            link(dve.tensor_scalar(B, B, 1.0 / GLA_TAU, None, ALU.mult))
            for h in range(GH):
                note(dve.tensor_tensor_scan(heads(QE)[:, 1, h, :], resetm, LG4[:, 1, h, :], 0.0, ALU.mult, ALU.add))
                note(dve.tensor_tensor_scan(heads(QE)[:, 0, h, :], resetm, LG4[:, 0, h, :], 0.0, ALU.mult, ALU.add))
            settle()
            QEc = QE.rearrange("p (w c j) -> p w c j", w=2, j=CHUNK)
            KDc = KD.rearrange("p (w c j) -> p w c j", w=2, j=CHUNK)
            full = (P, GH * NCH, CHUNK)
            job_copy(J_MOD[2][0])
            note(dve.tensor_copy(LG[:, 0, :], QE[:, 0:GH * NT]))
            link(dve.tensor_tensor(LG[:, 1, :], LG[:, 1, :], QE[:, GH * NT:], ALU.subtract))
            link(dve.tensor_tensor(LGc[:, 1], LGc[:, 1], QEc[:, 1, :, CHUNK - 1:CHUNK].to_broadcast(full), ALU.add))
            dve.tensor_tensor(KDc[:, 0], LGc[:, 0, :, CHUNK - 1:CHUNK].to_broadcast(full), LGc[:, 0], ALU.subtract).then_inc(lg_sum, 1)
            dve.tensor_tensor(KDc[:, 1], LGc[:, 1, :, 0:1].to_broadcast(full), LGc[:, 1], ALU.subtract).then_inc(lg_sum, 1)
            wait_job_copied(dve, J_KA[-1])
            wait_job_copied(dve, J_QA[-1])
            job_copy(J_MOD[2][1])
            both = (P, 2, GH * NT)
            for n, (dst, w) in enumerate(((KD, 1), (QE, 0), (KE, 1))):
                dve.wait_ge(lg_exp, n + 1)
                v = dst.rearrange("p (w m) -> p w m", w=2)
                src = A[:, w * GH * NT:(w + 1) * GH * NT]
                dve.tensor_tensor(v, v, src[:, None].to_broadcast(both), ALU.mult).then_inc(gla_in, 1)
            dve.wait_ge(lg_exp, 4)
            dve.wait_ge(gla_in, 3)
            job_copy(J_MOD[2][2])

            def split(m, k0=0, k1=KT):
                n = SPLIT[m]
                if k0 == 0:
                    wait_loaded(dve, n)
                    dve.wait_ge(job_done, freed_by(HIGH_SLOT_OF[n], n) + 1)
                w, high, low = w_slot(n), wpart[HIGH_SLOT_OF[n]], wpart[SLOT_OF[n]]
                for k in range(k0, k1):
                    note(dve.tensor_copy(high[:, k, :], w[:, k, :]))
                settle()
                for k in range(k0, k1):
                    dve.tensor_tensor(low[:, k, :], w[:, k, :], high[:, k, :].bitcast(F32), ALU.subtract).then_inc(w_split, 1)

            dve.tensor_copy(X_r[:], H[:]).then_inc(h_split, 1)
            split(0)
            job_copy(J_MOD[2][3])
            dve.wait_ge(job_done, J_VA[-1] + 1)
            dve.wait_ge(h_split, 1)
            for ks in (slice(0, 4 * NT), slice(4 * NT, 8 * NT)):
                dve.tensor_tensor(H_r[:, ks], H[:, ks], X_r[:, ks].bitcast(F32), ALU.subtract).then_inc(h_split, 1)
            dve.wait_ge(dot_exp, 1)
            link(dve.tensor_tensor(s("nlam"), s("edots", 1, 2), s("edots", 0, 1), ALU.subtract))
            note(dve.tensor_scalar(s("nlam"), s("nlam"), LAM_INIT, None, ALU.subtract))
            note(dve.tensor_scalar(s("sub_g"), s("sub_g"), 1.0 - LAM_INIT, None, ALU.mult))
            settle()
            dve.wait_ge(gla_kz, 2)
            for i, (h, q) in enumerate(GLA_ITEMS):
                nt = len(GLA_TILES[q])
                dve.wait_ge(gla_kt, i + 1)
                sc = banks[:, 3, 0:nt * 2 * P].rearrange("p (a w n) -> p a w n", w=2, n=P)
                for w, dst in enumerate((AF, AB)):
                    for a in range(nt):
                        x = dve.copy_predicated(dst[:, a, :], km[:, w * P:(w + 1) * P], sc[:, a, w, :])
                    x.then_inc(gla_msk, 1)
                dve.wait_ge(gla_msk, 3 * i + 2)
                dve.tensor_tensor(AS[i % 2][:, 0:nt], AF[:, 0:nt], AB[:, 0:nt], ALU.add).then_inc(gla_msk, 1)
                if q:
                    split(h + 1, 0, KT // 2)
                dve.wait_ge(gla_u, i + 1)
                if q == 0 and i >= 2:
                    dve.wait_ge(gla_st, 16 * i)
                if q == 1 and i == 1:
                    dve.wait_ge(ld_s0, 32)
                base = 10 * (i // 2) + (4 if q else 0)
                for u, (w, ch) in enumerate(GLA_UPD[q]):
                    up = banks[:, 4 + u // 2, (u % 2) * DV:(u % 2 + 1) * DV]
                    dst = SV[i % 2][:, u, :]
                    first = u % len([x for x in GLA_UPD[q] if x[0] == w]) == 0
                    if q == 0 and first:
                        dve.tensor_copy(dst, up).then_inc(gla_s, 1)
                        continue
                    prev = S0[:, w, h, :] if first else SV[i % 2][:, u - 1, :]
                    if not first:
                        dve.wait_ge(gla_s, base + u)
                    c0 = h * NCH + ch
                    dve.scalar_tensor_tensor(out=dst, in0=prev, scalar=eb[:, w, c0:c0 + 1], in1=up,
                                             op0=ALU.mult, op1=ALU.add).then_inc(gla_s, 1)
                if q:
                    split(h + 1, KT // 2, KT)
            dve.wait_ge(oa_sq, 1)
            dve.reciprocal(s("rsa"), s("msa")).then_inc(oa_rs, 1)
            for j in J_KD[-2:]:
                wait_job_copied(dve, j)
            dve.wait_ge(gla_o, len(GLA_ITEMS))
            for t in (1, 2):
                rope(dve, "k", kd, t, rope_k, t - 1)
            split(5)
            family_copies(dve, F_QT, lambda h, b: dve.tensor_copy(qT[:, h, :], b[:, 0:NT]), 1)
            family_copies(dve, F_KT, lambda h, b: dve.tensor_copy(kT[:, h, :], b), 1, lambda k: split(6, k - 1, k + 1))

            def neg_max(i):
                t, h = ATT_ITEMS[i]
                nk = SEQ if t == 0 else NKEY - SEQ
                m = 2 * (i % 2)
                dve.wait_ge(att_s, i + 1)
                link(dve.tensor_reduce(s("mx", m, m + 2), banks[:, 2 + m:4 + m, 0:nk], AX.X, ALU.max))
                if i >= 2:
                    dve.wait_ge(att_e, 2 * (i - 1))
                dve.tensor_scalar(s("nb", m, m + 2), s("mx", m, m + 2), -DH ** -0.5, None, ALU.mult).then_inc(att_nb, 1)

            def difference(i):
                t, h = ATT_ITEMS[i]
                nk = SEQ if t == 0 else NKEY - SEQ
                m = 2 * (i % 2)
                p0, p1, pd, _ = (x[:, 0:nk] for x in pp[i % 2])
                dve.wait_ge(att_e, 2 * (i + 1))
                link(dve.reciprocal(s("rs", m, m + 2), s("sum", m, m + 2)))
                note(dve.tensor_scalar(p1, p1, s("rs", m + 1, m + 2), s("nlam"), ALU.mult, ALU.mult))
                settle()
                if i >= 2:
                    dve.wait_ge(att_t, i - 1)
                dve.scalar_tensor_tensor(out=pd, in0=p0, scalar=s("rs", m, m + 1), in1=p1, op0=ALU.mult,
                                         op1=ALU.add).then_inc(att_pd, 1)

            n = len(ATT_ITEMS)
            for i in range(n + 2):
                if i < n:
                    neg_max(i)
                if 1 <= i <= n:
                    difference(i - 1)
                if i < n and i % 2 and JOBS[ATT_JOBS[i // 2]].engine == "v":
                    job_copy(ATT_JOBS[i // 2])
                if i < n and i % 6 >= 2:
                    split(7 + i // 6, 2 * (i % 6) - 4, 2 * (i % 6) - 2)
            dve.wait_ge(oa_n, T)
            dve.wait_ge(gates_on, 1)
            for t in range(T):
                dve.tensor_tensor(o_a[:, t, :], o_a[:, t, :], ra[:, t, :], ALU.mult).then_inc(oa_g, 1)
            dve.wait_ge(od_sq, 1)
            link(dve.reciprocal(s("eb", 0, 24), s("eb", 24, 48)))
            for t in range(T):
                v = o_d[:, t, :].rearrange("p (h v) -> p h v", h=AH)
                dve.tensor_tensor(v, v, s("eb", AH * t, AH * t + AH)[:, :, None].to_broadcast((P, AH, P)), ALU.mult).then_inc(od_g, 1)
            family_copies(dve, F_OA, lambda k, b: dve.tensor_scalar(oaT[:, k, :], b[:, 0:NT], s("gla_g", k % 2, k % 2 + 1), None, ALU.mult), 1,
                          lambda k: split(11, k - 1, k + 1))
            family_copies(dve, F_OD, lambda k, b: dve.tensor_scalar(odT[:, k, :], b[:, 0:NT], s("sub_g"), None, ALU.mult), 1)
            dve.wait_ge(gates_on, 2)
            for j in J_PA:
                job_copy(j)
            for j in J_GB[-2:]:
                wait_job_copied(dve, j)
            wait_job_copied(dve, J_PA[-1])
            for n, j in enumerate(J_PB):
                job_copy(j)
                if n % 2 == 0 and n:
                    tile_copy(dve, F_M, n // 2 - 1, mT, dve.tensor_copy, 1)
            dve.wait_ge(bc_loaded, 160)
            dve.wait_ge(ld_x2, 32)
            for g in range(2):
                note(dve.tensor_scalar(sc2b[:, g, :], sc2b[:, g, :], 1.0, None, ALU.add))

            def softmax_max(n):
                t = ORDER[n]
                dve.wait_ge(rt_log, n + 1)
                link(dve.tensor_reduce(rst[:, t:t + 1], banks[:, 4 + t, 0:NE], AX.X, ALU.max))
                dve.tensor_scalar(rst[:, 3 + t:4 + t], rst[:, t:t + 1], -1.0, None, ALU.mult).then_inc(rt_max, 1)

            def softmax_scale(n):
                t = ORDER[n]
                dve.wait_ge(rt_exp, n + 1)
                link(dve.reciprocal(rst[:, 9 + t:10 + t], rst[:, 6 + t:7 + t]))
                dve.tensor_scalar(aff[:, t, :], aff[:, t, :], rst[:, 9 + t:10 + t], None, ALU.mult).then_inc(rt_aff, 1)

            def layer_norms(n):
                t = ORDER[n]
                stats(t).then_inc(x1_var[0], 1)
                dve.wait_ge(x1_std[0], n + 1)
                link(affine(x_r, t, l1g, l1b))
                stats(t).then_inc(x1_var[1], 1)
                if n == 2:
                    softmax_max(1)
                dve.wait_ge(x1_std[1], n + 1)
                g = min(t, 1)
                affine(h2, t, sc2b[:, g, :], sh2b[:, g, :]).then_inc(h2_ready, 1)

            def turned_probs(n):
                t = ORDER[n]
                dve.wait_ge(rt_tr, n + 1)
                link(dve.tensor_copy(affT[:, t * P:(t + 1) * P], banks[0:NE, 4 + t, 0:P]))

            def best(a, b, s0, cap):
                for r in range(cap // 8):
                    v = gates[:, s0 + 8 * r:s0 + 8 * r + 8]
                    link(dve.max(v, affT[:, a:b]))
                    note(dve.max_index(idxu[:, s0 + 8 * r:s0 + 8 * r + 8], v, affT[:, a:b]))
                    if r < cap // 8 - 1:
                        settle()
                        link(dve.match_replace(affT[:, a:b], v, affT[:, a:b], -1.0))

            job_copy(J_WO[0])
            tile_copy(dve, F_M, 2, mT, dve.tensor_copy, 1)
            job_copy(J_WO[1])
            layer_norms(0)
            job_copy(J_WO[2])
            job_copy(J_WO[3])
            tile_copy(dve, F_H2, 0, h2T, dve.tensor_copy, 1)
            layer_norms(1)
            softmax_max(0)
            softmax_scale(0)
            job_copy(J_WO[4])
            job_copy(J_WO[5])
            tile_copy(dve, F_H2, 1, h2T, dve.tensor_copy, 1)
            layer_norms(2)
            softmax_scale(1)
            tile_copy(dve, F_H2, 2, h2T, dve.tensor_copy, 1)
            note(dve.memset(slots, -1.0))
            note(dve.memset(gates, 0.0))
            turned_probs(0)
            turned_probs(1)
            best(SEQ, NT, LAT0, CAP_L)
            softmax_max(2)
            softmax_scale(2)
            turned_probs(2)
            best(0, SEQ, CTX0, CAP_C)
            settle()
            note(dve.tensor_scalar(slots[:, LAT0:LAT0 + CAP_L], idxu[:, LAT0:LAT0 + CAP_L], float(SEQ), None, ALU.add))
            link(dve.tensor_copy(slots[:, CTX0:CTX0 + CAP_C], idxu[:, CTX0:CTX0 + CAP_C]))
            dve.tensor_copy(slots[:, SLOT:2 * SLOT], slots[:, 0:SLOT]).then_inc(rt_slots, 1)
            dve.tensor_copy(gates[:, SLOT:2 * SLOT], gates[:, 0:SLOT]).then_inc(rt_slots, 1)
            dve.wait_ge(rt_tt, 1)
            dve.tensor_copy(idxT, banks[:, 7, 0:NE]).then_inc(rt_cols, 1)
            dve.tensor_copy(gateT, banks[:, 7, NE:2 * NE]).then_inc(rt_cols, 1)
            dve.wait_ge(rt_cols, 2)
            dve.tensor_scalar(selT, iota_r, idxT[:, 0:1], None, ALU.is_equal).then_inc(sel0_rows, 1)
            dve.wait_ge(sel0_turned, 1)
            dve.tensor_copy(sel, banks[:, 6, 0:T * SLOT].rearrange("p (t s) -> p t s", t=T)).then_inc(sel_ready, T)
            dve.wait_ge(ld_g2, 64)
            dve.wait_ge(acc_done, 6)

            def at(e):
                return slice(e, e + 1) if isinstance(e, int) else bass.ds(e, 1)

            def expert(e, last=False):
                dve.tensor_scalar(selT, iota_r, idxT[:, at(e)], gateT[:, at(e)],
                                  ALU.is_equal, ALU.mult).then_inc(selT_ready, 1)
                dve.wait_ge(xet_done, e + 1)
                dve.tensor_copy(xeT, banks[:, 4, :].rearrange("p (i n) -> p i n", n=P)).then_inc(xet_cp, 1)
                if not last:
                    dve.wait_ge(rt_bc, 16)
                    for t in range(T):
                        dve.tensor_scalar(sel[:, t, :], slot_bc[:, at(e + 1), :].rearrange("p e s -> p (e s)"),
                                          iota_c[:, t:t + 1], None, ALU.is_equal).then_inc(sel_ready, 1)
                dve.wait_ge(up_used, e * 4 + 4)
                for b, (i0, i1) in enumerate(FCH):
                    dve.wait_ge(silu_done, e * 3 + b + 1)
                    dve.tensor_tensor(hid[:, i0 * P:i1 * P], hid[:, i0 * P:i1 * P], banks[:, 3 + b, 0:(i1 - i0) * P],
                                      ALU.mult).then_inc(hid_done, 1)
                dve.wait_ge(down_used, e * 4 + 4)
                for dc in range(2):
                    cs = slice(dc * BANK, (dc + 1) * BANK)
                    dve.tensor_tensor(yrow[:, cs], banks[:, 6 + dc, :], g2s[:, cs], ALU.mult).then_inc(y_cp, 1)
                if last:
                    return
                for t in range(T):
                    for dc in range(2):
                        n = 2 * t + dc
                        dve.wait_ge(comb_done, e * 6 + n + 1)
                        dst = x_r[:, t, dc * BANK:(dc + 1) * BANK]
                        dve.tensor_tensor(dst, dst, banks[:, n, :], ALU.add).then_inc(acc_done, 1)

            with dve.Fori(0, NE - 1) as e:
                expert(e)
            expert(NE - 1, last=True)
            sums = banks[:, 0:2 * T, :].rearrange("p (t w) n -> p t (w n)", t=T)
            dve.wait_ge(ld_end, 32)

            def final(t):
                dve.wait_ge(f_std, t + 1)
                affine(x_r, t, l2g, l2b, sums).then_inc(f_ready, 1)

            for t in range(T):
                dve.wait_ge(comb_done, 6 * (NE - 1) + 2 * t + 2)
                stats(t, sums).then_inc(f_var, 1)
                if t == 0:
                    final(0)
            for t in range(1, T):
                final(t)


_INS = ["x_prompt", "x_sample", "cache_diff_k", "cache_diff_v", "state_gla_fwd", "state_gla_bwd", "c", "c_ctx",
        "w_mod", "b_mod", "w_in", "w_alpha_f", "b_alpha_f", "w_alpha_b", "b_alpha_b", "gla_norm_g", "w_proj_a",
        "lambda_q1", "lambda_k1", "lambda_q2", "lambda_k2", "subln_g", "w_proj_b", "w_out", "ln1_g", "ln1_b",
        "w_router", "w_exp_gate", "w_exp_up", "w_exp_down", "ln2_g", "ln2_b"]
_OUTS = [(1, SEQ, D), (1, DEC, D), (1, 1, SEQ, AH, 2, DH), (1, 1, SEQ, AH, 2 * DH), (1, 1, GH, DK, DV), (1, 1, GH, DK, DV)]


def kernel(**inputs):
    import concourse.bacc as _bacc
    from concourse.bass_utils import run_bass_kernel_spmd as _run

    nc = _bacc.Bacc("TRN2", target_bir_lowering=False, num_devices=1)
    arrays, args = {}, []
    given = [(n, np.ascontiguousarray(inputs[n])) for n in _INS]
    given += list(zip(("const_f", "const_m", "const_r"), host_constants()))
    for name, a in given:
        arrays[f"in_{name}"] = a
        args.append(nc.dram_tensor(f"in_{name}", a.shape, mybir.dt.from_np(a.dtype), kind="ExternalInput").ap())
    for i, shape in enumerate(_OUTS):
        args.append(nc.dram_tensor(f"out_{i}", shape, F32, kind="ExternalOutput").ap())
    trunk_layer(nc, *args)
    r = _run(nc, [arrays], core_ids=[0])
    return tuple(r.results[0][f"out_{i}"] for i in range(len(_OUTS)))
```
